# Optimizing a Trainium2 kernel written in Bass

```python
import jax
import jax.numpy as jnp
from jax import lax
import numpy as np
import jax, jax.numpy as jnp

D_MODEL = 1024
BATCH = 1
SEQ = 256
DEPTH = 2

HEAD_DIM = 64
ROPE_THETA = 10000.0
RMS_EPS = 1e-6
N_BRANCH = 3

A_HEADS = 6
A_WIDTH = A_HEADS * HEAD_DIM
A_BLOCK = 256
A_TOPK = 3
A_QCHUNK = 32

B_HEADS = 6
B_WIDTH = B_HEADS * HEAD_DIM
B_KV_DIM = HEAD_DIM
B_TOPK = 256
B_IDX_HEADS = 4
B_IDX_DIM = HEAD_DIM
B_QCHUNK = 128

C_GROUPS = ((128, 1), (512, 4), (2048, 16))
C_SLOTS = 4
C_HEADS = C_SLOTS * len(C_GROUPS)
C_WIDTH = C_SLOTS * HEAD_DIM
C_BLOCK = 128

IN_SPLITS = (A_WIDTH, A_WIDTH, A_WIDTH, A_WIDTH,
             B_WIDTH, B_KV_DIM, B_KV_DIM, B_WIDTH, B_IDX_HEADS * B_IDX_DIM, B_IDX_DIM, B_IDX_HEADS,
             C_HEADS * HEAD_DIM, C_HEADS * HEAD_DIM, C_HEADS * HEAD_DIM, C_WIDTH,
             N_BRANCH * D_MODEL)
IN_WIDTH = sum(IN_SPLITS)
IN_OFFSETS = tuple(int(o) for o in np.cumsum(IN_SPLITS)[:-1])


def rmsnorm(x, g):
    xf = x.astype(jnp.float32)
    y = xf * lax.rsqrt(jnp.mean(xf * xf, axis=-1, keepdims=True) + RMS_EPS)
    return (y * g.astype(jnp.float32)).astype(x.dtype)

def rope_tables(seq_len):
    inv_freq = 1.0 / (ROPE_THETA ** (jnp.arange(0, HEAD_DIM, 2, dtype=jnp.float32) / HEAD_DIM))
    ang = jnp.arange(seq_len, dtype=jnp.float32)[:, None] * inv_freq[None, :]
    return jnp.cos(ang), jnp.sin(ang)

def apply_rope(x, cos, sin):
    half = HEAD_DIM // 2
    c = cos[None, :, None, :].astype(x.dtype)
    s = sin[None, :, None, :].astype(x.dtype)
    x1, x2 = x[..., :half], x[..., half:]
    return jnp.concatenate([x1 * c - x2 * s, x1 * s + x2 * c], axis=-1)

def moba_attention(q, k, v):
    bsz, seq, nh, hd = q.shape
    scale = hd ** -0.5
    n_blk = -(-seq // A_BLOCK)
    pad = n_blk * A_BLOCK - seq
    qh = q.transpose(0, 2, 1, 3)
    kb = jnp.pad(k.transpose(0, 2, 1, 3), ((0, 0), (0, 0), (0, pad), (0, 0))).reshape(bsz, nh, n_blk, A_BLOCK, hd)
    vb = jnp.pad(v.transpose(0, 2, 1, 3), ((0, 0), (0, 0), (0, pad), (0, 0))).reshape(bsz, nh, n_blk, A_BLOCK, hd)
    k_mean = jnp.mean(kb.astype(jnp.float32), axis=3)
    topk = max(1, min(A_TOPK, n_blk - 1))
    b_ix = jnp.arange(bsz)[:, None, None, None]
    h_ix = jnp.arange(nh)[None, :, None, None]
    blk_ids = jnp.arange(n_blk)
    n_sel = topk * A_BLOCK

    def chunk(ci):
        t0 = ci * A_QCHUNK
        own = t0 // A_BLOCK
        t_pos = t0 + jnp.arange(A_QCHUNK)
        qc = lax.dynamic_slice_in_dim(qh, t0, A_QCHUNK, axis=2)
        k_own = lax.dynamic_index_in_dim(kb, own, axis=2, keepdims=False)
        v_own = lax.dynamic_index_in_dim(vb, own, axis=2, keepdims=False)
        kpos_own = own * A_BLOCK + jnp.arange(A_BLOCK)
        s_own = jnp.einsum('bhqd,bhkd->bhqk', qc, k_own, preferred_element_type=jnp.float32) * scale
        s_own = jnp.where(kpos_own[None, :] <= t_pos[:, None], s_own, -jnp.inf)
        gate = jnp.einsum('bhqd,bhnd->bhqn', qc.astype(jnp.float32), k_mean)
        gate = jnp.where(blk_ids < own, gate, -jnp.inf)
        g_val, g_idx = lax.top_k(gate, topk)
        sel_ok = jnp.isfinite(g_val)
        k_sel = kb[b_ix, h_ix, g_idx]
        v_sel = vb[b_ix, h_ix, g_idx]
        s_sel = jnp.einsum('bhqd,bhqnkd->bhqnk', qc, k_sel, preferred_element_type=jnp.float32) * scale
        s_sel = jnp.where(sel_ok[..., None], s_sel, -jnp.inf)
        scores = jnp.concatenate([s_sel.reshape(bsz, nh, A_QCHUNK, n_sel), s_own], axis=-1)
        p = jax.nn.softmax(scores, axis=-1).astype(v.dtype)
        p_sel = p[..., :n_sel].reshape(bsz, nh, A_QCHUNK, topk, A_BLOCK)
        out = jnp.einsum('bhqnk,bhqnkd->bhqd', p_sel, v_sel)
        return out + jnp.einsum('bhqk,bhkd->bhqd', p[..., n_sel:], v_own)

    outs = lax.map(chunk, jnp.arange(seq // A_QCHUNK))
    return outs.transpose(1, 0, 3, 2, 4).reshape(bsz, seq, nh, hd)

def dsa_attention(q, k, v, iq, ik, iw):
    bsz, seq, nh, hd = q.shape
    scale = hd ** -0.5
    n_keep = min(B_TOPK, seq // 4)
    b_ix = jnp.arange(bsz)[:, None, None]
    key_pos = jnp.arange(seq)
    iw = iw.astype(jnp.float32) * (B_IDX_HEADS * B_IDX_DIM) ** -0.5

    def chunk(ci):
        t0 = ci * B_QCHUNK
        t_pos = t0 + jnp.arange(B_QCHUNK)
        iq_c = lax.dynamic_slice_in_dim(iq, t0, B_QCHUNK, axis=1)
        iw_c = lax.dynamic_slice_in_dim(iw, t0, B_QCHUNK, axis=1)
        logit = jnp.einsum('bqhd,bsd->bqhs', iq_c, ik, preferred_element_type=jnp.float32)
        idx_score = jnp.einsum('bqhs,bqh->bqs', jax.nn.relu(logit), iw_c)
        idx_score = jnp.where(key_pos[None, :] <= t_pos[:, None], idx_score, -jnp.inf)
        _, sel = lax.top_k(idx_score, n_keep)
        sel_ok = sel <= t_pos[None, :, None]
        k_g = k[b_ix, sel]
        v_g = v[b_ix, sel]
        qc = lax.dynamic_slice_in_dim(q, t0, B_QCHUNK, axis=1)
        s = jnp.einsum('bqhd,bqkd->bqhk', qc, k_g, preferred_element_type=jnp.float32) * scale
        s = jnp.where(sel_ok[:, :, None, :], s, -jnp.inf)
        p = jax.nn.softmax(s, axis=-1).astype(v.dtype)
        return jnp.einsum('bqhk,bqkd->bqhd', p, v_g)

    outs = lax.map(chunk, jnp.arange(seq // B_QCHUNK))
    return outs.transpose(1, 0, 2, 3, 4).reshape(bsz, seq, nh, hd)

def dilated_group(q, k, v, steps, dil):
    bsz, seq, nh, hd = q.shape
    n_sub = seq // dil
    n_blk = -(-n_sub // C_BLOCK)
    pad = n_blk * C_BLOCK - n_sub

    def to_sub(t):
        t = t.reshape(bsz, n_sub, dil, nh, hd).transpose(0, 2, 3, 1, 4)
        return jnp.pad(t, ((0, 0), (0, 0), (0, 0), (0, pad), (0, 0)))

    def band(t):
        tb = jnp.pad(to_sub(t), ((0, 0), (0, 0), (0, 0), (C_BLOCK, 0), (0, 0)))
        tb = tb.reshape(bsz, dil, nh, n_blk + 1, C_BLOCK, hd)
        return jnp.concatenate([tb[:, :, :, :-1], tb[:, :, :, 1:]], axis=4)

    qs = to_sub(q).reshape(bsz, dil, nh, n_blk, C_BLOCK, hd)
    kw = band(k)
    vw = band(v)
    s = jnp.einsum('brhnqd,brhnkd->brhnqk', qs, kw, preferred_element_type=jnp.float32) * hd ** -0.5
    blk = jnp.arange(n_blk)[:, None, None]
    qi = jnp.arange(C_BLOCK)[None, :, None]
    ki = jnp.arange(2 * C_BLOCK)[None, None, :]
    dist = C_BLOCK + qi - ki
    ok = (dist >= 0) & (dist <= steps) & (blk * C_BLOCK + ki >= C_BLOCK)
    s = jnp.where(ok, s, -jnp.inf)
    lse = jax.nn.logsumexp(s, axis=-1)
    p = jnp.exp(s - lse[..., None]).astype(v.dtype)
    o = jnp.einsum('brhnqk,brhnkd->brhnqd', p, vw)
    o = o.reshape(bsz, dil, nh, n_blk * C_BLOCK, hd)[:, :, :, :n_sub]
    o = o.transpose(0, 3, 1, 2, 4).reshape(bsz, seq, nh, hd)
    lse = lse.reshape(bsz, dil, nh, n_blk * C_BLOCK)[..., :n_sub]
    lse = lse.transpose(0, 3, 1, 2).reshape(bsz, seq, nh)
    return o, lse

def dilated_mixture(q, k, v):
    outs = []
    lses = []
    for g, (window, dil) in enumerate(C_GROUPS):
        sl = slice(g * C_SLOTS, (g + 1) * C_SLOTS)
        o, l = dilated_group(q[:, :, sl], k[:, :, sl], v[:, :, sl], window // dil, dil)
        outs.append(o)
        lses.append(l)
    w = jax.nn.softmax(jnp.stack(lses, axis=0), axis=0)
    return jnp.sum(w[..., None] * jnp.stack(outs, axis=0), axis=0).astype(q.dtype)

def hybrid_layer(x, norm_g, w_in, w_br_a, w_br_b, w_br_c, w_out, cos, sin):
    bsz, seq, _ = x.shape
    h = rmsnorm(x, norm_g)
    proj = h @ w_in
    (a_q, a_k, a_v, a_g, b_q, b_k, b_v, b_g, i_q, i_k, i_w,
     c_q, c_k, c_v, c_g, m_g) = jnp.split(proj, IN_OFFSETS, axis=-1)

    def heads(t, n):
        return t.reshape(bsz, seq, n, -1)

    def rope1(t):
        return apply_rope(t[:, :, None, :], cos, sin)[:, :, 0, :]

    ya = moba_attention(apply_rope(heads(a_q, A_HEADS), cos, sin),
                        apply_rope(heads(a_k, A_HEADS), cos, sin),
                        heads(a_v, A_HEADS))
    ya = ya.reshape(bsz, seq, A_WIDTH) * jax.nn.silu(a_g)
    yb = dsa_attention(apply_rope(heads(b_q, B_HEADS), cos, sin), rope1(b_k), b_v,
                       apply_rope(heads(i_q, B_IDX_HEADS), cos, sin), rope1(i_k), i_w)
    yb = yb.reshape(bsz, seq, B_WIDTH) * jax.nn.silu(b_g)
    yc = dilated_mixture(apply_rope(heads(c_q, C_HEADS), cos, sin),
                         apply_rope(heads(c_k, C_HEADS), cos, sin),
                         heads(c_v, C_HEADS))
    yc = yc.reshape(bsz, seq, C_WIDTH) * jax.nn.silu(c_g)
    gates = jax.nn.sigmoid(m_g).reshape(bsz, seq, N_BRANCH, D_MODEL)
    merged = (gates[:, :, 0] * (ya @ w_br_a)
              + gates[:, :, 1] * (yb @ w_br_b)
              + gates[:, :, 2] * (yc @ w_br_c))
    return x + merged @ w_out

def first_inputs(seed: int = 0) -> dict:
    key = jax.random.key(seed)
    ks = jax.random.split(key, 8)
    x = jax.random.normal(ks[0], (BATCH, SEQ, D_MODEL), jnp.float32)
    norm_g = 1.0 + 0.02 * jax.random.normal(ks[1], (DEPTH, D_MODEL), jnp.float32)
    w_in = jax.random.normal(ks[2], (DEPTH, D_MODEL, IN_WIDTH), jnp.float32) * D_MODEL ** -0.5
    w_br_a = jax.random.normal(ks[3], (DEPTH, A_WIDTH, D_MODEL), jnp.float32) * A_WIDTH ** -0.5
    w_br_b = jax.random.normal(ks[4], (DEPTH, B_WIDTH, D_MODEL), jnp.float32) * B_WIDTH ** -0.5
    w_br_c = jax.random.normal(ks[5], (DEPTH, C_WIDTH, D_MODEL), jnp.float32) * C_WIDTH ** -0.5
    w_out = jax.random.normal(ks[6], (DEPTH, D_MODEL, D_MODEL), jnp.float32) * D_MODEL ** -0.5
    final_norm_g = 1.0 + 0.02 * jax.random.normal(ks[7], (D_MODEL,), jnp.float32)
    return {'x': x, 'norm_g': norm_g, 'w_in': w_in, 'w_br_a': w_br_a, 'w_br_b': w_br_b,
            'w_br_c': w_br_c, 'w_out': w_out, 'final_norm_g': final_norm_g}

def first_block(x, norm_g, w_in, w_br_a, w_br_b, w_br_c, w_out, final_norm_g):
    cos, sin = rope_tables(x.shape[1])
    for layer in range(DEPTH):
        x = hybrid_layer(x, norm_g[layer], w_in[layer], w_br_a[layer], w_br_b[layer],
                         w_br_c[layer], w_out[layer], cos, sin)
    return rmsnorm(x, final_norm_g)


CTX_LEN = 256
GRID_W = 64
N_MIXERS = 2
FFN_DIM = 2816
N_FOURIER_GROUPS = 4
FOURIER_GROUP_DIM = D_MODEL // N_FOURIER_GROUPS
RET_HEADS = 4
RET_QK_DIM = D_MODEL // RET_HEADS
RET_V_DIM = 2 * D_MODEL // RET_HEADS
RET_QK_TOTAL = RET_HEADS * RET_QK_DIM
RET_V_TOTAL = RET_HEADS * RET_V_DIM
RET_IN_DIM = 2 * RET_QK_TOTAL + 2 * RET_V_TOTAL
RET_CHUNK = 128
ROPE_BASE = 10000.0
N_MOD = 9
NORM_EPS = 1e-6
N_FOURIER_LAYERS = (DEPTH + N_MIXERS - 1) // N_MIXERS
N_RET_LAYERS = DEPTH // N_MIXERS


def rmsnorm_2(x, g):
    xf = x.astype(jnp.float32)
    y = xf * lax.rsqrt(jnp.mean(xf * xf, axis=-1, keepdims=True) + NORM_EPS)
    return (y * g.astype(jnp.float32)).astype(x.dtype)

def modulate(h, shift, scale):
    return h * (1 + scale) + shift

def swiglu(h, w_gate, w_up, w_down):
    return (jax.nn.silu(h @ w_gate) * (h @ w_up)) @ w_down

def fourier_mix(h):
    b, n, d = h.shape
    hg = h.reshape(b, n, N_FOURIER_GROUPS, FOURIER_GROUP_DIM).astype(jnp.float32)
    f = jnp.fft.fft2(hg, axes=(1, 3), norm="ortho").real
    return f.reshape(b, n, d).astype(h.dtype)

def fourier_layer(h_lat, h_ctx, w, bias):
    y_lat = fourier_mix(h_lat) @ w + bias
    y_ctx = None if h_ctx is None else fourier_mix(h_ctx) @ w + bias
    return y_lat, y_ctx

def axial_rope(n_tokens):
    rows = n_tokens // GRID_W
    row = jnp.repeat(jnp.arange(rows, dtype=jnp.float32), GRID_W)
    col = jnp.tile(jnp.arange(GRID_W, dtype=jnp.float32), rows)
    n_freq = RET_QK_DIM // 4
    inv_freq = ROPE_BASE ** (-jnp.arange(n_freq, dtype=jnp.float32) / n_freq)
    ang = jnp.concatenate([row[:, None] * inv_freq, col[:, None] * inv_freq], axis=-1)
    return jnp.cos(ang), jnp.sin(ang)

def apply_rope_2(t, cos, sin):
    t1, t2 = jnp.split(t, 2, axis=-1)
    cos = cos.astype(t.dtype)
    sin = sin.astype(t.dtype)
    return jnp.concatenate([t1 * cos - t2 * sin, t2 * cos + t1 * sin], axis=-1)

def ret_project(h, w_in):
    b, n, _ = h.shape
    p = h @ w_in
    q, k, v, g = jnp.split(p, [RET_QK_TOTAL, 2 * RET_QK_TOTAL, 2 * RET_QK_TOTAL + RET_V_TOTAL], axis=-1)
    q = q.reshape(b, n, RET_HEADS, RET_QK_DIM).transpose(0, 2, 1, 3)
    k = k.reshape(b, n, RET_HEADS, RET_QK_DIM).transpose(0, 2, 1, 3) * (RET_QK_DIM ** -0.5)
    v = v.reshape(b, n, RET_HEADS, RET_V_DIM).transpose(0, 2, 1, 3)
    return q, k, v, g

def retention_scan(q, k, v, lg, s0):
    b, h, n, dk = q.shape
    dv = v.shape[-1]
    nc = n // RET_CHUNK
    dt = q.dtype
    pos = jnp.arange(RET_CHUNK, dtype=jnp.float32)
    diff = pos[:, None] - pos[None, :]
    intra = jnp.where(diff >= 0, jnp.exp(lg[:, None, None] * jnp.maximum(diff, 0.0)), 0.0).astype(dt)
    q_dec = jnp.exp(lg[:, None] * (pos + 1.0))[:, :, None].astype(dt)
    k_dec = jnp.exp(lg[:, None] * (RET_CHUNK - 1.0 - pos))[:, :, None].astype(dt)
    chunk_dec = jnp.exp(lg * RET_CHUNK)[:, None, None].astype(dt)

    def to_chunks(t):
        return jnp.moveaxis(t.reshape(b, h, nc, RET_CHUNK, t.shape[-1]), 2, 0)

    def step(s, qkv):
        qc, kc, vc = qkv
        scores = jnp.einsum('bhid,bhjd->bhij', qc, kc) * intra
        y = (jnp.einsum('bhij,bhje->bhie', scores, vc)
             + jnp.einsum('bhid,bhde->bhie', qc * q_dec, s))
        s = chunk_dec * s + jnp.einsum('bhjd,bhje->bhde', kc * k_dec, vc)
        return s, y

    s_final, y = lax.scan(step, s0, (to_chunks(q), to_chunks(k), to_chunks(v)))
    y = jnp.moveaxis(y, 0, 2).reshape(b, h, n, dv)
    return y, s_final

def bidirectional_retention(q, k, v, lg_fwd, lg_bwd, s_fwd, s_bwd):
    y_f, s_f = retention_scan(q, k, v, lg_fwd, s_fwd)
    y_b_rev, s_b = retention_scan(jnp.flip(q, 2), jnp.flip(k, 2), jnp.flip(v, 2), lg_bwd, s_bwd)
    return y_f + jnp.flip(y_b_rev, 2), s_f, s_b

def ret_output(y, g, w_out):
    b, h, n, dv = y.shape
    yf = y.astype(jnp.float32)
    mu = jnp.mean(yf, axis=-1, keepdims=True)
    var = jnp.mean(jnp.square(yf - mu), axis=-1, keepdims=True)
    yn = ((yf - mu) * lax.rsqrt(var + NORM_EPS)).astype(g.dtype)
    yn = yn.transpose(0, 2, 1, 3).reshape(b, n, h * dv)
    return (jax.nn.silu(g) * yn) @ w_out

def retention_layer(h_lat, h_ctx, w_in, w_out, decay, cos, sin, need_ctx_out):
    lg = -jnp.abs(decay.astype(jnp.float32))
    qc, kc, vc, gc = ret_project(h_ctx, w_in)
    zeros = jnp.zeros((h_ctx.shape[0], RET_HEADS, RET_QK_DIM, RET_V_DIM), vc.dtype)
    yc, s_f, s_b = bidirectional_retention(qc, kc, vc, lg[0], lg[1], zeros, zeros)
    ql, kl, vl, gl = ret_project(h_lat, w_in)
    ql = apply_rope_2(ql, cos, sin)
    kl = apply_rope_2(kl, cos, sin)
    yl, _, _ = bidirectional_retention(ql, kl, vl, lg[0], lg[1], s_f, s_b)
    y_lat = ret_output(yl, gl, w_out)
    y_ctx = ret_output(yc, gc, w_out) if need_ctx_out else None
    return y_lat, y_ctx

def second_inputs(seed: int = 0) -> dict:
    key = jax.random.key(seed)
    ks = jax.random.split(key, 16)
    f32 = jnp.float32
    base_rate = -np.log(1.0 - 2.0 ** (-5.0 - np.arange(RET_HEADS, dtype=np.float32)))
    base_rate = jnp.asarray(base_rate, dtype=f32)
    return {
        "x": jax.random.normal(ks[0], (BATCH, SEQ, D_MODEL), f32),
        "c": jax.random.normal(ks[1], (BATCH, D_MODEL), f32),
        "ctx": jax.random.normal(ks[2], (BATCH, CTX_LEN, D_MODEL), f32),
        "c_ctx": jax.random.normal(ks[3], (D_MODEL,), f32),
        "ada_w": jax.random.normal(ks[4], (DEPTH, D_MODEL, N_MOD * D_MODEL), f32) * (0.5 * D_MODEL ** -0.5),
        "ada_b": jax.random.normal(ks[5], (DEPTH, N_MOD * D_MODEL), f32) * 0.01,
        "norm_g": 1.0 + 0.02 * jax.random.normal(ks[6], (DEPTH, 3, D_MODEL), f32),
        "final_g": 1.0 + 0.02 * jax.random.normal(ks[7], (D_MODEL,), f32),
        "ffn_w_gate": jax.random.normal(ks[8], (DEPTH, 2, D_MODEL, FFN_DIM), f32) * D_MODEL ** -0.5,
        "ffn_w_up": jax.random.normal(ks[9], (DEPTH, 2, D_MODEL, FFN_DIM), f32) * D_MODEL ** -0.5,
        "ffn_w_down": jax.random.normal(ks[10], (DEPTH, 2, FFN_DIM, D_MODEL), f32) * FFN_DIM ** -0.5,
        "four_w": jax.random.normal(ks[11], (N_FOURIER_LAYERS, D_MODEL, D_MODEL), f32) * D_MODEL ** -0.5,
        "four_b": jax.random.normal(ks[12], (N_FOURIER_LAYERS, D_MODEL), f32) * 0.01,
        "ret_w_in": jax.random.normal(ks[13], (N_RET_LAYERS, D_MODEL, RET_IN_DIM), f32) * D_MODEL ** -0.5,
        "ret_w_out": jax.random.normal(ks[14], (N_RET_LAYERS, RET_V_TOTAL, D_MODEL), f32) * RET_V_TOTAL ** -0.5,
        "ret_decay": base_rate * (1.0 + 0.05 * jax.random.normal(ks[15], (N_RET_LAYERS, 2, RET_HEADS), f32)),
    }

def second_block(x, c, ctx, c_ctx, ada_w, ada_b, norm_g, final_g, ffn_w_gate, ffn_w_up, ffn_w_down,
              four_w, four_b, ret_w_in, ret_w_out, ret_decay):
    cos, sin = axial_rope(x.shape[1])
    silu_c = jax.nn.silu(c)
    silu_cc = jax.nn.silu(c_ctx)
    for l in range(DEPTH):
        last = l == DEPTH - 1
        mixer = l % N_MIXERS
        slot = l // N_MIXERS
        ctx_read = (not last) or (mixer == 1)
        m_lat = jnp.split((silu_c @ ada_w[l] + ada_b[l])[:, None, :], N_MOD, axis=-1)
        m_ctx = jnp.split(silu_cc @ ada_w[l] + ada_b[l], N_MOD, axis=-1)

        def half_ffn(t, m, j):
            h = modulate(rmsnorm_2(t, norm_g[l, j]), m[3 * j], m[3 * j + 1])
            return t + 0.5 * m[3 * j + 2] * swiglu(h, ffn_w_gate[l, j // 2], ffn_w_up[l, j // 2],
                                                  ffn_w_down[l, j // 2])

        x = half_ffn(x, m_lat, 0)
        if ctx_read:
            ctx = half_ffn(ctx, m_ctx, 0)

        h_lat = modulate(rmsnorm_2(x, norm_g[l, 1]), m_lat[3], m_lat[4])
        h_ctx = modulate(rmsnorm_2(ctx, norm_g[l, 1]), m_ctx[3], m_ctx[4]) if ctx_read else None
        if mixer == 0:
            y_lat, y_ctx = fourier_layer(h_lat, h_ctx, four_w[slot], four_b[slot])
        else:
            y_lat, y_ctx = retention_layer(h_lat, h_ctx, ret_w_in[slot], ret_w_out[slot], ret_decay[slot],
                                           cos, sin, not last)
        x = x + m_lat[5] * y_lat
        if not last:
            ctx = ctx + m_ctx[5] * y_ctx

        x = half_ffn(x, m_lat, 2)
        if not last:
            ctx = half_ffn(ctx, m_ctx, 2)
    return rmsnorm_2(x, final_g)


def setup_inputs(seed=0):
    out = dict(first_inputs(seed))
    for name, value in second_inputs(seed + 1).items():
        if name != "x":
            out[name + "_2"] = value
    return out


def reference(
    x, norm_g, w_in, w_br_a, w_br_b, w_br_c, w_out, final_norm_g, c_2, ctx_2, c_ctx_2, ada_w_2,
    ada_b_2, norm_g_2, final_g_2, ffn_w_gate_2, ffn_w_up_2, ffn_w_down_2, four_w_2, four_b_2,
    ret_w_in_2, ret_w_out_2, ret_decay_2,
):
    x = first_block(
        x, norm_g, w_in, w_br_a, w_br_b, w_br_c, w_out, final_norm_g,
    )
    return second_block(
        x, c_2, ctx_2, c_ctx_2, ada_w_2, ada_b_2, norm_g_2, final_g_2, ffn_w_gate_2, ffn_w_up_2,
        ffn_w_down_2, four_w_2, four_b_2, ret_w_in_2, ret_w_out_2, ret_decay_2,
    )


_drawn_inputs = setup_inputs


def setup_inputs(seed=0):
    import zlib

    import numpy as np

    out = dict(_drawn_inputs(seed))
    spreads = {}
    factors = {'norm_g': 3.55,
     'final_norm_g': 2.718,
     'ada_b_2': 3.807,
     'norm_g_2': 5.257,
     'final_g_2': 7.962,
     'four_b_2': 55.212}
    for name, (base, spread) in spreads.items():
        noise = np.random.default_rng([zlib.crc32(name.encode()), seed]).standard_normal(out[name].shape)
        drawn = base * np.exp(spread * noise) if base else spread * noise
        out[name] = jnp.asarray(drawn.astype(out[name].dtype))
    for name, factor in factors.items():
        out[name] = (out[name] * factor).astype(out[name].dtype)
    return out
```

```python
from contextlib import ExitStack, contextmanager

import numpy as np

import concourse.bass as bass
from concourse import mybir

F32 = mybir.dt.float32
F32R = mybir.dt.float32r
F16 = mybir.dt.float16
BF16 = mybir.dt.bfloat16
ACT = mybir.ActivationFunctionType
ALU = mybir.AluOpType
AX_X = mybir.AxisListType.X

P = 128
D = 1024
KT = D // P
T = 256
TT = T // P
HD = 64
LAYERS = 2
EPS = 1e-6
NEG = -1e30
TAKEN = -3e38
TOPK = 64
FFN = 2816
FT = FFN // P
DOWN = FT // 2
RING = 4
W8 = KT * P
VG, VW = 3, 408
WV = 2 * VW
WD = DOWN * P
RH = 4
RDV = 512
ADA = 9 * KT

QK, VN, GATE, MIXG, BR, OUT = 24, 12, 8, 24, 8, 8
PER_LAYER = QK + VN + GATE + MIXG + BR + OUT
PER_D = QK + VN + BR + OUT
PER_A = GATE + MIXG

AQ, AK, CQ, CK, BQ, IQ, BK, IK = 0, 6, 12, 24, 36, 42, 46, 47
NPOS = 48

MASK = {("tri", 0): (0, 128), ("d4", 0): (128, 128), ("d16", 0): (256, 128),
        ("w128", 1): (384, 256), ("d4", 1): (640, 256), ("d16", 1): (896, 256)}
MASKW = 1152


def softmax_units():
    units = []

    def place(pos):
        return pos // 2, pos % 2

    for h in range(6):
        for qt in range(TT):
            units.append((qt, [(place(AQ + h), place(AK + h), "tri")], [64 * h], 64 * h))
    for s in range(4):
        for qt in range(TT):
            first = "tri" if qt == 0 else "w128"
            segs = [(place(CQ + 4 * g + s), place(CK + 4 * g + s), m)
                    for g, m in enumerate((first, "d4", "d16"))]
            units.append((qt, segs, [448 + 64 * (4 * g + s) for g in range(3)], 768 + 64 * s))
    for h in range(6):
        for qt in range(TT):
            units.append((qt, [(place(BQ + h), (23, 0) if h % 2 == 0 else (24, 1), "picked")],
                          [384], 384 + 64 * h))
    return units


UNITS = softmax_units()
NU = len(UNITS)

COLS = {}
_at = 0
for _name, _n in (("norm_g", 16), ("final_norm_g", 8), ("norm_g_2", 48), ("final_g_2", 8),
                  ("four_b", 8), ("ada_b", 144), ("c", 16), ("decay", 8)):
    COLS[_name] = (_at, _n)
    _at += _n
NCOLS = _at


class Tally:

    def __init__(self, start=0):
        self.base, self.n = 0, start

    def __call__(self, k=1):
        self.n += k
        return self.base + self.n

    @property
    def now(self):
        return self.base + self.n


@contextmanager
def turns(eng, count, *tallies):
    kept = [(t, t.base, t.n) for t, _ in tallies]
    with eng.Fori(0, count) as i:
        for t, k in tallies:
            t.base = t.base + i * k
        yield i
    for (t, base, n), (_, k) in zip(kept, tallies):
        assert t.n - n == k, (t.n - n, k)
        t.base, t.n = base, n + k * count


def program(nc, xT_d, cols_d, ada_d, w1_d, wv_d, wu_d, wd_d, w2_d, rope_d, mask_d, ident_d, identb_d,
            dft_d, rope2_d, dist_d, dmask_d, out_d):
    with ExitStack() as ctx:
        top = [-(-nc.sbuf_base // 64) * 64]

        def at(name, shape, dt, offset):
            return nc.alloc_sbuf_tensor_at(name, shape, dt, offset=offset)

        def size(shape, dt):
            n = 2 if dt in (F16, BF16) else 4
            for s in shape[1:]:
                n *= s
            return -(-n // 64) * 64

        def keep(name, shape, dt=F32):
            t = at(name, shape, dt, top[0])
            top[0] += size(shape, dt)
            return t

        x = keep("x", [P, KT, 2 * T])
        hh = keep("h_high", [P, KT, 2 * T], F32R)
        hl = keep("h_low", [P, KT, 2 * T], F32R)
        raw = keep("raw", [P, RING, WD])
        wh = keep("w_high", [P, 2, WD], F32R)
        wl = keep("w_low", [P, 2, WD], F32R)
        cols = keep("cols", [P, NCOLS])
        ident = keep("ident", [P, P])
        ones = keep("ones", [P, P])
        identb = keep("identb", [P, P], BF16)
        mask = keep("mask", [P, MASKW], BF16)
        rope = keep("rope", [P, 2, T])
        mod = keep("mod", [P, LAYERS, ADA, 2])
        gain = keep("gain", [P, LAYERS * 3, KT, 2])
        gate = keep("gate", [P, LAYERS * 3, KT, 2])
        sc = keep("silu_c", [P, KT, 2])
        eps = keep("eps", [P, 1])
        sq = keep("sq", [P, 2, 2 * T])
        rs = keep("rs", [P, 2 * T])
        tn = keep("tn", [P, 2, 2 * T])
        yr = at("yr", [P, 4, T], F32, top[0])
        hn = keep("hn", [P, 2, 2 * T])
        rsum = keep("rsum", [P, NU])
        nmax = keep("nmax", [P, NU])
        rmax = keep("rmax", [P, NU])
        rrec = keep("rrec", [P, NU])
        iw = keep("iw", [P, TT, 4])
        top8 = keep("top8", [P, 8])
        lg = keep("lg", [P, 8])
        spare = keep("spare", [P, 8])
        arena = top[0]

        class Area:
            def __init__(self, base):
                self.at = base

            def __call__(self, name, shape, dt=F32):
                t = at(name, shape, dt, self.at)
                self.at += size(shape, dt)
                return t

        a1 = Area(arena)
        a1b = Area(arena)
        rot = a1("rot", [P, QK, T])
        prob = a1b("prob", [P, 2, 768])
        probT = a1b("probT", [P, 2, 768])
        y = a1b("y", [P, TT, D])
        picked = a1b("picked", [P, 3 * P], BF16)
        relu = at("relu", [P, 2, 2 * T], F32, arena + size([P, 2, 768], F32))
        idx = at("idx", [P, TT, T], F32, arena)
        assert a1b.at <= a1.at
        heads = a1("heads", [P, NPOS // 2 + 1, T])
        vn = a1("vn", [P, TT, VG * VW])
        sg = a1("sg", [P, KT, T])
        mg = a1("mg", [P, 3 * KT, T])

        a2 = Area(arena)
        ah = a2("act_high", [P, FT, 2 * T], F32R)
        al = a2("act_low", [P, FT, 2 * T], F32R)

        a3 = Area(arena)
        hf = a3("hf", [P, KT, 2 * T])
        pq = a3("pq", [P, 2, TT, 4, 2 * T])
        dft = a3("dft", [P, 2, 2 * T])
        dftn = a3("dftn", [P, TT, 2, T])

        a4 = Area(arena)
        qT = a4("qT", [P, KT, T])
        kT = a4("kT", [P, KT, 2 * T])
        vr = a4("vr", [P, 2 * TT, RH * RDV])
        sgr = a4("sgr", [P, 2 * KT, T])
        dist = a4("dist", [P, 2, 4, T], F16)
        dmask = a4("dmask", [P, 2, 2, T], F16)
        rope2 = a4("rope2", [P, 2, T])
        dec = a4("dec", [P, 2, 4, T])
        sT = a4("sT", [P, 4, T])
        for a in (a1, a2, a3, a4):
            assert a.at <= nc.sbuf_top, (a.at, nc.sbuf_top)

        ps = ctx.enter_context(nc.psum_tensor("ps", [P, 8, 512], F32))

        def sem(name):
            return ctx.enter_context(nc.semaphore(name))

        landed = [sem(f"landed{j}") for j in range(RING)]
        consts_in = sem("consts_in")
        tables_in = sem("tables_in")
        ret_tables_in = sem("ret_tables_in")
        heads_in = sem("heads_in")
        ones_set = sem("ones_set")
        eps_set = sem("eps_set")
        c_silu = sem("c_silu")
        ada_done = sem("ada_done")
        mod_ready = sem("mod_ready")
        hi_done = sem("hi_done")
        lo_done = sem("lo_done")
        chunk_done = sem("chunk_done")
        emptied_d = sem("emptied_d")
        emptied_a = sem("emptied_a")
        sq_done = sem("sq_done")
        sq_summed = sem("sq_summed")
        std_done = sem("std_done")
        scaled = sem("scaled")
        normed = sem("normed")
        norm_hi = sem("norm_hi")
        norm_split = sem("norm_split")
        act_hi = sem("act_hi")
        act_split = sem("act_split")
        logits = sem("logits")
        relu_done = sem("relu_done")
        idx_summed = sem("idx_summed")
        scored = sem("scored")
        maxed = sem("maxed")
        exped = sem("exped")
        turned = sem("turned")
        copied = sem("copied")
        weighed = sem("weighed")
        y_done = sem("y_done")
        yT_done = sem("yT_done")
        yT_out = sem("yT_out")
        f1_done = sem("f1_done")
        f1_out = sem("f1_out")
        f2_done = sem("f2_done")
        f2_hi = sem("f2_hi")
        decayed = sem("decayed")
        d_ready = sem("d_ready")
        rs_done = sem("rs_done")
        rs_out = sem("rs_out")
        ry_done = sem("ry_done")
        ry_out = sem("ry_out")
        rc_done = sem("rc_done")
        rmean = sem("rmean")
        rcent = sem("rcent")
        rstd = sem("rstd")
        rgn = sem("rgn")
        dve_step = sem("dve_step")
        act_step = sem("act_step")
        pool_step = sem("pool_step")
        stored = sem("stored")
        passed = sem("passed")

        def flat(t, k, lo=None, n=None):
            v = t[:, bass.ds(k, 1), :] if lo is None else t[:, bass.ds(k, 1), lo:lo + n]
            return v.rearrange("p a t -> p (a t)")

        def unit_width(u):
            qt, segs, _, _ = UNITS[u]
            return len(segs) * P * (qt + 1)

        hybrid = {}
        m = d = a = 0
        for name, n, kind in (("qk", QK, "d"), ("vn", VN, "d"), ("gate", GATE, "a"), ("mixg", MIXG, "a"),
                              ("br", BR, "d"), ("out", OUT, "d")):
            hybrid[name] = (m, d, a, n)
            m, d, a = m + n, d + (n if kind == "d" else 0), a + (n if kind == "a" else 0)
        later = {}
        m, d, a = LAYERS * m, LAYERS * d, LAYERS * a
        for name, n, kind in (("up0", 44, "d"), ("down0", 16, "d"), ("four", 8, "d"), ("up1", 44, "d"),
                              ("down1", 16, "d"), ("up2", 44, "d"), ("down2", 16, "d"), ("rq", 8, "d"),
                              ("rk", 8, "d"), ("rv", 16, "d"), ("rg", 16, "a"), ("ro", 16, "d"),
                              ("up3", 44, "d"), ("down3", 16, "d")):
            later[name] = (m, d, a, n)
            m, d, a = m + n, d + (n if kind == "d" else 0), a + (n if kind == "a" else 0)
        TOTAL = m
        ADA_LAPS = LAYERS * ADA // RING

        def of_layer(name, L):
            m, d, a, n = hybrid[name]
            return m + L * PER_LAYER, d + L * PER_D, a + L * PER_A, n

        block = ctx.enter_context(nc.Block())

        @block.sync
        def _(e):
            for dst, src in ((cols[:, :], cols_d), (x[:, :, :], xT_d.rearrange("(k p) t -> p k t", p=P)),
                             (ident[:, :], ident_d), (identb[:, :], identb_d), (mask[:, :], mask_d),
                             (rope[:, :, :], rope_d.rearrange("p (a t) -> p a t", a=2))):
                e.dma_start(dst, src).then_inc(consts_in, 16)

            def chunk(src, n):
                return src[bass.ds(n, 1)].rearrange("a p n -> p (a n)")

            for j in range(RING):
                e.dma_start(raw[:, j, 0:W8], chunk(ada_d, j)).then_inc(landed[j], 16)
            with e.Fori(1, ADA_LAPS) as i:
                for j in range(RING):
                    e.wait_ge(ada_done, RING * i + j - RING + 1)
                    e.dma_start(raw[:, j, 0:W8], chunk(ada_d, RING * i + j)).then_inc(landed[j], 16)
            e.wait_ge(ada_done, LAYERS * ADA)

            def load(m0, n, width, src, first):
                with e.Fori(0, n // RING) as i:
                    for j in range(RING):
                        e.wait_ge(lo_done, m0 + RING * i + j + 1)
                        e.dma_start(raw[:, j, 0:width], chunk(src, first + RING * i + j))\
                            .then_inc(landed[j], 16)

            with e.Fori(0, LAYERS) as L:
                per = PER_LAYER - VN
                load(of_layer("qk", L)[0], QK, W8, w1_d, per * L)
                load(of_layer("vn", L)[0], VN, WV, wv_d, VN * L)
                load(of_layer("gate", L)[0], per - QK, W8, w1_d, per * L + QK)

            def ffn(f):
                load(later[f"up{f}"][0], 2 * FT, W8, wu_d, 2 * FT * f)
                load(later[f"down{f}"][0], 2 * KT, WD, wd_d, 2 * KT * f)

            ffn(0)
            e.wait_ge(chunk_done, later["down0"][0] + 2 * KT)
            e.dma_start(dft[:, :, :], dft_d[:, 0:4 * T].rearrange("p (a t) -> p a t", a=2)).then_inc(tables_in, 16)
            e.dma_start(dftn[:, :, :, :], dft_d[:, 4 * T:8 * T].rearrange("p (a b t) -> p a b t", a=TT, b=2))\
                .then_inc(tables_in, 16)
            load(later["four"][0], KT, W8, w2_d, 0)
            ffn(1)
            ffn(2)
            e.wait_ge(chunk_done, later["down2"][0] + 2 * KT)
            e.dma_start(dist[:, :, :, :], dist_d.rearrange("p (a b t) -> p a b t", a=2, b=4)).then_inc(ret_tables_in, 16)
            e.dma_start(dmask[:, :, :, :], dmask_d.rearrange("p (a b t) -> p a b t", a=2, b=2)).then_inc(ret_tables_in, 16)
            e.dma_start(rope2[:, :, :], rope2_d.rearrange("p (a t) -> p a t", a=2)).then_inc(ret_tables_in, 16)
            load(later["rq"][0], 64, W8, w2_d, KT)
            ffn(3)
            e.wait_ge(normed, 8 * (LAYERS + 1 + 2 * 3 + 1))
            e.dma_start(out_d.rearrange("(k p) t -> p k t", p=P), hf[:, :, 0:T]).then_inc(stored, 16)
            e.wait_ge(stored, 16)

        @block.scalar
        def _(e):
            n_sq, n_scaled, n_normed, n_split = Tally(), Tally(), Tally(), Tally()

            def split(lap, mm, c, width):
                e.wait_ge(landed[c % RING], 16 * (lap + ADA_LAPS) + 16)
                if not (isinstance(mm, int) and mm < 2):
                    e.wait_ge(chunk_done, mm - 1)
                e.activation(wh[:, c % 2, 0:width], raw[:, c % RING, 0:width], ACT.Copy).then_inc(hi_done, 1)

            def phase(base, width, after, empty=None, n_own=()):
                m0, _, _, n = base
                lap0 = hybrid_lap(m0)

                def turn(i, widths):
                    for j in range(RING):
                        if widths[j]:
                            split(lap0 + i + (j + 2) // RING, m0 + RING * i + j + 2, j + 2, widths[j])
                        if empty:
                            empty(i, j)

                whole = n // RING - (after != width)
                if whole:
                    with turns(e, whole, *n_own) as i:
                        turn(i, [width] * RING)
                if after != width:
                    turn(whole, [width, width, after, after])

            def hybrid_lap(m0):
                return m0 // RING if isinstance(m0, int) else lap_of[0]

            lap_of = [None]

            def norm(cols_n, gains, dest, has_split, made):
                for k in range(KT):
                    e.wait_ge(*made(k))
                    if k >= 2 or n_sq.n >= 2:
                        e.wait_ge(sq_summed, n_sq.now - 1)
                    e.activation(sq[:, k % 2, 0:cols_n], x[:, k, 0:cols_n], ACT.Square).then_inc(sq_done, 1)
                    n_sq()
                e.wait_ge(sq_summed, n_sq.now)
                e.activation(rs[:, 0:cols_n], ps[:, 7, 0:cols_n], ACT.Sqrt, bias=eps[:, :], scale=1.0 / D)\
                    .then_inc(std_done, 1)
                per = (n_scaled, 2), (n_normed, 2), (n_split, 2 if has_split else 0)
                with turns(e, KT // 2, *per) as i:
                    for j in range(2):
                        e.wait_ge(scaled, n_scaled())
                        if has_split:
                            e.wait_ge(norm_split, n_split())
                        parts = gains(2 * i + j)
                        for q, (g, b) in enumerate(parts):
                            src = tn[:, j, T * q:T * q + T]
                            out = dest(2 * i + j, j, q)
                            if b is None:
                                last = e.activation(out, src, ACT.Copy, scale=g)
                            else:
                                last = e.activation(out, src, ACT.Identity, bias=b, scale=g)
                        last.then_inc(normed, 1)
                        n_normed()

            def after(base, tile, end):
                return lambda k: (emptied_d, 4 + base[1] + end - tile * (KT - 1 - k))

            def col(name, k):
                return cols[:, bass.ds(COLS[name][0] + k, 1)]

            def mod_gains(lj, l, mrow, halves):
                def get(k):
                    return [(gain[:, lj, bass.ds(k, 1), q], mod[:, l, bass.ds(mrow * KT + k, 1), q])
                            for q in range(halves)]
                return get

            def to_hn(k, j, q):
                return hn[:, j, T * q:T * q + T]

            e.wait_ge(eps_set, 2)
            e.wait_ge(consts_in, 96)
            e.activation(sc[:, :, :].rearrange("p k c -> p (k c)"), cols[:, COLS["c"][0]:COLS["c"][0] + 16],
                         ACT.Silu).then_inc(c_silu, 1)
            e.activation(spare[:, 5:6], eps[:, :], ACT.Copy).then_inc(emptied_a, 4)
            for c in range(2):
                split(0, c, c, W8)

            n_heads = Tally()
            n_relu, n_exp, n_copy = Tally(), Tally(), Tally()
            per = ((n_sq, KT), (n_scaled, KT), (n_normed, KT), (n_split, 2 * KT + KT),
                   (n_relu, TT), (n_exp, NU), (n_copy, NU), (n_heads, 192))
            with turns(e, LAYERS, *per) as L:
                def laps(name):
                    lap_of[0] = hybrid[name][0] // RING + L * (PER_LAYER // RING)
                    return of_layer(name, L)

                norm(T, lambda k: [(col("norm_g", L * KT + k), None)], to_hn, True,
                     lambda k: (emptied_d, 4 + of_layer("qk", L)[1]))
                phase(laps("qk"), W8, WV)
                phase(laps("vn"), WV, W8)
                e.wait_ge(emptied_d, 4 + of_layer("qk", L)[1] + QK)
                for jq in range(4):
                    for r in range(2):
                        dst = 64 * (jq % 2) + 32 * r
                        e.dma_start(heads[dst:dst + 32, jq // 2:NPOS // 2:2, :],
                                    rot[32 * jq:32 * jq + 32, r::2, :]).then_inc(heads_in, 16)
                for jq, half in ((2, 1), (3, 0)):
                    for r in range(2):
                        dst = 64 * half + 32 * r
                        e.dma_start(heads[dst:dst + 32, NPOS // 2, :], rot[32 * jq:32 * jq + 32, QK - 2 + r, :])\
                            .then_inc(heads_in, 16)
                n_heads(192)

                def silu_gate(i, j):
                    e.wait_ge(chunk_done, of_layer("gate", L)[0] + RING * i + j + 1)
                    e.activation(flat(sg, RING * i + j), ps[:, j, 0:T], ACT.Silu).then_inc(emptied_a, 1)

                def mix_gate(i, j):
                    e.wait_ge(chunk_done, of_layer("mixg", L)[0] + RING * i + j + 1)
                    e.activation(flat(mg, RING * i + j), ps[:, j, 0:T], ACT.Sigmoid).then_inc(emptied_a, 1)

                phase(laps("gate"), W8, W8, silu_gate)
                phase(laps("mixg"), W8, W8, mix_gate)

                e.wait_ge(heads_in, n_heads.now)
                for qt in range(TT):
                    w = P * (qt + 1)
                    e.wait_ge(logits, n_relu() )
                    if qt:
                        e.wait_ge(idx_summed, n_relu.now - 1)
                    e.activation(relu[:, :, 0:2 * w], ps[:, 2 * qt:2 * qt + 2, 0:2 * w], ACT.Relu)\
                        .then_inc(relu_done, 1)

                def exp(u):
                    w = unit_width(u)
                    e.wait_ge(maxed, n_exp())
                    if u >= 2:
                        e.wait_ge(turned, n_exp.now - 2)
                    slot = ps[:, 2 * (u % 2):2 * (u % 2) + 2, :].rearrange("p a t -> p (a t)")
                    e.activation(prob[:, u % 2, 0:w], slot[:, 0:w], ACT.Exp, bias=nmax[:, u:u + 1],
                                 scale=HD ** -0.5, accum_out=rsum[:, u:u + 1]).then_inc(exped, 1)

                exp(0)
                for u in range(NU):
                    if u + 1 < NU:
                        exp(u + 1)
                    w = unit_width(u)
                    e.wait_ge(turned, n_copy())
                    if u >= 2:
                        e.wait_ge(weighed, n_copy.now - 2)
                    e.activation(probT[:, u % 2, 0:w], ps[:, 4:6, :].rearrange("p a t -> p (a t)")[:, 0:w],
                                 ACT.Copy).then_inc(copied, 1)

                phase(laps("br"), W8, W8)
                phase(laps("out"), W8, W8)
                n_split(2 * KT)

            norm(T, lambda k: [(col("final_norm_g", k), None)], lambda k, j, q: flat(x, k, 0, T), False,
                 after(later["up0"], 1, 0))

            def ffn(f, l, jn, halves, made, width_after):
                norm(halves * T, mod_gains(3 * l + jn, l, 3 * jn, halves), to_hn, True, made)
                base = later[f"up{f}"]

                def silu(i, j):
                    if j % 2 == 0:
                        return
                    e.wait_ge(chunk_done, base[0] + RING * i + j)
                    e.wait_ge(emptied_d, 4 + base[1] + RING * i + j - 1 - 2)
                    e.activation(tn[:, j // 2, 0:halves * T], ps[:, j - 1, 0:halves * T], ACT.Silu)\
                        .then_inc(act_step, 1)

                phase(base, W8, WD, silu)
                phase(later[f"down{f}"], WD, width_after)

            ffn(0, 0, 0, 2, lambda k: (normed, n_normed.now), W8)
            norm(2 * T, mod_gains(1, 0, 3, 2), lambda k, j, q: flat(hf, k, T * q, T), False,
                 after(later["down0"], 2, 16))
            phase(later["four"], W8, W8)
            ffn(1, 0, 2, 2, after(later["four"], 1, 8), W8)
            ffn(2, 1, 0, 2, after(later["down1"], 2, 16), W8)

            norm(2 * T, mod_gains(4, 1, 3, 2), to_hn, True, after(later["down2"], 2, 16))
            phase(later["rq"], W8, W8)
            phase(later["rk"], W8, W8)
            phase(later["rv"], W8, W8)

            def silu_ret(i, j):
                e.wait_ge(chunk_done, later["rg"][0] + RING * i + j + 1)
                e.activation(flat(sgr, RING * i + j), ps[:, j, 0:T], ACT.Silu).then_inc(emptied_a, 1)

            phase(later["rg"], W8, W8, silu_ret)
            e.wait_ge(ret_tables_in, 48)
            for h in range(RH):
                if h:
                    e.wait_ge(rs_out, 4 * h)
                else:
                    e.wait_ge(mod_ready, 2)
                for b in range(2):
                    e.activation(dec[:, b, :, :], dist[:, b, :, :], ACT.Exp,
                                 scale=lg[:, RH * b + h:RH * b + h + 1]).then_inc(decayed, 1)
                e.wait_ge(rc_done, 4 * h + 4)
                e.activation(rs[:, 0:T], ps[:, 7, 0:T], ACT.Sqrt, bias=eps[:, :], scale=1.0 / RDV)\
                    .then_inc(rstd, 1)
            phase(later["ro"], W8, W8)
            ffn(3, 1, 2, 1, after(later["ro"], 2, 16), None)
            norm(T, lambda k: [(col("final_g_2", k), None)], lambda k, j, q: flat(hf, k, 0, T), False,
                 after(later["down3"], 2, 16))

        @block.gpsimd
        def _(e):
            n_hi, n_nhi = Tally(), Tally()
            e.memset(eps[:, :], EPS).then_inc(eps_set, 1)
            e.memset(ones[:, :], 1.0).then_inc(eps_set, 1)
            e.memset(spare[:, 0:1], 0.0).then_inc(lo_done, RING)
            e.memset(spare[:, 1:2], 0.0).then_inc(norm_split, 2)

            def split(mm, c, width):
                e.wait_ge(hi_done, mm + 1)
                e.tensor_tensor(wl[:, c % 2, 0:width], raw[:, c % RING, 0:width],
                                wh[:, c % 2, 0:width].bitcast(F32), ALU.subtract).then_inc(lo_done, 1)

            def phase(base, width, after, extra=None, n_own=()):
                m0, n = base[0], base[3]

                def turn(i, widths):
                    for j in range(RING):
                        if widths[j]:
                            split(m0 + RING * i + j + 2, j + 2, widths[j])
                        if extra:
                            extra(i, j)

                whole = n // RING - (after != width)
                if whole:
                    with turns(e, whole, *n_own) as i:
                        turn(i, [width] * RING)
                if after != width:
                    turn(whole, [width, width, after, after])

            def norm_low(cols_n, pos=0, src=None):
                with turns(e, KT // 2, (n_nhi, 2)) as i:
                    for j in range(2):
                        e.wait_ge(norm_hi, n_nhi())
                        e.tensor_tensor(flat(hl, 2 * i + j, pos, cols_n), hn[:, j, 0:cols_n],
                                        flat(hh, 2 * i + j, pos, cols_n).bitcast(F32), ALU.subtract)\
                            .then_inc(norm_split, 1)

            for c in range(2):
                split(c, c, W8)
            with turns(e, LAYERS, (n_nhi, 3 * KT)) as L:
                norm_low(T)
                phase(of_layer("qk", L), W8, WV)
                phase(of_layer("vn", L), WV, W8)
                phase(of_layer("gate", L), W8, W8)
                phase(of_layer("mixg", L), W8, W8)
                norm_low(T, T)

                def merged_low(i, j):
                    e.wait_ge(norm_hi, n_nhi())
                    e.tensor_tensor(flat(hl, RING * i + j, 0, T), hn[:, j % 2, 0:T],
                                    flat(hh, RING * i + j, 0, T).bitcast(F32), ALU.subtract)\
                        .then_inc(norm_split, 1)

                phase(of_layer("br", L), W8, W8, merged_low, ((n_nhi, RING),))
                phase(of_layer("out", L), W8, W8)

            n_act = Tally()

            def ffn(f, halves, after):
                norm_low(halves * T)

                def act_low(i, j):
                    if j % 2 == 0:
                        return
                    e.wait_ge(act_hi, n_act())
                    e.tensor_tensor(flat(al, 2 * i + j // 2, 0, halves * T), hn[:, j // 2, 0:halves * T],
                                    flat(ah, 2 * i + j // 2, 0, halves * T).bitcast(F32), ALU.subtract)\
                        .then_inc(act_split, 1)

                phase(later[f"up{f}"], W8, WD, act_low, ((n_act, 2),))
                phase(later[f"down{f}"], WD, after)

            ffn(0, 2, W8)
            phase(later["four"], W8, W8)
            ffn(1, 2, W8)
            ffn(2, 2, W8)
            norm_low(2 * T)
            for name in ("rq", "rk", "rv", "rg"):
                phase(later[name], W8, W8)
            phase(later["ro"], W8, W8)
            ffn(3, 1, None)

        @block.vector
        def _(e):
            step = Tally()
            n_std, n_scaled, n_normed, n_nhi, n_nsplit = Tally(), Tally(), Tally(), Tally(), Tally()

            def norm(cols_n, split):
                e.wait_ge(std_done, n_std())
                e.reciprocal(rs[:, 0:cols_n], rs[:, 0:cols_n]).then_inc(dve_step, 1)
                e.wait_ge(dve_step, step())

                def scale(k, j):
                    e.tensor_tensor(tn[:, j, 0:cols_n], flat(x, k, 0, cols_n), rs[:, 0:cols_n], ALU.mult)\
                        .then_inc(scaled, 1)

                def high(k, j):
                    e.wait_ge(normed, n_normed())
                    if split:
                        e.tensor_copy(flat(hh, k, 0, cols_n), hn[:, j, 0:cols_n]).then_inc(norm_hi, 1)
                        n_nhi()

                scale(0, 0)
                scale(1, 1)
                with turns(e, KT // 2 - 1, (n_normed, 2), (n_nhi, 2 if split else 0)) as i:
                    for j in range(2):
                        high(2 * i + j, j)
                        scale(2 * i + j + 2, j)
                high(KT - 2, 0)
                high(KT - 1, 1)
                n_scaled(KT)
                if split:
                    n_nsplit(KT)

            def own(k):
                e.wait_ge(dve_step, step(k))

            e.memset(spare[:, 2:3], 0.0).then_inc(emptied_d, 4)
            e.memset(spare[:, 3:4], 0.0).then_inc(act_split, 1)
            e.wait_ge(ada_done, LAYERS * ADA)
            e.wait_ge(consts_in, 96)
            b0 = COLS["ada_b"][0]
            for q in range(2):
                e.tensor_tensor(mod[:, :, :, q].rearrange("p l c -> p (l c)"), ps[:, 0, q:2 * LAYERS * ADA:2],
                                cols[:, b0:b0 + LAYERS * ADA], ALU.add).then_inc(dve_step, 1)
            own(2)
            g0 = COLS["norm_g_2"][0]
            for l in range(LAYERS):
                for jn in range(3):
                    for q in range(2):
                        k0 = g0 + (3 * l + jn) * KT
                        e.scalar_tensor_tensor(out=gain[:, 3 * l + jn, :, q], scalar=1.0,
                                               in0=mod[:, l, (3 * jn + 1) * KT:(3 * jn + 2) * KT, q],
                                               in1=cols[:, k0:k0 + KT], op0=ALU.add, op1=ALU.mult)\
                            .then_inc(dve_step, 1)
                        e.tensor_scalar(gate[:, 3 * l + jn, :, q],
                                        mod[:, l, (3 * jn + 2) * KT:(3 * jn + 3) * KT, q],
                                        1.0 if jn == 1 else 0.5, None, ALU.mult).then_inc(dve_step, 1)
            own(24)
            e.memset(spare[:, 4:5], 0.0).then_inc(mod_ready, 1)
            dc = COLS["decay"][0]
            e.scalar_tensor_tensor(out=lg[:, :], in0=cols[:, dc:dc + 8], scalar=-1.0, in1=cols[:, dc:dc + 8],
                                   op0=ALU.mult, op1=ALU.min).then_inc(mod_ready, 1)

            def rotate(ps1, ps2, cs, sn, out1, out2, ready, count):
                e.tensor_tensor(tn[:, 0, 0:T], ps1, cs, ALU.mult).then_inc(dve_step, 1)
                e.tensor_tensor(tn[:, 0, T:2 * T], ps2, sn, ALU.mult).then_inc(dve_step, 1)
                e.tensor_tensor(tn[:, 1, 0:T], ps1, sn, ALU.mult).then_inc(dve_step, 1)
                e.tensor_tensor(tn[:, 1, T:2 * T], ps2, cs, ALU.mult).then_inc(dve_step, 1)
                own(4)
                e.tensor_tensor(out1, tn[:, 0, 0:T], tn[:, 0, T:2 * T], ALU.subtract).then_inc(dve_step, 1)
                own(1)
                e.tensor_tensor(out2, tn[:, 1, 0:T], tn[:, 1, T:2 * T], ALU.add).then_inc(ready, count)

            n_relu, n_scored, n_weighed, n_yT = Tally(), Tally(), Tally(), Tally()
            idx_steps = TT * (3 + 1 + 2 * (TOPK // 8) + 2)
            STEPS_L = 1 + 5 * (QK // 2) + VG + 1 + idx_steps + 2 * NU + KT + 4 * BR
            per = ((step, STEPS_L), (n_std, 1), (n_scaled, KT), (n_normed, KT), (n_nhi, 3 * KT), (n_nsplit, 3 * KT),
                   (n_relu, TT), (n_scored, NU), (n_weighed, NU), (n_yT, KT))
            with turns(e, LAYERS, *per) as L:
                norm(T, True)
                m0, d0, _, _ = of_layer("qk", L)
                with turns(e, QK // RING, (step, 10)) as i:
                    for j in (0, 2):
                        e.wait_ge(chunk_done, m0 + RING * i + j + 2)
                        e.wait_ge(emptied_d, 4 + d0 + RING * i + j)
                        rotate(ps[:, j, 0:T], ps[:, j + 1, 0:T], rope[:, 0, :], rope[:, 1, :],
                               flat(rot, RING * i + j), flat(rot, RING * i + j + 1), emptied_d, 2)
                m0, d0, _, _ = of_layer("vn", L)
                for g in range(VG):
                    e.wait_ge(chunk_done, m0 + 4 * g + 4)
                    for tt in range(TT):
                        last = e.tensor_copy(vn[:, tt, VW * g:VW * g + VW], ps[:, 4 + 2 * (g % 2) + tt, 0:VW])
                        if tt == 0:
                            last.then_inc(dve_step, 1)
                            step()
                    last.then_inc(emptied_d, 4)
                e.wait_ge(emptied_d, 4 + d0 + VN)
                e.tensor_scalar(iw[:, :, :], vn[:, :, 1216:1220], 1.0 / 16, None, ALU.mult).then_inc(dve_step, 1)
                own(1)

                e.wait_ge(heads_in, 192 * L + 192)
                for qt in range(TT):
                    w = P * (qt + 1)
                    acc = idx[:, qt, 0:w]
                    e.wait_ge(relu_done, n_relu())
                    e.tensor_scalar(acc, relu[:, 0, 0:w], iw[:, qt, 0:1], None, ALU.mult).then_inc(dve_step, 1)
                    own(1)
                    for h in range(1, 4):
                        last = e.scalar_tensor_tensor(out=acc, in0=relu[:, h % 2, w * (h // 2):w * (h // 2) + w], scalar=iw[:, qt, h:h + 1],
                                                      in1=acc, op0=ALU.mult, op1=ALU.add)
                        if h < 3:
                            last.then_inc(dve_step, 1)
                            own(1)
                    last.then_inc(idx_summed, 1)
                    e.wait_ge(idx_summed, n_relu.now)
                    tri = mask[:, 0:P]
                    e.tensor_tensor(idx[:, qt, w - P:w], idx[:, qt, w - P:w], tri, ALU.add).then_inc(dve_step, 1)
                    own(1)
                    for _ in range(TOPK // 8):
                        e.sem_inc(passed, 1)
                        e.max(top8[:, :], acc).then_inc(dve_step, 1)
                        own(1)
                        e.sem_inc(passed, 1)
                        e.match_replace(acc, top8[:, :], acc, TAKEN).then_inc(dve_step, 1)
                        own(1)
                    pk = picked[:, P * qt:P * qt + w]
                    e.tensor_scalar(pk, acc, TAKEN / 2, NEG, ALU.is_gt, ALU.mult).then_inc(dve_step, 1)
                    own(1)
                    e.tensor_tensor(pk[:, w - P:w], pk[:, w - P:w], tri, ALU.add).then_inc(dve_step, 1)
                    own(1)

                def maximum(u):
                    w = unit_width(u)
                    slot = ps[:, 2 * (u % 2):2 * (u % 2) + 2, :].rearrange("p a t -> p (a t)")
                    e.wait_ge(scored, n_scored())
                    e.reduce_max(rmax[:, u:u + 1], slot[:, 0:w], axis=AX_X).then_inc(dve_step, 1)
                    own(1)
                    e.tensor_scalar(nmax[:, u:u + 1], rmax[:, u:u + 1], -HD ** -0.5, None, ALU.mult)\
                        .then_inc(maxed, 1)

                def finish(u):
                    qt, _, _, yc = UNITS[u]
                    e.wait_ge(weighed, n_weighed())
                    e.reciprocal(rrec[:, u:u + 1], rsum[:, u:u + 1]).then_inc(dve_step, 1)
                    own(1)
                    e.tensor_scalar(y[:, qt, yc:yc + HD], ps[:, 6 + u % 2, 0:HD], rrec[:, u:u + 1], None, ALU.mult)\
                        .then_inc(y_done, 1)

                for u in range(NU):
                    maximum(u)
                    if u >= 2:
                        finish(u - 2)
                finish(NU - 2)
                finish(NU - 1)

                for f in range(KT):
                    e.wait_ge(yT_done, n_yT())
                    e.wait_ge(norm_split, n_nsplit.now + f + 1)
                    e.tensor_tensor(hn[:, f % 2, 0:T], ps[:, f % 4, 0:T], sg[:, f, :], ALU.mult).then_inc(dve_step, 1)
                    own(1)
                    e.tensor_copy(hh[:, f, T:2 * T], hn[:, f % 2, 0:T]).then_inc(norm_hi, 1)
                n_nhi(KT)
                n_nsplit(KT)

                m0, d0, _, _ = of_layer("br", L)
                with turns(e, BR // RING, (step, 4 * RING), (n_nhi, RING), (n_nsplit, RING)) as i:
                    for j in range(RING):
                        bank = 4 * (j % 2)
                        e.wait_ge(chunk_done, m0 + RING * i + j + 1)
                        for b in range(3):
                            last = e.tensor_tensor(tn[:, b // 2, T * (b % 2):T * (b % 2) + T], ps[:, bank + b, 0:T],
                                                   flat(mg, b * KT + RING * i + j), ALU.mult)
                            if b < 2:
                                last.then_inc(dve_step, 1)
                        last.then_inc(emptied_d, 1)
                        e.wait_ge(emptied_d, 4 + d0 + RING * i + j + 1)
                        e.tensor_tensor(tn[:, 0, 0:T], tn[:, 0, 0:T], tn[:, 0, T:2 * T], ALU.add).then_inc(dve_step, 1)
                        own(3)
                        e.wait_ge(norm_split, n_nsplit())
                        e.tensor_tensor(hn[:, j % 2, 0:T], tn[:, 0, 0:T], tn[:, 1, 0:T], ALU.add).then_inc(dve_step, 1)
                        own(1)
                        e.tensor_copy(flat(hh, RING * i + j, 0, T), hn[:, j % 2, 0:T]).then_inc(norm_hi, 1)
                        n_nhi()
                m0, d0, _, _ = of_layer("out", L)
                with turns(e, OUT // RING) as i:
                    for j in range(RING):
                        e.wait_ge(chunk_done, m0 + RING * i + j + 1)
                        xs = flat(x, RING * i + j, 0, T)
                        e.tensor_tensor(xs, ps[:, j, 0:T], xs, ALU.add).then_inc(emptied_d, 1)
                e.wait_ge(emptied_d, 4 + d0 + OUT)

            norm(T, False)

            n_act = Tally()

            def ffn(f, l, jn, halves):
                norm(halves * T, True)
                w = halves * T
                m0, d0, _, _ = later[f"up{f}"]
                with turns(e, 2 * FT // RING, (n_act, 2)) as i:
                    for j in (0, 1):
                        e.wait_ge(chunk_done, m0 + RING * i + 2 * j + 2)
                        e.wait_ge(act_step, n_act())
                        e.wait_ge(act_split, n_act.now - 1)
                        e.tensor_tensor(hn[:, j, 0:w], tn[:, j, 0:w], ps[:, 2 * j + 1, 0:w], ALU.mult)\
                            .then_inc(emptied_d, 2)
                        e.wait_ge(emptied_d, 4 + d0 + RING * i + 2 * j + 2)
                        e.tensor_copy(flat(ah, 2 * i + j, 0, w), hn[:, j, 0:w]).then_inc(act_hi, 1)
                m0, d0, _, _ = later[f"down{f}"]
                with turns(e, KT // 2, (step, 2 * (halves - 1))) as i:
                    for j in range(2):
                        e.wait_ge(chunk_done, m0 + RING * i + 2 * j + 2)
                        for q in range(halves):
                            xs = flat(x, 2 * i + j, T * q, T)
                            last = e.scalar_tensor_tensor(
                                out=xs, in0=ps[:, j, T * q:T * q + T],
                                scalar=gate[:, 3 * l + jn, bass.ds(2 * i + j, 1), q], in1=xs,
                                op0=ALU.mult, op1=ALU.add)
                            if q < halves - 1:
                                last.then_inc(dve_step, 1)
                                step()
                        last.then_inc(emptied_d, 2)
                e.wait_ge(emptied_d, 4 + d0 + 2 * KT)

            ffn(0, 0, 0, 2)

            norm(2 * T, False)
            for n in range(16):
                b, r = divmod(n, 8)
                g, tt = divmod(r, 2)
                e.wait_ge(f1_done, n + 1)
                e.tensor_copy(pq[:, b, tt, g, :], ps[:, n % 4, :]).then_inc(f1_out, 1)
            for n in range(16):
                b, f = divmod(n, 8)
                e.wait_ge(f2_done, n + 1)
                dst = hh[:, f, T * b:T * b + T]
                e.tensor_copy(dst, ps[:, 4 + n % 4, 0:T]).then_inc(dve_step, 1)
                own(1)
                e.tensor_tensor(hl[:, f, T * b:T * b + T], ps[:, 4 + n % 4, 0:T], dst.bitcast(F32), ALU.subtract)\
                    .then_inc(f2_hi, 1)
            m0, d0, _, _ = later["four"]
            fb = COLS["four_b"][0]
            with turns(e, KT // RING, (step, 2 * RING)) as i:
                for j in range(RING):
                    o = RING * i + j
                    e.wait_ge(chunk_done, m0 + RING * i + j + 1)
                    e.wait_ge(emptied_d, 4 + d0 + RING * i + j)
                    for q in range(2):
                        e.tensor_scalar(tn[:, 0, T * q:T * q + T], ps[:, j, T * q:T * q + T],
                                        cols[:, bass.ds(fb + o, 1)], gate[:, 1, bass.ds(o, 1), q], ALU.add, ALU.mult)\
                            .then_inc(dve_step, 1)
                    own(2)
                    xs = flat(x, o)
                    e.tensor_tensor(xs, xs, tn[:, 0, :], ALU.add).then_inc(emptied_d, 1)
            e.wait_ge(emptied_d, 4 + d0 + KT)

            ffn(1, 0, 2, 2)
            ffn(2, 1, 0, 2)

            norm(2 * T, True)
            e.wait_ge(ret_tables_in, 48)
            for name, dst in (("rq", qT), ("rk", kT)):
                m0, d0, _, _ = later[name]
                with turns(e, KT // RING, (step, 14 if name == "rk" else 10)) as i:
                    for j in (0, 2):
                        e.wait_ge(chunk_done, m0 + RING * i + j + 2)
                        e.wait_ge(emptied_d, 4 + d0 + RING * i + j)
                        if name == "rk":
                            for b in range(2):
                                e.tensor_copy(flat(kT, RING * i + j + b, T, T), ps[:, j + b, T:2 * T])\
                                    .then_inc(dve_step, 1)
                                step()
                        rotate(ps[:, j, 0:T], ps[:, j + 1, 0:T], rope2[:, 0, :], rope2[:, 1, :],
                               flat(dst, RING * i + j, 0, T), flat(dst, RING * i + j + 1, 0, T), emptied_d, 2)
            m0, d0, _, _ = later["rv"]
            for g in range(RH):
                e.wait_ge(chunk_done, m0 + 4 * g + 4)
                for tt in range(2 * TT):
                    last = e.tensor_copy(vr[:, tt, RDV * g:RDV * g + RDV], ps[:, 4 * (g % 2) + tt, :])
                    if tt < 2 * TT - 1:
                        last.then_inc(dve_step, 1)
                        step()
                last.then_inc(emptied_d, 4)
            for h in range(RH):
                e.wait_ge(decayed, 2 * h + 2)
                for b in range(2):
                    e.tensor_tensor(dec[:, b, 0:2, :], dec[:, b, 0:2, :], dmask[:, b, :, :], ALU.mult)\
                        .then_inc(dve_step, 1)
                own(2)
                e.tensor_tensor(dec[:, 0, :, :], dec[:, 0, :, :], dec[:, 1, :, :], ALU.add).then_inc(dve_step, 1)
                own(1)
                for jt in range(4):
                    e.wait_ge(rs_done, 4 * h + jt + 1)
                    e.scalar_tensor_tensor(out=sT[:, jt, :], in0=ps[:, jt % 2, 0:T], scalar=1.0 / 16,
                                           in1=dec[:, 0, jt, :], op0=ALU.mult, op1=ALU.mult).then_inc(rs_out, 1)
                for dv in range(4):
                    e.wait_ge(ry_done, 4 * h + dv + 1)
                    e.tensor_copy(yr[:, dv, :], ps[:, 2 + dv % 2, 0:T]).then_inc(ry_out, 1)
                e.wait_ge(rmean, h + 1)
                e.tensor_scalar(tn[:, 0, 0:T], ps[:, 6, 0:T], 1.0 / RDV, None, ALU.mult).then_inc(dve_step, 1)
                own(1)
                for dv in range(4):
                    e.tensor_tensor(yr[:, dv, :], yr[:, dv, :], tn[:, 0, 0:T], ALU.subtract).then_inc(dve_step, 1)
                own(4)
                for dv in range(4):
                    if h or dv >= 2:
                        e.wait_ge(rc_done, 4 * h + dv - 1)
                    e.tensor_tensor(sq[:, dv % 2, 0:T], yr[:, dv, :], yr[:, dv, :], ALU.mult).then_inc(rcent, 1)
                e.wait_ge(rstd, h + 1)
                e.reciprocal(rs[:, 0:T], rs[:, 0:T]).then_inc(dve_step, 1)
                own(1)
                for dv in range(4):
                    f = 4 * h + dv
                    e.tensor_tensor(yr[:, dv, :], yr[:, dv, :], rs[:, 0:T], ALU.mult).then_inc(dve_step, 1)
                    own(1)
                    e.tensor_tensor(yr[:, dv, :], yr[:, dv, :], sgr[:, f, :], ALU.mult).then_inc(dve_step, 1)
                    own(1)
                    dst = hh[:, f // 2, T * (f % 2):T * (f % 2) + T]
                    e.tensor_copy(dst, yr[:, dv, :]).then_inc(dve_step, 1)
                    own(1)
                    e.tensor_tensor(hl[:, f // 2, T * (f % 2):T * (f % 2) + T], yr[:, dv, :], dst.bitcast(F32),
                                    ALU.subtract).then_inc(rgn, 1)
                e.wait_ge(rgn, 4 * h + 4)
            m0, d0, _, _ = later["ro"]
            with turns(e, KT // 2) as i:
                for j in range(2):
                    e.wait_ge(chunk_done, m0 + RING * i + 2 * j + 2)
                    xs = flat(x, 2 * i + j, 0, T)
                    e.scalar_tensor_tensor(out=xs, in0=ps[:, j, 0:T], scalar=gate[:, 4, bass.ds(2 * i + j, 1), 0],
                                           in1=xs, op0=ALU.mult, op1=ALU.add).then_inc(emptied_d, 2)
            e.wait_ge(emptied_d, 4 + d0 + 2 * KT)
            ffn(3, 1, 2, 1)
            norm(T, False)

        @block.tensor
        def _(e):
            n_sq, n_split = Tally(), Tally()

            def norm(cols_n, split):
                for k in range(KT):
                    e.wait_ge(sq_done, n_sq())
                    e.matmul(ps[:, 7, 0:cols_n], ones[:, :], sq[:, k % 2, 0:cols_n], start=(k == 0),
                             stop=(k == KT - 1)).then_inc(sq_summed, 1)
                if split:
                    e.wait_ge(norm_split, n_split(KT) + 2)

            def products(bank, j, tiles, k0, move, lo, n, first, last):
                mh, ml = move
                for t in tiles:
                    w = slice(t * P, t * P + P)
                    k = k0 + t
                    hi, low = mh[:, k, lo:lo + n], ml[:, k, lo:lo + n]
                    e.matmul(ps[:, bank, 0:n], wh[:, j % 2, w], hi, start=(first and t == tiles[0]), stop=False)
                    e.matmul(ps[:, bank, 0:n], wh[:, j % 2, w], low, start=False, stop=False)
                    end = e.matmul(ps[:, bank, 0:n], wl[:, j % 2, w], hi, start=False,
                                   stop=(last and t == tiles[-1]))
                return end

            h = (hh, hl)

            def plain(base, cols_n, freed, lo=0):
                m0, d0, a0, n = base
                e.sem_inc(passed, 1)
                with e.Fori(0, n // RING) as i:
                    for j in range(RING):
                        e.wait_ge(lo_done, RING + m0 + RING * i + j + 1)
                        f0 = d0 if freed is emptied_d else a0
                        e.wait_ge(freed, f0 + RING * i + j + 1)
                        products(j, j, range(KT), 0, h, lo, cols_n, True, True).then_inc(chunk_done, 1)

            def natural(j, c, width, bank, tts, first, last):
                for tt in range(tts):
                    for t in range(2):
                        tok = slice(P * tt, P * tt + P)
                        w = slice(t * width, t * width + width)
                        k = 2 * c + t
                        out = ps[:, bank + tt, 0:width]
                        e.matmul(out, hh[:, k, tok], wh[:, j % 2, w], start=(first and t == 0), stop=False)
                        e.matmul(out, hh[:, k, tok], wl[:, j % 2, w], start=False, stop=False)
                        end = e.matmul(out, hl[:, k, tok], wh[:, j % 2, w], start=False, stop=(last and t == 1))
                return end

            e.wait_ge(c_silu, 1)
            with e.Fori(0, ADA_LAPS) as i:
                for j in range(RING):
                    e.wait_ge(landed[j], 16 * i + 16)
                    for k in range(KT):
                        end = e.matmul(ps[:, 0, bass.ds(2 * (RING * i + j), 2)], raw[:, j, k * P:k * P + P],
                                       sc[:, k, :], start=(k == 0), stop=(k == KT - 1))
                    end.then_inc(ada_done, 1)
            e.wait_ge(mod_ready, 1)

            n_y, n_sc, n_ex, n_co = Tally(), Tally(), Tally(), Tally()
            n_relu, n_yTo = Tally(), Tally()
            per = ((n_sq, KT), (n_split, 3 * KT), (n_y, NU), (n_ex, NU), (n_co, NU), (n_relu, TT))
            with turns(e, LAYERS, *per) as L:
                norm(T, True)
                plain(of_layer("qk", L), T, emptied_d)
                m0, d0, a0, _ = of_layer("vn", L)
                for g in range(VG):
                    for c in range(4):
                        e.wait_ge(lo_done, RING + m0 + 4 * g + c + 1)
                        if g == 2 and c == 0:
                            e.wait_ge(emptied_d, 4 + d0 + 4)
                        natural(c, c, VW, 4 + 2 * (g % 2), TT, c == 0, c == 3).then_inc(chunk_done, 1)
                e.wait_ge(emptied_d, 4 + d0)
                plain(of_layer("gate", L), T, emptied_a)
                plain(of_layer("mixg", L), T, emptied_a)

                m0, d0, a0, _ = of_layer("br", L)
                e.wait_ge(emptied_d, 4 + d0)
                e.wait_ge(emptied_a, 4 + a0)
                e.wait_ge(heads_in, 192 * L + 192)

                def head(pl, lo, n):
                    tile, half = pl
                    return heads[64 * half:64 * half + 64, tile, lo:lo + n]

                for qt in range(TT):
                    w = P * (qt + 1)
                    for ih in range(4):
                        pos = IQ + ih
                        key = (24, 0) if pos % 2 == 0 else (23, 1)
                        lo = w * (ih // 2)
                        end = e.matmul(ps[:, 2 * qt + ih % 2, lo:lo + w],
                                       head((pos // 2, pos % 2), P * qt, P), head(key, 0, w), start=True, stop=True)
                    end.then_inc(logits, 1)

                def score(u):
                    qt, segs, _, _ = UNITS[u]
                    w = P * (qt + 1)
                    if u < 2:
                        if u == 0:
                            e.wait_ge(relu_done, n_relu(TT))
                    else:
                        e.wait_ge(exped, n_ex.now + u - 1)
                    if u == 20:
                        e.wait_ge(maxed, NU * L + 1)
                    for s, (qp, kp, mk) in enumerate(segs):
                        at_ = w * s
                        bank, lo = 2 * (u % 2) + at_ // 512, at_ % 512
                        e.matmul(ps[:, bank, lo:lo + w], head(qp, P * qt, P), head(kp, 0, w), start=True, stop=False)
                        if mk == "picked":
                            out, src = ps[:, bank, lo:lo + w], picked[:, P * qt:P * qt + w]
                        elif (mk, qt) == ("tri", 1):
                            out, src = ps[:, bank, lo + P:lo + w], mask[:, 0:P]
                        else:
                            m_at, m_n = MASK[mk, qt]
                            out, src = ps[:, bank, lo:lo + w], mask[:, m_at:m_at + m_n]
                        end = e.matmul(out, identb[:, :], src, start=False, stop=True)
                    end.then_inc(scored, 1)

                def weigh(u):
                    qt, segs, vcols, _ = UNITS[u]
                    e.wait_ge(copied, n_co.now + u + 1)
                    if u >= 2:
                        e.wait_ge(y_done, n_y.now + u - 1)
                    blocks = [(s, kt) for s in range(len(segs)) for kt in range(qt + 1)]
                    for b, (s, kt) in enumerate(blocks):
                        end = e.matmul(ps[:, 6 + u % 2, 0:HD], probT[:, u % 2, b * P:b * P + P],
                                       vn[:, kt, vcols[s]:vcols[s] + HD], start=(b == 0), stop=(b == len(blocks) - 1))
                    end.then_inc(weighed, 1)

                score(0)
                for u in range(NU):
                    if u + 1 < NU:
                        score(u + 1)
                    if u:
                        weigh(u - 1)
                    e.wait_ge(exped, n_ex.now + u + 1)
                    if u:
                        e.wait_ge(copied, n_co.now + u)
                    for b in range(unit_width(u) // P):
                        end = e.transpose(ps[:, 4 + b // 4, (b % 4) * P:(b % 4) * P + P],
                                          prob[:, u % 2, b * P:b * P + P], ident[:, :])
                    end.then_inc(turned, 1)
                weigh(NU - 1)
                n_ex(NU)
                n_co(NU)
                n_y(NU)
                e.wait_ge(y_done, n_y.now)
                for f in range(KT):
                    if f >= 4:
                        e.wait_ge(norm_hi, 3 * KT * L + LAYERS * 0 + KT + f - 3)
                    for tt in range(TT):
                        end = e.transpose(ps[:, f % 4, P * tt:P * tt + P], y[:, tt, f * P:f * P + P], ident[:, :])
                    end.then_inc(yT_done, 1)
                e.wait_ge(norm_split, n_split(KT) + 2)

                m0, d0, a0, n = of_layer("br", L)
                e.sem_inc(passed, 1)
                with e.Fori(0, n // RING) as i:
                    for j in range(RING):
                        e.wait_ge(lo_done, RING + m0 + RING * i + j + 1)
                        e.wait_ge(emptied_d, d0 + RING * i + j + 3)
                        bank = 4 * (j % 2)
                        products(bank, j, range(0, 3), 0, h, T, T, True, True)
                        products(bank + 1, j, range(3, 6), 0, h, T, T, True, True)
                        products(bank + 2, j, range(6, 8), 0, h, T, T, True, True).then_inc(chunk_done, 1)
                e.wait_ge(norm_split, n_split(KT) + 2)
                plain(of_layer("out", L), T, emptied_d)

            norm(T, False)
            n_act = Tally()

            def ffn(f, halves):
                w = halves * T
                norm(w, True)
                m0, d0, a0, n = later[f"up{f}"]
                with e.Fori(0, n // RING) as i:
                    for j in range(RING):
                        e.wait_ge(lo_done, RING + m0 + RING * i + j + 1)
                        e.wait_ge(emptied_d, d0 + RING * i + j - j % 2 + 2)
                        products(j, j, range(KT), 0, h, 0, w, True, True).then_inc(chunk_done, 1)
                e.wait_ge(act_split, n_act(FT) + 1)
                m0, d0, a0, n = later[f"down{f}"]
                with e.Fori(0, n // RING) as i:
                    for j in range(RING):
                        e.wait_ge(lo_done, RING + m0 + RING * i + j + 1)
                        if j % 2 == 0:
                            e.wait_ge(emptied_d, 4 + d0 + RING * i + j - 2)
                        products(j // 2, j, range(DOWN), DOWN * (j % 2), (ah, al), 0, w, j % 2 == 0, j % 2 == 1)\
                            .then_inc(chunk_done, 1)

            ffn(0, 2)

            norm(2 * T, False)
            e.wait_ge(tables_in, 32)
            e.wait_ge(emptied_d, 4 + later["four"][1])
            e.wait_ge(normed, KT * (LAYERS + 3))
            for n in range(16):
                b, r = divmod(n, 8)
                g, tt = divmod(r, 2)
                if n >= 4:
                    e.wait_ge(f1_out, n - 3)
                for kk in range(2):
                    tok = T * b + P * tt
                    end = e.matmul(ps[:, n % 4, :], hf[:, 2 * g + kk, tok:tok + P], dft[:, kk, :], start=(kk == 0),
                                   stop=(kk == 1))
                end.then_inc(f1_done, 1)
            for n in range(16):
                b, f = divmod(n, 8)
                e.wait_ge(f1_out, 8 * b + 8)
                if n >= 4:
                    e.wait_ge(f2_hi, n - 3)
                for q, (tt, part) in enumerate((tt, part) for tt in range(TT) for part in range(2)):
                    lo = T * part + P * (f % 2)
                    end = e.matmul(ps[:, 4 + n % 4, 0:T], pq[:, b, tt, f // 2, lo:lo + P], dftn[:, tt, part, :],
                                   start=(q == 0), stop=(q == 3))
                end.then_inc(f2_done, 1)
            e.wait_ge(f2_hi, 16)
            plain(later["four"], 2 * T, emptied_d)
            ffn(1, 2)
            ffn(2, 2)

            norm(2 * T, True)
            plain(later["rq"], T, emptied_d)
            plain(later["rk"], 2 * T, emptied_d)
            m0, d0, a0, _ = later["rv"]
            for g in range(RH):
                for c in range(4):
                    e.wait_ge(lo_done, RING + m0 + 4 * g + c + 1)
                    if c == 0:
                        e.wait_ge(emptied_d, 4 + d0 + max(0, 4 * g - 4))
                    natural(c, c, RDV, 4 * (g % 2), 2 * TT, c == 0, c == 3).then_inc(chunk_done, 1)
            e.wait_ge(emptied_d, 4 + d0 + 12)
            plain(later["rg"], T, emptied_a)
            e.wait_ge(emptied_d, 4 + later["ro"][1])
            e.wait_ge(emptied_a, 4 + later["ro"][2])
            for h_ in range(RH):
                for jt in range(4):
                    n = 4 * h_ + jt
                    if n >= 2:
                        e.wait_ge(rs_out, n - 1)
                    for dd in range(2):
                        end = e.matmul(ps[:, jt % 2, 0:T], kT[:, 2 * h_ + dd, P * jt:P * jt + P], qT[:, 2 * h_ + dd, :],
                                       start=(dd == 0), stop=(dd == 1))
                    end.then_inc(rs_done, 1)
                for dv in range(4):
                    n = 4 * h_ + dv
                    e.wait_ge(rs_out, 4 * h_ + 4)
                    if n >= 2:
                        e.wait_ge(ry_out, n - 1)
                    for jt in range(4):
                        lo = RDV * h_ + P * dv
                        end = e.matmul(ps[:, 2 + dv % 2, 0:T], vr[:, jt, lo:lo + P], sT[:, jt, :], start=(jt == 0),
                                       stop=(jt == 3))
                    end.then_inc(ry_done, 1)
                e.wait_ge(ry_out, 4 * h_ + 4)
                for dv in range(4):
                    end = e.matmul(ps[:, 6, 0:T], ones[:, :], yr[:, dv, :], start=(dv == 0), stop=(dv == 3))
                end.then_inc(rmean, 1)
                for dv in range(4):
                    e.wait_ge(rcent, 4 * h_ + dv + 1)
                    end = e.matmul(ps[:, 7, 0:T], ones[:, :], sq[:, dv % 2, 0:T], start=(dv == 0), stop=(dv == 3))
                    end.then_inc(rc_done, 1)
            e.wait_ge(rgn, 4 * RH)
            m0, d0, a0, n = later["ro"]
            with e.Fori(0, n // RING) as i:
                for j in range(RING):
                    e.wait_ge(lo_done, RING + m0 + RING * i + j + 1)
                    if j % 2 == 0:
                        e.wait_ge(emptied_d, 4 + d0 + RING * i + j - 2)
                    for t in range(KT):
                        f = KT * (j % 2) + t
                        w = slice(t * P, t * P + P)
                        mh, ml = (b[:, f // 2, T * (f % 2):T * (f % 2) + T] for b in h)
                        out = ps[:, j // 2, 0:T]
                        e.matmul(out, wh[:, j % 2, w], mh, start=(f == 0), stop=False)
                        e.matmul(out, wh[:, j % 2, w], ml, start=False, stop=False)
                        end = e.matmul(out, wl[:, j % 2, w], mh, start=False, stop=(f == 2 * KT - 1))
                    end.then_inc(chunk_done, 1)
            ffn(3, 1)
            norm(T, False)


IN_SIZES = (384, 384, 384, 384, 384, 64, 64, 384, 256, 64, 4, 768, 768, 768, 256, 3072)
IN_AT = dict(zip(("a_q", "a_k", "a_v", "a_g", "b_q", "b_k", "b_v", "b_g", "i_q", "i_k", "i_w", "c_q", "c_k", "c_v",
                  "c_g", "m_g"), zip(np.cumsum((0,) + IN_SIZES[:-1]).tolist(), IN_SIZES)))


def tiles(w):
    k, n = w.shape
    return w.reshape(k // P, P, n // P, P).transpose(2, 1, 0, 3).reshape(n // P, P, k)


def natural_chunks(w, width):
    g = w.shape[1] // width
    return w.reshape(4, 2, P, g, width).transpose(3, 0, 2, 1, 4).reshape(4 * g, P, 2 * width)


def rows(v):
    return v.reshape(-1, P).transpose(1, 0)


def tables():
    f32 = np.float32
    inv = (1.0 / (f32(10000.0) ** (np.arange(0, HD, 2, dtype=f32) / f32(HD)))).astype(f32)
    ang = np.arange(T, dtype=f32)[:, None] * inv[None, :]
    cos, sin = np.cos(ang).T, np.sin(ang).T
    rope = np.concatenate([np.tile(cos, (4, 1)), np.tile(sin, (4, 1))], 1).astype(f32)

    i = np.arange(T)
    diff = i[:, None] - i[None, :]
    ok = {"tri": diff >= 0, "w128": (diff >= 0) & (diff <= 128), "d4": (diff >= 0) & (diff % 4 == 0),
          "d16": (diff >= 0) & (diff % 16 == 0)}
    mask = np.zeros((P, MASKW), f32)
    for (name, qt), (at, n) in MASK.items():
        mask[:, at:at + n] = np.where(ok[name][P * qt:P * qt + P, 0:n], 0.0, NEG)

    n = np.arange(T)
    ph = 2 * np.pi * ((n[:, None] * n[None, :]) % T) / T
    c, s = np.cos(ph), np.sin(ph)
    by_feature = np.concatenate([c, s], 1).reshape(2, P, 2 * T).transpose(1, 0, 2).reshape(P, -1)
    by_token = (np.stack([c, -s], 1) / T).reshape(TT, P, 2, T).transpose(1, 0, 2, 3).reshape(P, -1)
    dft = np.concatenate([by_feature, by_token], 1).astype(f32)

    rws = T // 64
    row = np.repeat(np.arange(rws, dtype=f32), 64)
    col = np.tile(np.arange(64, dtype=f32), rws)
    inv2 = f32(10000.0) ** (-np.arange(64, dtype=f32) / f32(64))
    ang2 = np.concatenate([row[:, None] * inv2, col[:, None] * inv2], 1).astype(f32)
    rope2 = np.concatenate([np.cos(ang2).T, np.sin(ang2).T], 1).astype(f32)

    j, q = np.arange(T)[:, None], np.arange(T)[None, :]
    fwd = np.concatenate([np.maximum(q - j, 0), q - j + T], 0)
    bwd = np.concatenate([np.maximum(j - q, 0), T - q + j], 0)
    dist = np.stack([fwd, bwd]).reshape(2, 4, P, T).transpose(2, 0, 1, 3).reshape(P, -1).astype(np.float16)
    dmask = np.stack([q >= j, j >= q]).reshape(2, 2, P, T).transpose(2, 0, 1, 3).reshape(P, -1).astype(np.float16)
    return rope, mask, dft, rope2, dist, dmask


def kernel(x, norm_g, w_in, w_br_a, w_br_b, w_br_c, w_out, final_norm_g, c_2, ctx_2, c_ctx_2, ada_w_2, ada_b_2,
           norm_g_2, final_g_2, ffn_w_gate_2, ffn_w_up_2, ffn_w_down_2, four_w_2, four_b_2, ret_w_in_2,
           ret_w_out_2, ret_decay_2):
    import ml_dtypes
    import concourse.bacc as _bacc
    from concourse import mybir as _mybir
    from concourse.bass_utils import run_bass_kernel_spmd as _run

    xT = np.concatenate([x[0].transpose(1, 0), ctx_2[0].transpose(1, 0)], 1)
    decay = np.broadcast_to(ret_decay_2.reshape(1, 8), (P, 8))
    cc = np.stack([rows(c_2), rows(c_ctx_2)], 2).reshape(P, 16)
    cols = np.concatenate([rows(norm_g), rows(final_norm_g), rows(norm_g_2), rows(final_g_2), rows(four_b_2),
                           rows(ada_b_2), cc, decay], 1)
    ada = np.concatenate([tiles(w) for w in ada_w_2], 0)

    heads = ([("a_q", h) for h in range(6)] + [("a_k", h) for h in range(6)] + [("c_q", h) for h in range(12)]
             + [("c_k", h) for h in range(12)] + [("b_q", h) for h in range(6)] + [("i_q", h) for h in range(4)]
             + [("b_k", 0), ("i_k", 0)])
    qk_cols = []
    for g in range(NPOS // 4):
        for half in range(2):
            for name, h in heads[4 * g:4 * g + 4]:
                at = IN_AT[name][0] + HD * h + 32 * half
                qk_cols += list(range(at, at + 32))

    def span(*names):
        return [i for name in names for i in range(IN_AT[name][0], IN_AT[name][0] + IN_AT[name][1])]

    v_cols = span("a_v", "b_v", "c_v", "i_w")
    g_cols = span("a_g", "b_g", "c_g", "m_g")
    w1, wv = [], []
    for l in range(LAYERS):
        branch = np.concatenate([w_br_a[l], w_br_b[l], w_br_c[l]], 0)
        w1 += [tiles(w_in[l][:, qk_cols]), tiles(w_in[l][:, g_cols]), tiles(branch), tiles(w_out[l])]
        padded = np.concatenate([w_in[l][:, v_cols], np.zeros((D, VG * VW - len(v_cols)), np.float32)], 1)
        wv.append(natural_chunks(padded, VW))
    w1, wv = np.concatenate(w1, 0), np.concatenate(wv, 0)

    wu, wd = [], []
    for l in range(LAYERS):
        for f in range(2):
            both = np.stack([tiles(ffn_w_gate_2[l, f]), tiles(ffn_w_up_2[l, f])], 1)
            wu.append(both.reshape(2 * FT, P, W8))
            wd.append(tiles(ffn_w_down_2[l, f]).reshape(KT, P, 2, WD).transpose(0, 2, 1, 3).reshape(2 * KT, P, WD))
    wu, wd = np.concatenate(wu, 0), np.concatenate(wd, 0)
    ret = ret_w_in_2[0]
    ro = tiles(ret_w_out_2[0]).reshape(KT, P, 2, W8).transpose(0, 2, 1, 3).reshape(2 * KT, P, W8)
    w2 = np.concatenate([tiles(four_w_2[0]), tiles(ret[:, 0:D]), tiles(ret[:, D:2 * D]),
                         natural_chunks(ret[:, 2 * D:4 * D], RDV), tiles(ret[:, 4 * D:6 * D]), ro], 0)
    rope, mask, dft, rope2, dist, dmask = tables()

    given = [("xT", xT), ("cols", cols), ("ada", ada), ("w1", w1), ("wv", wv), ("wu", wu), ("wd", wd), ("w2", w2),
             ("rope", rope), ("mask", mask.astype(ml_dtypes.bfloat16)), ("ident", np.eye(P, dtype=np.float32)),
             ("identb", np.eye(P, dtype=ml_dtypes.bfloat16)), ("dft", dft), ("rope2", rope2), ("dist", dist),
             ("dmask", dmask)]
    nc = _bacc.Bacc("TRN2", target_bir_lowering=False, num_devices=1)
    arrays, args = {}, []
    for name, a in given:
        a = np.ascontiguousarray(a)
        arrays[f"in_{name}_dram"] = a
        args.append(nc.dram_tensor(f"in_{name}_dram", a.shape, _mybir.dt.from_np(a.dtype), kind="ExternalInput").ap())
    args.append(nc.dram_tensor("out_0_dram", (D, T), F32, kind="ExternalOutput").ap())
    program(nc, *args)
    r = _run(nc, [arrays], core_ids=[0])
    return r.results[0]["out_0_dram"].transpose(1, 0).reshape(1, T, D)
```

```python
from contextlib import ExitStack, contextmanager

import numpy as np

import concourse.bass as bass
from concourse import mybir

F32 = mybir.dt.float32
F32R = mybir.dt.float32r
F16 = mybir.dt.float16
BF16 = mybir.dt.bfloat16
ACT = mybir.ActivationFunctionType
ALU = mybir.AluOpType
AX_X = mybir.AxisListType.X

P = 128
D = 1024
KT = D // P
T = 256
TT = T // P
HD = 64
LAYERS = 2
EPS = 1e-6
NEG = -1e30
TAKEN = -3e38
TOPK = 64
FFN = 2816
FT = FFN // P
RING = 4
AHEAD = 3
VG, VW = 3, 408
DOWN = (6, 5, 6, 5)
W8 = (KT * P,) * RING
WV = (2 * VW,) * RING
WD = tuple(k * P for k in DOWN)
CW = KT * P
RH = 4
RDV = 512
ADA = 9 * KT

QK, VN, GATE, MIXG, BR, OUT = 24, 12, 8, 24, 8, 8
PER_LAYER = QK + VN + GATE + MIXG + BR + OUT
PER_D = QK + VN + BR + OUT
PER_A = GATE + MIXG

AQ, AK, CQ, CK, BQ, IQ, BK, IK = 0, 6, 12, 24, 36, 42, 46, 47
NPOS = 48

MASK = {("tri", 0): (0, 128), ("d4", 0): (128, 128), ("d16", 0): (256, 128),
        ("w128", 1): (384, 256), ("d4", 1): (640, 256), ("d16", 1): (896, 256)}
MASKW = 1152


def softmax_units():
    units = []

    def place(pos):
        return pos // 2, pos % 2

    for h in range(6):
        for qt in range(TT):
            units.append((qt, [(place(AQ + h), place(AK + h), "tri")], [64 * h], 64 * h))
    for s in range(4):
        for qt in (1, 0):
            first = "tri" if qt == 0 else "w128"
            segs = [(place(CQ + 4 * g + s), place(CK + 4 * g + s), m)
                    for g, m in enumerate((first, "d4", "d16"))]
            units.append((qt, segs, [448 + 64 * (4 * g + s) for g in range(3)], 768 + 64 * s))
    for h in range(6):
        for qt in range(TT):
            units.append((qt, [(place(BQ + h), (23, 0) if h % 2 == 0 else (24, 1), "picked")],
                          [384], 384 + 64 * h))
    return units


UNITS = softmax_units()
NU = len(UNITS)

COLS = {}
_at = 0
for _name, _n in (("norm_g", 16), ("final_norm_g", 8), ("norm_g_2", 48), ("final_g_2", 8),
                  ("four_b", 8), ("ada_b", 144), ("c", 16), ("decay", 8)):
    COLS[_name] = (_at, _n)
    _at += _n
NCOLS = _at


class Tally:

    def __init__(self, start=0):
        self.base, self.n = 0, start

    def __call__(self, k=1):
        self.n += k
        return self.base + self.n

    @property
    def now(self):
        return self.base + self.n


@contextmanager
def turns(eng, count, *tallies):
    kept = [(t, t.base, t.n) for t, _ in tallies]
    with eng.Fori(0, count) as i:
        for t, k in tallies:
            t.base = t.base + i * k
        yield i
    for (t, base, n), (_, k) in zip(kept, tallies):
        assert t.n - n == k, (t.n - n, k)
        t.base, t.n = base, n + k * count


def program(nc, xT_d, cols_d, ada_d, w1_d, wv_d, wu_d, wd_d, w2_d, rope_d, mask_d, ident_d, identb_d,
            dft_d, rope2_d, dist_d, dmask_d, out_d):
    with ExitStack() as ctx:
        top = [-(-nc.sbuf_base // 64) * 64]

        def at(name, shape, dt, offset):
            return nc.alloc_sbuf_tensor_at(name, shape, dt, offset=offset)

        def size(shape, dt):
            n = 2 if dt in (F16, BF16) else 4
            for s in shape[1:]:
                n *= s
            return -(-n // 64) * 64

        def keep(name, shape, dt=F32):
            t = at(name, shape, dt, top[0])
            top[0] += size(shape, dt)
            return t

        x_at = top[0]
        x = keep("x", [P, 2, KT, T])
        hh = keep("h_high", [P, KT, 2 * T], F32R)
        sg = at("sg", [P, KT, 2 * T], F32, top[0])
        hl = keep("h_low", [P, KT, 2 * T], F32R)
        raw = keep("raw", [P, RING, CW])
        wh = keep("w_high", [P, RING, CW], F32R)
        wl = keep("w_low", [P, RING, CW], F32R)
        cols = keep("cols", [P, NCOLS])
        ident = keep("ident", [P, P])
        ones = keep("ones", [P, P])
        identb = keep("identb", [P, P], BF16)
        mask = keep("mask", [P, MASKW], BF16)
        rope = keep("rope", [P, 2, T])
        mod = keep("mod", [P, LAYERS * ADA, 2])
        gain = keep("gain", [P, LAYERS * 3, KT, 2])
        gate = keep("gate", [P, LAYERS * 3, KT, 2])
        sc = keep("silu_c", [P, KT, 2])
        eps = keep("eps", [P, 1])
        sq = keep("sq", [P, 2, 2 * T])
        rs = keep("rs", [P, 2 * T])
        sT = at("sT", [P, 4, T], F32, top[0])
        tn = keep("tn", [P, 2, 2 * T])
        yr = at("yr", [P, 4, T], F32, top[0])
        hn = keep("hn", [P, 2, 2 * T])
        rsum = keep("rsum", [P, NU])
        nmax = keep("nmax", [P, NU])
        rmax = keep("rmax", [P, NU])
        rrec = keep("rrec", [P, NU])
        iw = keep("iw", [P, TT, 4])
        top8 = keep("top8", [P, 8])
        lg = keep("lg", [P, 8])
        spare = keep("spare", [P, 8])
        arena = top[0]

        class Area:
            def __init__(self, base):
                self.at = base

            def __call__(self, name, shape, dt=F32):
                t = at(name, shape, dt, self.at)
                self.at += size(shape, dt)
                return t

        a1 = Area(arena)
        rot = a1("rot", [P, QK, T])
        mg = at("mg", [P, 3 * KT, T], F32, arena)
        heads = a1("heads", [P, NPOS // 2 + 1, T])
        vn = a1("vn", [P, TT, VG * VW])
        relu = at("relu", [P, 2, 2 * T], F32, a1.at)
        prob = [a1("prob0", [P, 768]), a1("prob1", [P, 384])]
        idx = at("idx", [P, TT, T], F32, a1.at)
        probT = [a1("probT0", [P, 768]), a1("probT1", [P, 384])]
        y = a1("y", [P, TT, D])
        picked = a1("picked", [P, 3 * P], BF16)
        ada_x = at("ada_x", [P, 2, CW], F32, x_at + 4 * KT * T)
        ada_a = a1("ada_a", [P, 2, CW])
        ada = [ada_x[:, 0, :], ada_x[:, 1, :], ada_a[:, 0, :], ada_a[:, 1, :]]

        a2 = Area(arena)
        ah = a2("act_high", [P, FT, 2 * T], F32R)
        al = a2("act_low", [P, FT, 2 * T], F32R)

        a3 = Area(arena)
        hf = a3("hf", [P, KT, 2 * T])
        pq = a3("pq", [P, 2, TT, 4, 2 * T])
        dft = a3("dft", [P, 2, 2 * T])
        dftn = a3("dftn", [P, TT, 2, T])

        a4 = Area(arena)
        qT = a4("qT", [P, KT, T])
        kT = a4("kT", [P, KT, 2 * T])
        vr = a4("vr", [P, 2 * TT, RH * RDV])
        sgr = a4("sgr", [P, 2 * KT, T])
        dist = a4("dist", [P, 2, 4, T], F16)
        dmask = a4("dmask", [P, 2, 2, T], F16)
        rope2 = a4("rope2", [P, 2, T])
        dec = a4("dec", [P, 2, 4, T])
        for a in (a1, a2, a3, a4):
            assert a.at <= nc.sbuf_top, (a.at, nc.sbuf_top)

        ps = ctx.enter_context(nc.psum_tensor("ps", [P, 8, 512], F32))

        def sem(name):
            return ctx.enter_context(nc.semaphore(name))

        landed = [sem(f"landed{j}") for j in range(RING)]
        ada_landed = [sem(f"ada_landed{j}") for j in range(RING)]
        consts_in = sem("consts_in")
        context_in = sem("context_in")
        tables_in = sem("tables_in")
        ret_tables_in = sem("ret_tables_in")
        heads_in = sem("heads_in")
        ones_set = sem("ones_set")
        eps_set = sem("eps_set")
        c_silu = sem("c_silu")
        ada_done = sem("ada_done")
        mod_ready = sem("mod_ready")
        hi_done = sem("hi_done")
        lo_done = sem("lo_done")
        chunk_done = sem("chunk_done")
        emptied_d = sem("emptied_d")
        emptied_a = sem("emptied_a")
        sq_done = sem("sq_done")
        sq_summed = sem("sq_summed")
        std_done = sem("std_done")
        scaled = sem("scaled")
        normed = sem("normed")
        norm_hi = sem("norm_hi")
        norm_split = sem("norm_split")
        act_hi = sem("act_hi")
        act_split = sem("act_split")
        logits = sem("logits")
        relu_done = sem("relu_done")
        idx_summed = sem("idx_summed")
        scored = sem("scored")
        maxed = sem("maxed")
        exped = sem("exped")
        turned = sem("turned")
        copied = sem("copied")
        weighed = sem("weighed")
        y_done = sem("y_done")
        yT_done = sem("yT_done")
        yT_out = sem("yT_out")
        f1_done = sem("f1_done")
        f1_out = sem("f1_out")
        f2_done = sem("f2_done")
        f2_hi = sem("f2_hi")
        decayed = sem("decayed")
        d_ready = sem("d_ready")
        rs_done = sem("rs_done")
        rs_out = sem("rs_out")
        ry_done = sem("ry_done")
        ry_out = sem("ry_out")
        rc_done = sem("rc_done")
        rmean = sem("rmean")
        rcent = sem("rcent")
        rstd = sem("rstd")
        rgn = sem("rgn")
        dve_step = sem("dve_step")
        act_step = sem("act_step")
        pool_step = sem("pool_step")
        stored = sem("stored")
        passed = sem("passed")

        def flat(t, k, lo=None, n=None):
            v = t[:, bass.ds(k, 1), :] if lo is None else t[:, bass.ds(k, 1), lo:lo + n]
            return v.rearrange("p a t -> p (a t)")

        MIX_CHUNK = [3 * (u // 4) + u % 4 if u % 4 < 3 else None for u in range(NU)]
        assert max(c for c in MIX_CHUNK if c is not None) == MIXG - 1

        def score_slot(u):
            return ps[:, 2, :] if u % 2 else ps[:, 0:2, :].rearrange("p a t -> p (a t)")

        def unit_width(u):
            qt, segs, _, _ = UNITS[u]
            return len(segs) * P * (qt + 1)

        hybrid = {}
        m = d = a = 0
        for name, n, kind in (("qk", QK, "d"), ("vn", VN, "d"), ("gate", GATE, "a"), ("mixg", MIXG, "a"),
                              ("br", BR, "d"), ("out", OUT, "d")):
            hybrid[name] = (m, d, a, n)
            m, d, a = m + n, d + (n if kind == "d" else 0), a + (n if kind == "a" else 0)
        later = {}
        m, d, a = LAYERS * m, LAYERS * d, LAYERS * a
        for name, n, kind in (("up0", 44, "d"), ("down0", 32, "d"), ("four", 8, "d"), ("up1", 44, "d"),
                              ("down1", 32, "d"), ("up2", 44, "d"), ("down2", 32, "d"), ("rq", 8, "d"),
                              ("rk", 8, "d"), ("rv", 16, "d"), ("rg", 16, "a"), ("ro", 16, "d"),
                              ("up3", 44, "d"), ("down3", 32, "d")):
            later[name] = (m, d, a, n)
            m, d, a = m + n, d + (n if kind == "d" else 0), a + (n if kind == "a" else 0)

        def xk(k, halves):
            return x[:, 0:halves, bass.ds(k, 1), :].rearrange("p a k t -> p a (k t)")

        def both(ap, halves):
            return ap.rearrange("p (a t) -> p a t", a=halves)

        ADA_AT = {"qk": 0, "gate": QK, "mixg": QK + GATE, "br": QK + PER_A, "out": QK + PER_A + BR}

        def of_layer(name, L):
            m, d, a, n = hybrid[name]
            return m + L * PER_LAYER, d + L * PER_D, a + L * PER_A, n

        block = ctx.enter_context(nc.Block())

        @block.sync
        def _(e):
            xT = xT_d.rearrange("(k p) t -> p k t", p=P)
            for dst, src in ((cols[:, :], cols_d), (x[:, 0, :, :], xT[:, :, 0:T]),
                             (ident[:, :], ident_d), (identb[:, :], identb_d), (mask[:, :], mask_d),
                             (rope[:, :, :], rope_d.rearrange("p (a t) -> p a t", a=2))):
                e.dma_start(dst, src).then_inc(consts_in, 16)

            def load(m0, n, widths, src, first, ada0=None):
                with e.Fori(0, n // RING) as i:
                    for j in range(RING):
                        e.wait_ge(lo_done, m0 + RING * i + j + 1)
                        at_ = sum(widths[0:j]) if widths is WD else 0
                        row = i if widths is WD else RING * i + j
                        e.dma_start(raw[:, j, 0:widths[j]],
                                    src[bass.ds(first + row, 1), :, at_:at_ + widths[j]].rearrange("a p n -> p (a n)"))\
                            .then_inc(landed[j], 16)
                        if ada0 is not None:
                            e.wait_ge(ada_done, ada0 + RING * i + j + 1)
                            e.dma_start(ada[j], ada_d[bass.ds(ada0 + RING * i + j, 1)].rearrange("a p n -> p (a n)"))\
                                .then_inc(ada_landed[j], 16)

            with e.Fori(0, LAYERS) as L:
                per = PER_LAYER - VN
                load(of_layer("qk", L)[0], QK, W8, w1_d, per * L, ADA * L)
                load(of_layer("vn", L)[0], VN, WV, wv_d, VN * L)
                load(of_layer("gate", L)[0], per - QK, W8, w1_d, per * L + QK, ADA * L + QK)
            e.wait_ge(ada_done, RING + LAYERS * ADA)
            e.dma_start(x[:, 1, :, :], xT[:, :, T:2 * T]).then_inc(context_in, 16)

            def ffn(f):
                load(later[f"up{f}"][0], 2 * FT, W8, wu_d, 2 * FT * f)
                load(later[f"down{f}"][0], RING * KT, WD, wd_d, KT * f)

            ffn(0)
            e.wait_ge(chunk_done, later["down0"][0] + RING * KT)
            e.dma_start(dft[:, :, :], dft_d[:, 0:4 * T].rearrange("p (a t) -> p a t", a=2)).then_inc(tables_in, 16)
            e.dma_start(dftn[:, :, :, :], dft_d[:, 4 * T:8 * T].rearrange("p (a b t) -> p a b t", a=TT, b=2))\
                .then_inc(tables_in, 16)
            load(later["four"][0], KT, W8, w2_d, 0)
            ffn(1)
            ffn(2)
            e.wait_ge(chunk_done, later["down2"][0] + RING * KT)
            e.dma_start(dist[:, :, :, :], dist_d.rearrange("p (a b t) -> p a b t", a=2, b=4)).then_inc(ret_tables_in, 16)
            e.dma_start(dmask[:, :, :, :], dmask_d.rearrange("p (a b t) -> p a b t", a=2, b=2)).then_inc(ret_tables_in, 16)
            e.dma_start(rope2[:, :, :], rope2_d.rearrange("p (a t) -> p a t", a=2)).then_inc(ret_tables_in, 16)
            load(later["rq"][0], 64, W8, w2_d, KT)
            ffn(3)
            e.wait_ge(normed, 8 * (LAYERS + 1 + 2 * 3 + 1))
            e.dma_start(out_d.rearrange("(k p) t -> p k t", p=P), hf[:, :, 0:T]).then_inc(stored, 16)
            e.wait_ge(stored, 16)

        @block.scalar
        def _(e):
            n_sq, n_scaled, n_normed, n_split = Tally(), Tally(), Tally(), Tally()

            def split(lap, mm, c, width):
                e.wait_ge(landed[c % RING], 16 * lap + 16)
                if not (isinstance(mm, int) and mm < RING):
                    e.wait_ge(chunk_done, mm - RING + 1)
                e.activation(wh[:, c % RING, 0:width], raw[:, c % RING, 0:width], ACT.Copy).then_inc(hi_done, 1)

            def phase(base, widths, after, empty=None, n_own=()):
                m0, _, _, n = base
                lap0 = hybrid_lap(m0)

                def turn(i, nxt):
                    for j in range(RING):
                        c = j + AHEAD
                        w = widths[c] if c < RING else nxt and nxt[c % RING]
                        if w:
                            split(lap0 + i + c // RING, m0 + RING * i + c, c, w)
                        if empty:
                            empty(i, j)

                whole = n // RING - (after != widths)
                if whole:
                    with turns(e, whole, *n_own) as i:
                        turn(i, widths)
                if after != widths:
                    turn(whole, after)

            def hybrid_lap(m0):
                return m0 // RING if isinstance(m0, int) else lap_of[0]

            lap_of = [None]

            def norm(cols_n, gains, dest, has_split, made):
                for k in range(KT):
                    e.wait_ge(*made(k))
                    if k >= 2 or n_sq.n >= 2:
                        e.wait_ge(sq_summed, n_sq.now - 1)
                    halves = cols_n // T
                    e.activation(both(sq[:, k % 2, 0:cols_n], halves), xk(k, halves), ACT.Square).then_inc(sq_done, 1)
                    n_sq()
                e.wait_ge(sq_summed, n_sq.now)
                e.activation(rs[:, 0:cols_n], ps[:, 7, 0:cols_n], ACT.Sqrt, bias=eps[:, :], scale=1.0 / D)\
                    .then_inc(std_done, 1)
                per = (n_scaled, 2), (n_normed, 2), (n_split, 2 if has_split else 0)
                with turns(e, KT // 2, *per) as i:
                    for j in range(2):
                        e.wait_ge(scaled, n_scaled())
                        if has_split:
                            e.wait_ge(norm_split, n_split())
                        parts = gains(2 * i + j)
                        for q, (g, b) in enumerate(parts):
                            src = tn[:, j, T * q:T * q + T]
                            out = dest(2 * i + j, j, q)
                            if b is None:
                                last = e.activation(out, src, ACT.Copy, scale=g)
                            else:
                                last = e.activation(out, src, ACT.Identity, bias=b, scale=g)
                        last.then_inc(normed, 1)
                        n_normed()

            def after(base, tile, end):
                return lambda k: (emptied_d, 4 + base[1] + end - tile * (KT - 1 - k))

            def col(name, k):
                return cols[:, bass.ds(COLS[name][0] + k, 1)]

            def mod_gains(lj, l, mrow, halves):
                def get(k):
                    return [(gain[:, lj, bass.ds(k, 1), q], mod[:, bass.ds(l * ADA + mrow * KT + k, 1), q])
                            for q in range(halves)]
                return get

            def to_hn(k, j, q):
                return hn[:, j, T * q:T * q + T]

            e.wait_ge(eps_set, 2)
            e.wait_ge(consts_in, 96)
            e.activation(sc[:, :, :].rearrange("p k c -> p (k c)"), cols[:, COLS["c"][0]:COLS["c"][0] + 16],
                         ACT.Silu).then_inc(c_silu, 1)
            e.activation(spare[:, 5:6], eps[:, :], ACT.Copy).then_inc(emptied_a, 4)
            for c in range(AHEAD):
                split(0, c, c, CW)

            n_relu, n_exp, n_copy = Tally(), Tally(), Tally()
            per = ((n_sq, KT), (n_scaled, KT), (n_normed, KT), (n_split, 2 * KT + KT),
                   (n_relu, TT), (n_exp, NU), (n_copy, NU))
            with turns(e, LAYERS, *per) as L:
                def laps(name):
                    lap_of[0] = hybrid[name][0] // RING + L * (PER_LAYER // RING)
                    return of_layer(name, L)

                norm(T, lambda k: [(col("norm_g", L * KT + k), None)], to_hn, True,
                     lambda k: (emptied_d, 4 + of_layer("qk", L)[1]))
                phase(laps("qk"), W8, WV)

                m0 = laps("vn")[0]
                for c in range(AHEAD, VN + AHEAD):
                    split(lap_of[0] + c // RING, m0 + c, c, WV[0] if c < VN else CW)
                    if c == 2 * AHEAD:
                        e.wait_ge(emptied_d, 4 + of_layer("qk", L)[1] + QK)
                        for jq in range(4):
                            for r in range(2):
                                dst = 64 * (jq % 2) + 32 * r
                                e.dma_start(heads[dst:dst + 32, jq // 2:NPOS // 2:2, :],
                                            rot[32 * jq:32 * jq + 32, r::2, :]).then_inc(heads_in, 16)
                        for jq, half in ((2, 1), (3, 0)):
                            for r in range(2):
                                dst = 64 * half + 32 * r
                                e.dma_start(heads[dst:dst + 32, NPOS // 2, :],
                                            rot[32 * jq:32 * jq + 32, QK - 2 + r, :]).then_inc(heads_in, 16)

                for qt in range(TT):
                    w = P * (qt + 1)
                    e.wait_ge(logits, n_relu())
                    if qt:
                        e.wait_ge(idx_summed, n_relu.now - 1)
                    bank = 6 - 2 * qt
                    e.activation(relu[:, :, 0:2 * w], ps[:, bank:bank + 2, 0:2 * w], ACT.Relu)\
                        .then_inc(relu_done, 1)

                def mod_column(r, bank):
                    e.activation(mod[:, bass.ds(r, 1), :].rearrange("p a c -> p (a c)"), ps[:, bank, T:T + 2],
                                 ACT.Identity, bias=col("ada_b", r), scale=1.0).then_inc(emptied_a, 1)

                def silu_gate(i, j):
                    e.wait_ge(chunk_done, of_layer("gate", L)[0] + RING * i + j + 1)
                    e.activation(flat(sg, RING * i + j, T, T), ps[:, j, 0:T], ACT.Silu)
                    mod_column(ADA * L + ADA_AT["gate"] + RING * i + j, j)

                phase(laps("gate"), W8, W8, silu_gate)

                def exp(u):
                    w = unit_width(u)
                    e.wait_ge(maxed, n_exp())
                    if u >= 2:
                        e.wait_ge(turned, n_exp.now - 2)
                    e.activation(prob[u % 2][:, 0:w], score_slot(u)[:, 0:w], ACT.Exp, bias=nmax[:, u:u + 1],
                                 scale=HD ** -0.5, accum_out=rsum[:, u:u + 1]).then_inc(exped, 1)

                m0 = laps("mixg")[0]
                exp(0)
                for u in range(NU):
                    c = MIX_CHUNK[u]
                    if c is not None:
                        split(lap_of[0] + (c + AHEAD) // RING, m0 + c + AHEAD, c + AHEAD, CW)
                    if u + 1 < NU:
                        exp(u + 1)
                    if c is not None:
                        e.wait_ge(chunk_done, m0 + c + 1)
                        e.activation(mg[:, c, :], ps[:, 6 + c % 2, 0:T], ACT.Exp, scale=-1.0)
                        mod_column(ADA * L + ADA_AT["mixg"] + c, 6 + c % 2)
                    w = unit_width(u)
                    e.wait_ge(turned, n_copy())
                    if u >= 2:
                        e.wait_ge(weighed, n_copy.now - 2)
                    e.activation(probT[u % 2][:, 0:w], ps[:, 3:5, :].rearrange("p a t -> p (a t)")[:, 0:w],
                                 ACT.Copy).then_inc(copied, 1)

                phase(laps("br"), W8, W8)
                phase(laps("out"), W8, W8)
                n_split(2 * KT)

            norm(T, lambda k: [(col("final_norm_g", k), None)], lambda k, j, q: xk(k, 1)[:, 0, :], False,
                 after(later["up0"], 1, 0))

            def ffn(f, l, jn, halves, made, width_after):
                norm(halves * T, mod_gains(3 * l + jn, l, 3 * jn, halves), to_hn, True, made)
                base = later[f"up{f}"]

                def silu(i, j):
                    if j % 2 == 0:
                        return
                    e.wait_ge(chunk_done, base[0] + RING * i + j)
                    e.wait_ge(emptied_d, 4 + base[1] + RING * i + j - 1 - 2)
                    e.activation(tn[:, j // 2, 0:halves * T], ps[:, j - 1, 0:halves * T], ACT.Silu)\
                        .then_inc(act_step, 1)

                phase(base, W8, WD, silu)
                phase(later[f"down{f}"], WD, width_after)

            e.wait_ge(context_in, 16)
            e.wait_ge(mod_ready, 2)
            ffn(0, 0, 0, 2, lambda k: (normed, n_normed.now), W8)
            norm(2 * T, mod_gains(1, 0, 3, 2), lambda k, j, q: flat(hf, k, T * q, T), False,
                 after(later["down0"], RING, RING * KT))
            phase(later["four"], W8, W8)
            ffn(1, 0, 2, 2, after(later["four"], 1, 8), W8)
            ffn(2, 1, 0, 2, after(later["down1"], RING, RING * KT), W8)

            norm(2 * T, mod_gains(4, 1, 3, 2), to_hn, True, after(later["down2"], RING, RING * KT))
            phase(later["rq"], W8, W8)
            phase(later["rk"], W8, W8)
            phase(later["rv"], W8, W8)

            def silu_ret(i, j):
                e.wait_ge(chunk_done, later["rg"][0] + RING * i + j + 1)
                e.activation(flat(sgr, RING * i + j), ps[:, j, 0:T], ACT.Silu).then_inc(emptied_a, 1)

            phase(later["rg"], W8, W8, silu_ret)
            e.wait_ge(ret_tables_in, 48)
            for h in range(RH):
                if h:
                    e.wait_ge(rs_out, 4 * h)
                for b in range(2):
                    e.activation(dec[:, b, :, :], dist[:, b, :, :], ACT.Exp,
                                 scale=lg[:, RH * b + h:RH * b + h + 1]).then_inc(decayed, 1)
                e.wait_ge(rc_done, 4 * h + 4)
                e.activation(rs[:, 0:T], ps[:, 7, 0:T], ACT.Sqrt, bias=eps[:, :], scale=1.0 / RDV)\
                    .then_inc(rstd, 1)
            phase(later["ro"], W8, W8)
            ffn(3, 1, 2, 1, after(later["ro"], 2, 16), None)
            norm(T, lambda k: [(col("final_g_2", k), None)], lambda k, j, q: flat(hf, k, 0, T), False,
                 after(later["down3"], RING, RING * KT))

        @block.gpsimd
        def _(e):
            n_hi, n_nhi = Tally(), Tally()
            e.memset(eps[:, :], EPS).then_inc(eps_set, 1)
            e.memset(ones[:, :], 1.0).then_inc(eps_set, 1)
            e.memset(spare[:, 0:1], 0.0).then_inc(lo_done, RING)
            e.memset(spare[:, 1:2], 0.0).then_inc(norm_split, 2)
            e.memset(spare[:, 6:7], 0.0).then_inc(ada_done, RING)

            def split(mm, c, width):
                e.wait_ge(hi_done, mm + 1)
                e.tensor_tensor(wl[:, c % RING, 0:width], raw[:, c % RING, 0:width],
                                wh[:, c % RING, 0:width].bitcast(F32), ALU.subtract).then_inc(lo_done, 1)

            def phase(base, widths, after, extra=None, n_own=()):
                m0, n = base[0], base[3]

                def turn(i, nxt):
                    for j in range(RING):
                        c = j + AHEAD
                        w = widths[c] if c < RING else nxt and nxt[c % RING]
                        if w:
                            split(m0 + RING * i + c, c, w)
                        if extra:
                            extra(i, j)

                whole = n // RING - (after != widths)
                if whole:
                    with turns(e, whole, *n_own) as i:
                        turn(i, widths)
                if after != widths:
                    turn(whole, after)

            def norm_low(cols_n, pos=0, src=None):
                with turns(e, KT // 2, (n_nhi, 2)) as i:
                    for j in range(2):
                        e.wait_ge(norm_hi, n_nhi())
                        e.tensor_tensor(flat(hl, 2 * i + j, pos, cols_n), hn[:, j, 0:cols_n],
                                        flat(hh, 2 * i + j, pos, cols_n).bitcast(F32), ALU.subtract)\
                            .then_inc(norm_split, 1)

            for c in range(AHEAD):
                split(c, c, CW)
            with turns(e, LAYERS, (n_nhi, 3 * KT)) as L:
                norm_low(T)
                phase(of_layer("qk", L), W8, WV)
                phase(of_layer("vn", L), WV, W8)
                phase(of_layer("gate", L), W8, W8)
                phase(of_layer("mixg", L), W8, W8)
                norm_low(T, T)

                def merged_low(i, j):
                    e.wait_ge(norm_hi, n_nhi())
                    e.tensor_tensor(flat(hl, RING * i + j, 0, T), hn[:, j % 2, 0:T],
                                    flat(hh, RING * i + j, 0, T).bitcast(F32), ALU.subtract)\
                        .then_inc(norm_split, 1)

                phase(of_layer("br", L), W8, W8, merged_low, ((n_nhi, RING),))
                phase(of_layer("out", L), W8, W8)

            n_act = Tally()

            def ffn(f, halves, after):
                norm_low(halves * T)

                def act_low(i, j):
                    if j % 2 == 0:
                        return
                    e.wait_ge(act_hi, n_act())
                    e.tensor_tensor(flat(al, 2 * i + j // 2, 0, halves * T), hn[:, j // 2, 0:halves * T],
                                    flat(ah, 2 * i + j // 2, 0, halves * T).bitcast(F32), ALU.subtract)\
                        .then_inc(act_split, 1)

                phase(later[f"up{f}"], W8, WD, act_low, ((n_act, 2),))
                phase(later[f"down{f}"], WD, after)

            ffn(0, 2, W8)
            phase(later["four"], W8, W8)
            ffn(1, 2, W8)
            ffn(2, 2, W8)
            norm_low(2 * T)
            for name in ("rq", "rk", "rv", "rg"):
                phase(later[name], W8, W8)
            phase(later["ro"], W8, W8)
            ffn(3, 1, None)

        @block.vector
        def _(e):
            step = Tally()
            n_std, n_scaled, n_normed, n_nhi, n_nsplit = Tally(), Tally(), Tally(), Tally(), Tally()

            def norm(cols_n, split):
                halves = cols_n // T
                e.wait_ge(std_done, n_std())
                e.reciprocal(rs[:, 0:cols_n], rs[:, 0:cols_n]).then_inc(dve_step, 1)
                e.wait_ge(dve_step, step())

                def scale(k, j):
                    e.tensor_tensor(both(tn[:, j, 0:cols_n], halves), xk(k, halves), both(rs[:, 0:cols_n], halves), ALU.mult)\
                        .then_inc(scaled, 1)

                def high(k, j):
                    e.wait_ge(normed, n_normed())
                    if split:
                        e.tensor_copy(flat(hh, k, 0, cols_n), hn[:, j, 0:cols_n]).then_inc(norm_hi, 1)
                        n_nhi()

                scale(0, 0)
                scale(1, 1)
                with turns(e, KT // 2 - 1, (n_normed, 2), (n_nhi, 2 if split else 0)) as i:
                    for j in range(2):
                        high(2 * i + j, j)
                        scale(2 * i + j + 2, j)
                high(KT - 2, 0)
                high(KT - 1, 1)
                n_scaled(KT)
                if split:
                    n_nsplit(KT)

            def own(k):
                e.wait_ge(dve_step, step(k))

            e.memset(spare[:, 2:3], 0.0).then_inc(emptied_d, 4)
            e.memset(spare[:, 3:4], 0.0).then_inc(act_split, 1)
            e.wait_ge(consts_in, 96)

            def rotate(ps1, ps2, cs, sn, out1, out2, ready, count):
                e.tensor_tensor(tn[:, 0, 0:T], ps1, cs, ALU.mult).then_inc(dve_step, 1)
                e.tensor_tensor(tn[:, 0, T:2 * T], ps2, sn, ALU.mult).then_inc(dve_step, 1)
                e.tensor_tensor(tn[:, 1, 0:T], ps1, sn, ALU.mult).then_inc(dve_step, 1)
                e.tensor_tensor(tn[:, 1, T:2 * T], ps2, cs, ALU.mult).then_inc(dve_step, 1)
                own(4)
                e.tensor_tensor(out1, tn[:, 0, 0:T], tn[:, 0, T:2 * T], ALU.subtract).then_inc(dve_step, 1)
                own(1)
                e.tensor_tensor(out2, tn[:, 1, 0:T], tn[:, 1, T:2 * T], ALU.add).then_inc(ready, count)

            def mod_column(r, bank):
                return e.tensor_scalar(mod[:, bass.ds(r, 1), :].rearrange("p a c -> p (a c)"), ps[:, bank, T:T + 2],
                                       cols[:, bass.ds(COLS["ada_b"][0] + r, 1)], None, ALU.add)

            n_relu, n_scored, n_weighed, n_yT = Tally(), Tally(), Tally(), Tally()
            idx_steps = TT * (3 + 1 + 2 * (TOPK // 8) + 2)
            STEPS_L = 1 + 7 * (QK // 2) + VG + 1 + idx_steps + 2 * NU + MIXG + KT + 5 * BR + OUT
            per = ((step, STEPS_L), (n_std, 1), (n_scaled, KT), (n_normed, KT), (n_nhi, 3 * KT), (n_nsplit, 3 * KT),
                   (n_relu, TT), (n_scored, NU), (n_weighed, NU), (n_yT, KT))
            with turns(e, LAYERS, *per) as L:
                norm(T, True)
                m0, d0, _, _ = of_layer("qk", L)
                with turns(e, QK // RING, (step, 14)) as i:
                    for j in (0, 2):
                        e.wait_ge(chunk_done, m0 + RING * i + j + 2)
                        e.wait_ge(emptied_d, 4 + d0 + RING * i + j)
                        for b in range(2):
                            mod_column(ADA * L + RING * i + j + b, j + b).then_inc(dve_step, 1)
                            step()
                        rotate(ps[:, j, 0:T], ps[:, j + 1, 0:T], rope[:, 0, :], rope[:, 1, :],
                               flat(rot, RING * i + j), flat(rot, RING * i + j + 1), emptied_d, 2)
                m0, d0, _, _ = of_layer("vn", L)
                for g in range(VG):
                    e.wait_ge(chunk_done, m0 + 4 * g + 4)
                    for tt in range(TT):
                        last = e.tensor_copy(vn[:, tt, VW * g:VW * g + VW], ps[:, 4 + 2 * (g % 2) + tt, 0:VW])
                        if tt == 0:
                            last.then_inc(dve_step, 1)
                            step()
                    last.then_inc(emptied_d, 4)
                e.wait_ge(emptied_d, 4 + d0 + VN)
                e.tensor_scalar(iw[:, :, :], vn[:, :, 1216:1220], 1.0 / 16, None, ALU.mult).then_inc(dve_step, 1)
                own(1)

                for qt in range(TT):
                    w = P * (qt + 1)
                    acc = idx[:, qt, 0:w]
                    e.wait_ge(relu_done, n_relu())
                    e.tensor_scalar(acc, relu[:, 0, 0:w], iw[:, qt, 0:1], None, ALU.mult).then_inc(dve_step, 1)
                    own(1)
                    for h in range(1, 4):
                        last = e.scalar_tensor_tensor(out=acc, in0=relu[:, h % 2, w * (h // 2):w * (h // 2) + w], scalar=iw[:, qt, h:h + 1],
                                                      in1=acc, op0=ALU.mult, op1=ALU.add)
                        if h < 3:
                            last.then_inc(dve_step, 1)
                            own(1)
                    last.then_inc(idx_summed, 1)
                    e.wait_ge(idx_summed, n_relu.now)
                    tri = mask[:, 0:P]
                    e.tensor_tensor(idx[:, qt, w - P:w], idx[:, qt, w - P:w], tri, ALU.add).then_inc(dve_step, 1)
                    own(1)
                    for _ in range(TOPK // 8):
                        e.sem_inc(passed, 1)
                        e.max(top8[:, :], acc).then_inc(dve_step, 1)
                        own(1)
                        e.sem_inc(passed, 1)
                        e.match_replace(acc, top8[:, :], acc, TAKEN).then_inc(dve_step, 1)
                        own(1)
                    pk = picked[:, P * qt:P * qt + w]
                    e.tensor_scalar(pk, acc, TAKEN / 2, NEG, ALU.is_gt, ALU.mult).then_inc(dve_step, 1)
                    own(1)
                    e.tensor_tensor(pk[:, w - P:w], pk[:, w - P:w], tri, ALU.add).then_inc(dve_step, 1)
                    own(1)

                def maximum(u):
                    w = unit_width(u)
                    e.wait_ge(scored, n_scored())
                    e.reduce_max(rmax[:, u:u + 1], score_slot(u)[:, 0:w], axis=AX_X).then_inc(dve_step, 1)
                    own(1)
                    e.tensor_scalar(nmax[:, u:u + 1], rmax[:, u:u + 1], -HD ** -0.5, None, ALU.mult)\
                        .then_inc(maxed, 1)

                def finish(u):
                    qt, _, _, yc = UNITS[u]
                    e.wait_ge(weighed, n_weighed())
                    e.reciprocal(rrec[:, u:u + 1], rsum[:, u:u + 1]).then_inc(dve_step, 1)
                    own(1)
                    e.tensor_scalar(y[:, qt, yc:yc + HD], ps[:, 5, 0:HD], rrec[:, u:u + 1], None, ALU.mult)\
                        .then_inc(y_done, 1)

                a0 = of_layer("mixg", L)[2]
                maximum(0)
                for u in range(NU):
                    if u + 1 < NU:
                        maximum(u + 1)
                    if u:
                        c = MIX_CHUNK[u - 1]
                        if c is not None:
                            e.wait_ge(emptied_a, 4 + a0 + c + 1)
                            e.tensor_scalar(mg[:, c, :], mg[:, c, :], 1.0, None, ALU.add).then_inc(dve_step, 1)
                            own(1)
                            e.reciprocal(mg[:, c, :], mg[:, c, :])
                        finish(u - 1)
                finish(NU - 1)

                for f in range(KT):
                    e.wait_ge(yT_done, n_yT())
                    e.wait_ge(norm_split, n_nsplit.now + f + 1)
                    e.tensor_tensor(hn[:, f % 2, 0:T], ps[:, f % 4, 0:T], sg[:, f, T:2 * T], ALU.mult).then_inc(dve_step, 1)
                    own(1)
                    e.tensor_copy(hh[:, f, T:2 * T], hn[:, f % 2, 0:T]).then_inc(norm_hi, 1)
                n_nhi(KT)
                n_nsplit(KT)

                m0, d0, _, _ = of_layer("br", L)
                with turns(e, BR // RING, (step, 5 * RING), (n_nhi, RING), (n_nsplit, RING)) as i:
                    for j in range(RING):
                        bank = 4 * (j % 2)
                        e.wait_ge(chunk_done, m0 + RING * i + j + 1)
                        for b in range(3):
                            e.tensor_tensor(tn[:, b // 2, T * (b % 2):T * (b % 2) + T], ps[:, bank + b, 0:T],
                                            flat(mg, b * KT + RING * i + j), ALU.mult).then_inc(dve_step, 1)
                        mod_column(ADA * L + ADA_AT["br"] + RING * i + j, bank + 2).then_inc(emptied_d, 1)
                        e.wait_ge(emptied_d, 4 + d0 + RING * i + j + 1)
                        e.tensor_tensor(tn[:, 0, 0:T], tn[:, 0, 0:T], tn[:, 0, T:2 * T], ALU.add).then_inc(dve_step, 1)
                        own(4)
                        e.wait_ge(norm_split, n_nsplit())
                        e.tensor_tensor(hn[:, j % 2, 0:T], tn[:, 0, 0:T], tn[:, 1, 0:T], ALU.add).then_inc(dve_step, 1)
                        own(1)
                        e.tensor_copy(flat(hh, RING * i + j, 0, T), hn[:, j % 2, 0:T]).then_inc(norm_hi, 1)
                        n_nhi()
                m0, d0, _, _ = of_layer("out", L)
                with turns(e, OUT // RING, (step, RING)) as i:
                    for j in range(RING):
                        e.wait_ge(chunk_done, m0 + RING * i + j + 1)
                        mod_column(ADA * L + ADA_AT["out"] + RING * i + j, j).then_inc(dve_step, 1)
                        step()
                        xs = xk(RING * i + j, 1)[:, 0, :]
                        e.tensor_tensor(xs, ps[:, j, 0:T], xs, ALU.add).then_inc(emptied_d, 1)
                e.wait_ge(emptied_d, 4 + d0 + OUT)

            g0 = COLS["norm_g_2"][0]
            for l in range(LAYERS):
                for jn in range(3):
                    for q in range(2):
                        k0 = g0 + (3 * l + jn) * KT
                        c0 = ADA * l + 3 * jn * KT
                        e.scalar_tensor_tensor(out=gain[:, 3 * l + jn, :, q], scalar=1.0,
                                               in0=mod[:, c0 + KT:c0 + 2 * KT, q],
                                               in1=cols[:, k0:k0 + KT], op0=ALU.add, op1=ALU.mult)\
                            .then_inc(dve_step, 1)
                        e.tensor_scalar(gate[:, 3 * l + jn, :, q], mod[:, c0 + 2 * KT:c0 + 3 * KT, q],
                                        1.0 if jn == 1 else 0.5, None, ALU.mult).then_inc(dve_step, 1)
            own(24)
            e.memset(spare[:, 4:5], 0.0).then_inc(mod_ready, 1)
            dc = COLS["decay"][0]
            e.scalar_tensor_tensor(out=lg[:, :], in0=cols[:, dc:dc + 8], scalar=-1.0, in1=cols[:, dc:dc + 8],
                                   op0=ALU.mult, op1=ALU.min).then_inc(mod_ready, 1)

            norm(T, False)
            e.wait_ge(context_in, 16)

            n_act = Tally()

            def ffn(f, l, jn, halves):
                norm(halves * T, True)
                w = halves * T
                m0, d0, _, _ = later[f"up{f}"]
                with turns(e, 2 * FT // RING, (n_act, 2)) as i:
                    for j in (0, 1):
                        e.wait_ge(chunk_done, m0 + RING * i + 2 * j + 2)
                        e.wait_ge(act_step, n_act())
                        e.wait_ge(act_split, n_act.now - 1)
                        e.tensor_tensor(hn[:, j, 0:w], tn[:, j, 0:w], ps[:, 2 * j + 1, 0:w], ALU.mult)\
                            .then_inc(emptied_d, 2)
                        e.wait_ge(emptied_d, 4 + d0 + RING * i + 2 * j + 2)
                        e.tensor_copy(flat(ah, 2 * i + j, 0, w), hn[:, j, 0:w]).then_inc(act_hi, 1)
                m0, d0, _, _ = later[f"down{f}"]
                with turns(e, KT // 2, (step, 2 * (halves - 1))) as i:
                    for j in range(2):
                        e.wait_ge(chunk_done, m0 + 2 * RING * i + RING * j + RING)
                        for q in range(halves):
                            xs = xk(2 * i + j, 2)[:, q, :]
                            last = e.scalar_tensor_tensor(
                                out=xs, in0=ps[:, j, T * q:T * q + T],
                                scalar=gate[:, 3 * l + jn, bass.ds(2 * i + j, 1), q], in1=xs,
                                op0=ALU.mult, op1=ALU.add)
                            if q < halves - 1:
                                last.then_inc(dve_step, 1)
                                step()
                        last.then_inc(emptied_d, RING)
                e.wait_ge(emptied_d, 4 + d0 + RING * KT)

            ffn(0, 0, 0, 2)

            norm(2 * T, False)
            for n in range(16):
                b, r = divmod(n, 8)
                g, tt = divmod(r, 2)
                e.wait_ge(f1_done, n + 1)
                e.tensor_copy(pq[:, b, tt, g, :], ps[:, n % 4, :]).then_inc(f1_out, 1)
            for n in range(16):
                b, f = divmod(n, 8)
                e.wait_ge(f2_done, n + 1)
                dst = hh[:, f, T * b:T * b + T]
                e.tensor_copy(dst, ps[:, 4 + n % 4, 0:T]).then_inc(dve_step, 1)
                own(1)
                e.tensor_tensor(hl[:, f, T * b:T * b + T], ps[:, 4 + n % 4, 0:T], dst.bitcast(F32), ALU.subtract)\
                    .then_inc(f2_hi, 1)
            m0, d0, _, _ = later["four"]
            fb = COLS["four_b"][0]
            with turns(e, KT // RING, (step, 2 * RING)) as i:
                for j in range(RING):
                    o = RING * i + j
                    e.wait_ge(chunk_done, m0 + RING * i + j + 1)
                    e.wait_ge(emptied_d, 4 + d0 + RING * i + j)
                    for q in range(2):
                        e.tensor_scalar(tn[:, 0, T * q:T * q + T], ps[:, j, T * q:T * q + T],
                                        cols[:, bass.ds(fb + o, 1)], gate[:, 1, bass.ds(o, 1), q], ALU.add, ALU.mult)\
                            .then_inc(dve_step, 1)
                    own(2)
                    xs = xk(o, 2)
                    e.tensor_tensor(xs, xs, both(tn[:, 0, :], 2), ALU.add).then_inc(emptied_d, 1)
            e.wait_ge(emptied_d, 4 + d0 + KT)

            ffn(1, 0, 2, 2)
            ffn(2, 1, 0, 2)

            norm(2 * T, True)
            e.wait_ge(ret_tables_in, 48)
            for name, dst in (("rq", qT), ("rk", kT)):
                m0, d0, _, _ = later[name]
                with turns(e, KT // RING, (step, 14 if name == "rk" else 10)) as i:
                    for j in (0, 2):
                        e.wait_ge(chunk_done, m0 + RING * i + j + 2)
                        e.wait_ge(emptied_d, 4 + d0 + RING * i + j)
                        if name == "rk":
                            for b in range(2):
                                e.tensor_copy(flat(kT, RING * i + j + b, T, T), ps[:, j + b, T:2 * T])\
                                    .then_inc(dve_step, 1)
                                step()
                        rotate(ps[:, j, 0:T], ps[:, j + 1, 0:T], rope2[:, 0, :], rope2[:, 1, :],
                               flat(dst, RING * i + j, 0, T), flat(dst, RING * i + j + 1, 0, T), emptied_d, 2)
            m0, d0, _, _ = later["rv"]
            for g in range(RH):
                e.wait_ge(chunk_done, m0 + 4 * g + 4)
                for tt in range(2 * TT):
                    last = e.tensor_copy(vr[:, tt, RDV * g:RDV * g + RDV], ps[:, 4 * (g % 2) + tt, :])
                    if tt < 2 * TT - 1:
                        last.then_inc(dve_step, 1)
                        step()
                last.then_inc(emptied_d, 4)
            for h in range(RH):
                e.wait_ge(decayed, 2 * h + 2)
                for b in range(2):
                    e.tensor_tensor(dec[:, b, 0:2, :], dec[:, b, 0:2, :], dmask[:, b, :, :], ALU.mult)\
                        .then_inc(dve_step, 1)
                own(2)
                e.tensor_tensor(dec[:, 0, :, :], dec[:, 0, :, :], dec[:, 1, :, :], ALU.add).then_inc(dve_step, 1)
                own(1)
                for jt in range(4):
                    e.wait_ge(rs_done, 4 * h + jt + 1)
                    e.scalar_tensor_tensor(out=sT[:, jt, :], in0=ps[:, jt % 2, 0:T], scalar=1.0 / 16,
                                           in1=dec[:, 0, jt, :], op0=ALU.mult, op1=ALU.mult).then_inc(rs_out, 1)
                for dv in range(4):
                    e.wait_ge(ry_done, 4 * h + dv + 1)
                    e.tensor_copy(yr[:, dv, :], ps[:, 2 + dv % 2, 0:T]).then_inc(ry_out, 1)
                e.wait_ge(rmean, h + 1)
                e.tensor_scalar(sq[:, 0, T:2 * T], ps[:, 6, 0:T], 1.0 / RDV, None, ALU.mult).then_inc(dve_step, 1)
                own(1)
                for dv in range(4):
                    e.tensor_tensor(yr[:, dv, :], yr[:, dv, :], sq[:, 0, T:2 * T], ALU.subtract).then_inc(dve_step, 1)
                own(4)
                for dv in range(4):
                    if h or dv >= 2:
                        e.wait_ge(rc_done, 4 * h + dv - 1)
                    e.tensor_tensor(sq[:, dv % 2, 0:T], yr[:, dv, :], yr[:, dv, :], ALU.mult).then_inc(rcent, 1)
                e.wait_ge(rstd, h + 1)
                e.reciprocal(rs[:, 0:T], rs[:, 0:T]).then_inc(dve_step, 1)
                own(1)
                for dv in range(4):
                    f = 4 * h + dv
                    e.tensor_tensor(yr[:, dv, :], yr[:, dv, :], rs[:, 0:T], ALU.mult).then_inc(dve_step, 1)
                    own(1)
                    e.tensor_tensor(yr[:, dv, :], yr[:, dv, :], sgr[:, f, :], ALU.mult).then_inc(dve_step, 1)
                    own(1)
                    dst = hh[:, f // 2, T * (f % 2):T * (f % 2) + T]
                    e.tensor_copy(dst, yr[:, dv, :]).then_inc(dve_step, 1)
                    own(1)
                    e.tensor_tensor(hl[:, f // 2, T * (f % 2):T * (f % 2) + T], yr[:, dv, :], dst.bitcast(F32),
                                    ALU.subtract).then_inc(rgn, 1)
                e.wait_ge(rgn, 4 * h + 4)
            m0, d0, _, _ = later["ro"]
            with turns(e, KT // 2) as i:
                for j in range(2):
                    e.wait_ge(chunk_done, m0 + RING * i + 2 * j + 2)
                    xs = xk(2 * i + j, 1)[:, 0, :]
                    e.scalar_tensor_tensor(out=xs, in0=ps[:, j, 0:T], scalar=gate[:, 4, bass.ds(2 * i + j, 1), 0],
                                           in1=xs, op0=ALU.mult, op1=ALU.add).then_inc(emptied_d, 2)
            e.wait_ge(emptied_d, 4 + d0 + 2 * KT)
            ffn(3, 1, 2, 1)
            norm(T, False)

        @block.tensor
        def _(e):
            n_sq, n_split = Tally(), Tally()

            def norm(cols_n, split):
                for k in range(KT):
                    e.wait_ge(sq_done, n_sq())
                    e.matmul(ps[:, 7, 0:cols_n], ones[:, :], sq[:, k % 2, 0:cols_n], start=(k == 0),
                             stop=(k == KT - 1)).then_inc(sq_summed, 1)
                if split:
                    e.wait_ge(norm_split, n_split(KT) + 2)

            def products(bank, j, tiles, k0, move, lo, n, first, last):
                mh, ml = move
                for t in tiles:
                    w = slice(t * P, t * P + P)
                    k = k0 + t
                    hi, low = mh[:, k, lo:lo + n], ml[:, k, lo:lo + n]
                    e.matmul(ps[:, bank, 0:n], wh[:, j, w], hi, start=(first and t == tiles[0]), stop=False)
                    e.matmul(ps[:, bank, 0:n], wh[:, j, w], low, start=False, stop=False)
                    end = e.matmul(ps[:, bank, 0:n], wl[:, j, w], hi, start=False,
                                   stop=(last and t == tiles[-1]))
                return end

            h = (hh, hl)

            def modulation(lap, j, bank):
                e.wait_ge(ada_landed[j], 16 * lap + 16)
                for k in range(KT):
                    end = e.matmul(ps[:, bank, T:T + 2], ada[j][:, k * P:k * P + P], sc[:, k, :], start=(k == 0),
                                   stop=(k == KT - 1))
                end.then_inc(ada_done, 1)

            def plain(base, cols_n, freed, lo=0, ada_lap=None):
                m0, d0, a0, n = base
                e.sem_inc(passed, 1)
                with e.Fori(0, n // RING) as i:
                    for j in range(RING):
                        e.wait_ge(lo_done, RING + m0 + RING * i + j + 1)
                        f0 = d0 if freed is emptied_d else a0
                        e.wait_ge(freed, f0 + RING * i + j + 1)
                        if ada_lap is not None:
                            modulation(ada_lap + i, j, j)
                        products(j, j, range(KT), 0, h, lo, cols_n, True, True).then_inc(chunk_done, 1)

            def natural(j, c, width, bank, tts, first, last):
                for tt in range(tts):
                    for t in range(2):
                        tok = slice(P * tt, P * tt + P)
                        w = slice(t * width, t * width + width)
                        k = 2 * c + t
                        out = ps[:, bank + tt, 0:width]
                        e.matmul(out, hh[:, k, tok], wh[:, j, w], start=(first and t == 0), stop=False)
                        e.matmul(out, hh[:, k, tok], wl[:, j, w], start=False, stop=False)
                        end = e.matmul(out, hl[:, k, tok], wh[:, j, w], start=False, stop=(last and t == 1))
                return end

            e.wait_ge(c_silu, 1)

            n_y, n_sc, n_ex, n_co = Tally(), Tally(), Tally(), Tally()
            n_relu, n_yTo = Tally(), Tally()
            per = ((n_sq, KT), (n_split, 3 * KT), (n_y, NU), (n_ex, NU), (n_co, NU), (n_relu, TT))
            with turns(e, LAYERS, *per) as L:
                norm(T, True)
                lap = {name: at_ // RING + L * (ADA // RING) for name, at_ in ADA_AT.items()}
                plain(of_layer("qk", L), T, emptied_d, 0, lap["qk"])
                m0, d0, a0, _ = of_layer("vn", L)
                for g in range(VG):
                    for c in range(4):
                        e.wait_ge(lo_done, RING + m0 + 4 * g + c + 1)
                        if g == 2 and c == 0:
                            e.wait_ge(emptied_d, 4 + d0 + 4)
                        natural(c, c, VW, 4 + 2 * (g % 2), TT, c == 0, c == 3).then_inc(chunk_done, 1)

                e.wait_ge(heads_in, 192 * L + 192)

                def head(pl, lo, n):
                    tile, half = pl
                    return heads[64 * half:64 * half + 64, tile, lo:lo + n]

                for qt in range(TT):
                    w = P * (qt + 1)
                    e.wait_ge(emptied_d, 4 + d0 + 4 * (qt + 2))
                    for ih in range(4):
                        pos = IQ + ih
                        key = (24, 0) if pos % 2 == 0 else (23, 1)
                        lo = w * (ih // 2)
                        end = e.matmul(ps[:, 6 - 2 * qt + ih % 2, lo:lo + w],
                                       head((pos // 2, pos % 2), P * qt, P), head(key, 0, w), start=True, stop=True)
                    end.then_inc(logits, 1)
                plain(of_layer("gate", L), T, emptied_a, 0, lap["gate"])
                e.wait_ge(relu_done, n_relu(TT))
                m0, d0, a0, _ = of_layer("mixg", L)
                e.wait_ge(emptied_a, 4 + a0)

                def mix_chunk(c):
                    e.wait_ge(lo_done, RING + m0 + c + 1)
                    e.wait_ge(emptied_a, a0 + c + 3)
                    modulation(lap["mixg"] + c // RING, c % RING, 6 + c % 2)
                    products(6 + c % 2, c % RING, range(KT), 0, h, 0, T, True, True).then_inc(chunk_done, 1)

                def score(u):
                    qt, segs, _, _ = UNITS[u]
                    w = P * (qt + 1)
                    if u >= 2:
                        e.wait_ge(exped, n_ex.now + u - 1)
                    if u == 20:
                        e.wait_ge(maxed, NU * L + 1)
                    for s, (qp, kp, mk) in enumerate(segs):
                        at_ = w * s
                        bank, lo = 2 * (u % 2) + at_ // 512, at_ % 512
                        e.matmul(ps[:, bank, lo:lo + w], head(qp, P * qt, P), head(kp, 0, w), start=True, stop=False)
                        if mk == "picked":
                            out, src = ps[:, bank, lo:lo + w], picked[:, P * qt:P * qt + w]
                        elif (mk, qt) == ("tri", 1):
                            out, src = ps[:, bank, lo + P:lo + w], mask[:, 0:P]
                        else:
                            m_at, m_n = MASK[mk, qt]
                            out, src = ps[:, bank, lo:lo + w], mask[:, m_at:m_at + m_n]
                        end = e.matmul(out, identb[:, :], src, start=False, stop=True)
                    end.then_inc(scored, 1)

                def weigh(u):
                    qt, segs, vcols, _ = UNITS[u]
                    e.wait_ge(copied, n_co.now + u + 1)
                    if u >= 1:
                        e.wait_ge(y_done, n_y.now + u)
                    blocks = [(s, kt) for s in range(len(segs)) for kt in range(qt + 1)]
                    for b, (s, kt) in enumerate(blocks):
                        end = e.matmul(ps[:, 5, 0:HD], probT[u % 2][:, b * P:b * P + P],
                                       vn[:, kt, vcols[s]:vcols[s] + HD], start=(b == 0), stop=(b == len(blocks) - 1))
                    end.then_inc(weighed, 1)

                score(0)
                for u in range(NU):
                    if u + 1 < NU:
                        score(u + 1)
                    if MIX_CHUNK[u] is not None:
                        mix_chunk(MIX_CHUNK[u])
                    if u:
                        weigh(u - 1)
                    e.wait_ge(exped, n_ex.now + u + 1)
                    if u:
                        e.wait_ge(copied, n_co.now + u)
                    for b in range(unit_width(u) // P):
                        end = e.transpose(ps[:, 3 + b // 4, (b % 4) * P:(b % 4) * P + P],
                                          prob[u % 2][:, b * P:b * P + P], ident[:, :])
                    end.then_inc(turned, 1)
                weigh(NU - 1)
                n_ex(NU)
                n_co(NU)
                n_y(NU)
                e.wait_ge(y_done, n_y.now)
                for f in range(KT):
                    if f >= 4:
                        e.wait_ge(norm_hi, 3 * KT * L + KT + f - 3)
                    for tt in range(TT):
                        end = e.transpose(ps[:, f % 4, P * tt:P * tt + P], y[:, tt, f * P:f * P + P], ident[:, :])
                    end.then_inc(yT_done, 1)
                e.wait_ge(norm_split, n_split(KT) + 2)

                m0, d0, a0, n = of_layer("br", L)
                e.wait_ge(emptied_a, 4 + a0)
                e.sem_inc(passed, 1)
                with e.Fori(0, n // RING) as i:
                    for j in range(RING):
                        e.wait_ge(lo_done, RING + m0 + RING * i + j + 1)
                        e.wait_ge(emptied_d, d0 + RING * i + j + 3)
                        bank = 4 * (j % 2)
                        modulation(lap["br"] + i, j, bank + 2)
                        products(bank, j, range(0, 3), 0, h, T, T, True, True)
                        products(bank + 1, j, range(3, 6), 0, h, T, T, True, True)
                        products(bank + 2, j, range(6, 8), 0, h, T, T, True, True).then_inc(chunk_done, 1)
                e.wait_ge(norm_split, n_split(KT) + 2)
                plain(of_layer("out", L), T, emptied_d, 0, lap["out"])

            norm(T, False)
            n_act = Tally()

            def ffn(f, halves):
                w = halves * T
                norm(w, True)
                m0, d0, a0, n = later[f"up{f}"]
                with e.Fori(0, n // RING) as i:
                    for j in range(RING):
                        e.wait_ge(lo_done, RING + m0 + RING * i + j + 1)
                        e.wait_ge(emptied_d, d0 + RING * i + j - j % 2 + 2)
                        products(j, j, range(KT), 0, h, 0, w, True, True).then_inc(chunk_done, 1)
                e.wait_ge(act_split, n_act(FT) + 1)
                m0, d0, a0, n = later[f"down{f}"]
                with e.Fori(0, n // (2 * RING)) as i:
                    for o in range(2):
                        for j in range(RING):
                            c = RING * o + j
                            e.wait_ge(lo_done, RING + m0 + 2 * RING * i + c + 1)
                            if j == 0:
                                e.wait_ge(emptied_d, 4 + d0 + 2 * RING * i + c - RING)
                            products(o, j, range(DOWN[j]), sum(DOWN[0:j]), (ah, al), 0, w, j == 0, j == 3)\
                                .then_inc(chunk_done, 1)

            ffn(0, 2)

            norm(2 * T, False)
            e.wait_ge(tables_in, 32)
            e.wait_ge(emptied_d, 4 + later["four"][1])
            e.wait_ge(normed, KT * (LAYERS + 3))
            for n in range(16):
                b, r = divmod(n, 8)
                g, tt = divmod(r, 2)
                if n >= 4:
                    e.wait_ge(f1_out, n - 3)
                for kk in range(2):
                    tok = T * b + P * tt
                    end = e.matmul(ps[:, n % 4, :], hf[:, 2 * g + kk, tok:tok + P], dft[:, kk, :], start=(kk == 0),
                                   stop=(kk == 1))
                end.then_inc(f1_done, 1)
            for n in range(16):
                b, f = divmod(n, 8)
                e.wait_ge(f1_out, 8 * b + 8)
                if n >= 4:
                    e.wait_ge(f2_hi, n - 3)
                for q, (tt, part) in enumerate((tt, part) for tt in range(TT) for part in range(2)):
                    lo = T * part + P * (f % 2)
                    end = e.matmul(ps[:, 4 + n % 4, 0:T], pq[:, b, tt, f // 2, lo:lo + P], dftn[:, tt, part, :],
                                   start=(q == 0), stop=(q == 3))
                end.then_inc(f2_done, 1)
            e.wait_ge(f2_hi, 16)
            plain(later["four"], 2 * T, emptied_d)
            ffn(1, 2)
            ffn(2, 2)

            norm(2 * T, True)
            plain(later["rq"], T, emptied_d)
            plain(later["rk"], 2 * T, emptied_d)
            m0, d0, a0, _ = later["rv"]
            for g in range(RH):
                for c in range(4):
                    e.wait_ge(lo_done, RING + m0 + 4 * g + c + 1)
                    if c == 0:
                        e.wait_ge(emptied_d, 4 + d0 + max(0, 4 * g - 4))
                    natural(c, c, RDV, 4 * (g % 2), 2 * TT, c == 0, c == 3).then_inc(chunk_done, 1)
            e.wait_ge(emptied_d, 4 + d0 + 12)
            plain(later["rg"], T, emptied_a)
            e.wait_ge(emptied_d, 4 + later["ro"][1])
            e.wait_ge(emptied_a, 4 + later["ro"][2])
            for h_ in range(RH):
                for jt in range(4):
                    n = 4 * h_ + jt
                    if n >= 2:
                        e.wait_ge(rs_out, n - 1)
                    for dd in range(2):
                        end = e.matmul(ps[:, jt % 2, 0:T], kT[:, 2 * h_ + dd, P * jt:P * jt + P], qT[:, 2 * h_ + dd, :],
                                       start=(dd == 0), stop=(dd == 1))
                    end.then_inc(rs_done, 1)
                for dv in range(4):
                    n = 4 * h_ + dv
                    e.wait_ge(rs_out, 4 * h_ + 4)
                    if n >= 2:
                        e.wait_ge(ry_out, n - 1)
                    for jt in range(4):
                        lo = RDV * h_ + P * dv
                        end = e.matmul(ps[:, 2 + dv % 2, 0:T], vr[:, jt, lo:lo + P], sT[:, jt, :], start=(jt == 0),
                                       stop=(jt == 3))
                    end.then_inc(ry_done, 1)
                e.wait_ge(ry_out, 4 * h_ + 4)
                for dv in range(4):
                    end = e.matmul(ps[:, 6, 0:T], ones[:, :], yr[:, dv, :], start=(dv == 0), stop=(dv == 3))
                end.then_inc(rmean, 1)
                for dv in range(4):
                    e.wait_ge(rcent, 4 * h_ + dv + 1)
                    end = e.matmul(ps[:, 7, 0:T], ones[:, :], sq[:, dv % 2, 0:T], start=(dv == 0), stop=(dv == 3))
                    end.then_inc(rc_done, 1)
            e.wait_ge(rgn, 4 * RH)
            m0, d0, a0, n = later["ro"]
            with e.Fori(0, n // RING) as i:
                for j in range(RING):
                    e.wait_ge(lo_done, RING + m0 + RING * i + j + 1)
                    if j % 2 == 0:
                        e.wait_ge(emptied_d, 4 + d0 + RING * i + j - 2)
                    for t in range(KT):
                        f = KT * (j % 2) + t
                        w = slice(t * P, t * P + P)
                        mh, ml = (b[:, f // 2, T * (f % 2):T * (f % 2) + T] for b in h)
                        out = ps[:, j // 2, 0:T]
                        e.matmul(out, wh[:, j, w], mh, start=(f == 0), stop=False)
                        e.matmul(out, wh[:, j, w], ml, start=False, stop=False)
                        end = e.matmul(out, wl[:, j, w], mh, start=False, stop=(f == 2 * KT - 1))
                    end.then_inc(chunk_done, 1)
            ffn(3, 1)
            norm(T, False)


IN_SIZES = (384, 384, 384, 384, 384, 64, 64, 384, 256, 64, 4, 768, 768, 768, 256, 3072)
IN_AT = dict(zip(("a_q", "a_k", "a_v", "a_g", "b_q", "b_k", "b_v", "b_g", "i_q", "i_k", "i_w", "c_q", "c_k", "c_v",
                  "c_g", "m_g"), zip(np.cumsum((0,) + IN_SIZES[:-1]).tolist(), IN_SIZES)))


def tiles(w):
    k, n = w.shape
    return w.reshape(k // P, P, n // P, P).transpose(2, 1, 0, 3).reshape(n // P, P, k)


def natural_chunks(w, width):
    g = w.shape[1] // width
    return w.reshape(4, 2, P, g, width).transpose(3, 0, 2, 1, 4).reshape(4 * g, P, 2 * width)


def rows(v):
    return v.reshape(-1, P).transpose(1, 0)


def tables():
    f32 = np.float32
    inv = (1.0 / (f32(10000.0) ** (np.arange(0, HD, 2, dtype=f32) / f32(HD)))).astype(f32)
    ang = np.arange(T, dtype=f32)[:, None] * inv[None, :]
    cos, sin = np.cos(ang).T, np.sin(ang).T
    rope = np.concatenate([np.tile(cos, (4, 1)), np.tile(sin, (4, 1))], 1).astype(f32)

    i = np.arange(T)
    diff = i[:, None] - i[None, :]
    ok = {"tri": diff >= 0, "w128": (diff >= 0) & (diff <= 128), "d4": (diff >= 0) & (diff % 4 == 0),
          "d16": (diff >= 0) & (diff % 16 == 0)}
    mask = np.zeros((P, MASKW), f32)
    for (name, qt), (at, n) in MASK.items():
        mask[:, at:at + n] = np.where(ok[name][P * qt:P * qt + P, 0:n], 0.0, NEG)

    n = np.arange(T)
    ph = 2 * np.pi * ((n[:, None] * n[None, :]) % T) / T
    c, s = np.cos(ph), np.sin(ph)
    by_feature = np.concatenate([c, s], 1).reshape(2, P, 2 * T).transpose(1, 0, 2).reshape(P, -1)
    by_token = (np.stack([c, -s], 1) / T).reshape(TT, P, 2, T).transpose(1, 0, 2, 3).reshape(P, -1)
    dft = np.concatenate([by_feature, by_token], 1).astype(f32)

    rws = T // 64
    row = np.repeat(np.arange(rws, dtype=f32), 64)
    col = np.tile(np.arange(64, dtype=f32), rws)
    inv2 = f32(10000.0) ** (-np.arange(64, dtype=f32) / f32(64))
    ang2 = np.concatenate([row[:, None] * inv2, col[:, None] * inv2], 1).astype(f32)
    rope2 = np.concatenate([np.cos(ang2).T, np.sin(ang2).T], 1).astype(f32)

    j, q = np.arange(T)[:, None], np.arange(T)[None, :]
    fwd = np.concatenate([np.maximum(q - j, 0), q - j + T], 0)
    bwd = np.concatenate([np.maximum(j - q, 0), T - q + j], 0)
    dist = np.stack([fwd, bwd]).reshape(2, 4, P, T).transpose(2, 0, 1, 3).reshape(P, -1).astype(np.float16)
    dmask = np.stack([q >= j, j >= q]).reshape(2, 2, P, T).transpose(2, 0, 1, 3).reshape(P, -1).astype(np.float16)
    return rope, mask, dft, rope2, dist, dmask


def kernel(x, norm_g, w_in, w_br_a, w_br_b, w_br_c, w_out, final_norm_g, c_2, ctx_2, c_ctx_2, ada_w_2, ada_b_2,
           norm_g_2, final_g_2, ffn_w_gate_2, ffn_w_up_2, ffn_w_down_2, four_w_2, four_b_2, ret_w_in_2,
           ret_w_out_2, ret_decay_2):
    import ml_dtypes
    import concourse.bacc as _bacc
    from concourse import mybir as _mybir
    from concourse.bass_utils import run_bass_kernel_spmd as _run

    xT = np.concatenate([x[0].transpose(1, 0), ctx_2[0].transpose(1, 0)], 1)
    decay = np.broadcast_to(ret_decay_2.reshape(1, 8), (P, 8))
    cc = np.stack([rows(c_2), rows(c_ctx_2)], 2).reshape(P, 16)
    cols = np.concatenate([rows(norm_g), rows(final_norm_g), rows(norm_g_2), rows(final_g_2), rows(four_b_2),
                           rows(ada_b_2), cc, decay], 1)
    ada = np.concatenate([tiles(w) for w in ada_w_2], 0)

    heads = ([("a_q", h) for h in range(6)] + [("a_k", h) for h in range(6)] + [("c_q", h) for h in range(12)]
             + [("c_k", h) for h in range(12)] + [("b_q", h) for h in range(6)] + [("i_q", h) for h in range(4)]
             + [("b_k", 0), ("i_k", 0)])
    qk_cols = []
    for g in range(NPOS // 4):
        for half in range(2):
            for name, h in heads[4 * g:4 * g + 4]:
                at = IN_AT[name][0] + HD * h + 32 * half
                qk_cols += list(range(at, at + 32))

    def span(*names):
        return [i for name in names for i in range(IN_AT[name][0], IN_AT[name][0] + IN_AT[name][1])]

    v_cols = span("a_v", "b_v", "c_v", "i_w")
    g_cols = span("a_g", "b_g", "c_g", "m_g")
    w1, wv = [], []
    for l in range(LAYERS):
        branch = np.concatenate([w_br_a[l], w_br_b[l], w_br_c[l]], 0)
        w1 += [tiles(w_in[l][:, qk_cols]), tiles(w_in[l][:, g_cols]), tiles(branch), tiles(w_out[l])]
        padded = np.concatenate([w_in[l][:, v_cols], np.zeros((D, VG * VW - len(v_cols)), np.float32)], 1)
        wv.append(natural_chunks(padded, VW))
    w1, wv = np.concatenate(w1, 0), np.concatenate(wv, 0)

    wu, wd = [], []
    for l in range(LAYERS):
        for f in range(2):
            both = np.stack([tiles(ffn_w_gate_2[l, f]), tiles(ffn_w_up_2[l, f])], 1)
            wu.append(both.reshape(2 * FT, P, CW))
            wd.append(tiles(ffn_w_down_2[l, f]))
    wu, wd = np.concatenate(wu, 0), np.concatenate(wd, 0)
    ret = ret_w_in_2[0]
    ro = tiles(ret_w_out_2[0]).reshape(KT, P, 2, CW).transpose(0, 2, 1, 3).reshape(2 * KT, P, CW)
    w2 = np.concatenate([tiles(four_w_2[0]), tiles(ret[:, 0:D]), tiles(ret[:, D:2 * D]),
                         natural_chunks(ret[:, 2 * D:4 * D], RDV), tiles(ret[:, 4 * D:6 * D]), ro], 0)
    rope, mask, dft, rope2, dist, dmask = tables()

    given = [("xT", xT), ("cols", cols), ("ada", ada), ("w1", w1), ("wv", wv), ("wu", wu), ("wd", wd), ("w2", w2),
             ("rope", rope), ("mask", mask.astype(ml_dtypes.bfloat16)), ("ident", np.eye(P, dtype=np.float32)),
             ("identb", np.eye(P, dtype=ml_dtypes.bfloat16)), ("dft", dft), ("rope2", rope2), ("dist", dist),
             ("dmask", dmask)]
    nc = _bacc.Bacc("TRN2", target_bir_lowering=False, num_devices=1)
    arrays, args = {}, []
    for name, a in given:
        a = np.ascontiguousarray(a)
        arrays[f"in_{name}_dram"] = a
        args.append(nc.dram_tensor(f"in_{name}_dram", a.shape, _mybir.dt.from_np(a.dtype), kind="ExternalInput").ap())
    args.append(nc.dram_tensor("out_0_dram", (D, T), F32, kind="ExternalOutput").ap())
    program(nc, *args)
    r = _run(nc, [arrays], core_ids=[0])
    return r.results[0]["out_0_dram"].transpose(1, 0).reshape(1, T, D)
```

```python
from contextlib import ExitStack, contextmanager

import numpy as np

import concourse.bass as bass
from concourse import mybir

F32 = mybir.dt.float32
F32R = mybir.dt.float32r
F16 = mybir.dt.float16
BF16 = mybir.dt.bfloat16
ACT = mybir.ActivationFunctionType
ALU = mybir.AluOpType
AX_X = mybir.AxisListType.X

P = 128
D = 1024
KT = D // P
T = 256
TT = T // P
HD = 64
LAYERS = 2
EPS = 1e-6
NEG = -1e30
TAKEN = -3e38
TOPK = 64
FFN = 2816
FT = FFN // P
RING = 4
AHEAD = 3
VG, VW = 3, 408
DOWN = (6, 5, 6, 5)
W8 = (KT * P,) * RING
WV = (2 * VW,) * RING
WD = tuple(k * P for k in DOWN)
CW = KT * P
RH = 4
RDV = 512
ADA = 9 * KT

QK, VN, GATE, MIXG, BR, OUT = 24, 12, 8, 24, 8, 8
PER_LAYER = QK + VN + GATE + MIXG + BR + OUT
PER_D = QK + VN + BR + OUT
PER_A = GATE + MIXG

AQ, AK, CQ, CK, BQ, IQ, BK, IK = 0, 6, 12, 24, 36, 42, 46, 47
NPOS = 48

MASK = {("tri", 0): (0, 128), ("d4", 0): (128, 128), ("d16", 0): (256, 128),
        ("w128", 1): (384, 256), ("d4", 1): (640, 256), ("d16", 1): (896, 256)}
MASKW = 1152


def softmax_units():
    units = []

    def place(pos):
        return pos // 2, pos % 2

    for h in range(6):
        for qt in range(TT):
            units.append((qt, [(place(AQ + h), place(AK + h), "tri")], [64 * h], 64 * h))
    for s in range(4):
        for qt in (1, 0):
            first = "tri" if qt == 0 else "w128"
            segs = [(place(CQ + 4 * g + s), place(CK + 4 * g + s), m)
                    for g, m in enumerate((first, "d4", "d16"))]
            units.append((qt, segs, [448 + 64 * (4 * g + s) for g in range(3)], 768 + 64 * s))
    for h in range(6):
        for qt in range(TT):
            units.append((qt, [(place(BQ + h), (23, 0) if h % 2 == 0 else (24, 1), "picked")],
                          [384], 384 + 64 * h))
    return units


UNITS = softmax_units()
NU = len(UNITS)

COLS = {}
_at = 0
for _name, _n in (("norm_g", 16), ("final_norm_g", 8), ("norm_g_2", 48), ("final_g_2", 8),
                  ("four_b", 8), ("ada_b", 144), ("decay", 8)):
    COLS[_name] = (_at, _n)
    _at += _n
NCOLS = _at


class Tally:

    def __init__(self, start=0):
        self.base, self.n = 0, start

    def __call__(self, k=1):
        self.n += k
        return self.base + self.n

    @property
    def now(self):
        return self.base + self.n


@contextmanager
def turns(eng, count, *tallies):
    kept = [(t, t.base, t.n) for t, _ in tallies]
    with eng.Fori(0, count) as i:
        for t, k in tallies:
            t.base = t.base + i * k
        yield i
    for (t, base, n), (_, k) in zip(kept, tallies):
        assert t.n - n == k, (t.n - n, k)
        t.base, t.n = base, n + k * count


def program(nc, xT_d, cols_d, cond_d, ada_d, w1_d, wv_d, wu_d, wd_d, w2_d, rope_d, mask_d, ident_d, identb_d,
            dft_d, rope2_d, dist_d, dmask_d, out_d):
    with ExitStack() as ctx:
        top = [-(-nc.sbuf_base // 64) * 64]

        def at(name, shape, dt, offset):
            return nc.alloc_sbuf_tensor_at(name, shape, dt, offset=offset)

        def size(shape, dt):
            n = 2 if dt in (F16, BF16) else 4
            for s in shape[1:]:
                n *= s
            return -(-n // 64) * 64

        def keep(name, shape, dt=F32):
            t = at(name, shape, dt, top[0])
            top[0] += size(shape, dt)
            return t

        x_at = top[0]
        h_at = x_at + size([P, 2, KT, T], F32)
        x = keep("x", [P, 2, KT, T])
        hh = keep("h_high", [P, KT, 2 * T], F32R)
        sg = at("sg", [P, KT, 2 * T], F32, top[0])
        hl = keep("h_low", [P, KT, 2 * T], F32R)
        raw = keep("raw", [P, RING, CW])
        wh = keep("w_high", [P, RING, CW], F32R)
        wl = keep("w_low", [P, RING, CW], F32R)
        cols = keep("cols", [P, NCOLS])
        ident = keep("ident", [P, P])
        ones = keep("ones", [P, P])
        identb = keep("identb", [P, P], BF16)
        mask = keep("mask", [P, MASKW], BF16)
        rope = keep("rope", [P, 2, T])
        mod = keep("mod", [P, LAYERS * ADA, 2])
        gain = keep("gain", [P, LAYERS * 3, KT, 2])
        gate = keep("gate", [P, LAYERS * 3, KT, 2])
        eps = keep("eps", [P, 1])
        sq = keep("sq", [P, 2, 2 * T])
        rs = keep("rs", [P, 2 * T])
        sT = at("sT", [P, 4, T], F32, top[0])
        tn = keep("tn", [P, 2, 2 * T])
        nb = at("norm_buf", [P, 4, 2 * T], F32, top[0] - size([P, 2, 2 * T], F32))
        yr = at("yr", [P, 4, T], F32, top[0])
        hn = keep("hn", [P, 2, 2 * T])
        rsum = keep("rsum", [P, NU])
        nmax = keep("nmax", [P, NU])
        rmax = keep("rmax", [P, NU])
        rrec = keep("rrec", [P, NU])
        iw = keep("iw", [P, TT, 4])
        top8 = keep("top8", [P, 8])
        lg = keep("lg", [P, 8])
        spare = keep("spare", [P, 8])
        arena = top[0]

        class Area:
            def __init__(self, base):
                self.at = base

            def __call__(self, name, shape, dt=F32):
                t = at(name, shape, dt, self.at)
                self.at += size(shape, dt)
                return t

        a1 = Area(arena)
        rot = a1("rot", [P, QK, T])
        mg = at("mg", [P, 3 * KT, T], F32, arena)
        heads = a1("heads", [P, NPOS // 2 + 1, T])
        vn = a1("vn", [P, TT, VG * VW])
        relu = at("relu", [P, 2, 2 * T], F32, a1.at)
        prob = [a1("prob0", [P, 768]), a1("prob1", [P, 384])]
        idx = at("idx", [P, TT, T], F32, a1.at)
        probT = [a1("probT0", [P, 768]), a1("probT1", [P, 384])]
        y = a1("y", [P, TT, D])
        picked = a1("picked", [P, 3 * P], BF16)
        ada = at("ada", [P, 2, D], F32, x_at + 4 * KT * T)
        cb = a1("silu_c", [P, 2, D])
        ada_prod = a1("ada_prod", [P, D])
        ada2 = at("ada2", [P, RING, D], F32, h_at)
        cb2 = at("silu_c2", [P, 2, D], F32, h_at + size([P, KT, 2 * T], F32))

        a2 = Area(arena)
        ah = a2("act_high", [P, FT, 2 * T], F32R)
        al = a2("act_low", [P, FT, 2 * T], F32R)

        a3 = Area(arena)
        hf = a3("hf", [P, KT, 2 * T])
        pq = a3("pq", [P, 2, TT, 4, 2 * T])
        dft = a3("dft", [P, 2, 2 * T])
        dftn = a3("dftn", [P, TT, 2, T])

        a4 = Area(arena)
        qT = a4("qT", [P, KT, T])
        kT = a4("kT", [P, KT, 2 * T])
        vr = a4("vr", [P, 2 * TT, RH * RDV])
        sgr = a4("sgr", [P, 2 * KT, T])
        dist = a4("dist", [P, 2, 4, T], F16)
        dmask = a4("dmask", [P, 2, 2, T], F16)
        rope2 = a4("rope2", [P, 2, T])
        dec = a4("dec", [P, 2, 4, T])
        for a in (a1, a2, a3, a4):
            assert a.at <= nc.sbuf_top, (a.at, nc.sbuf_top)

        ps = ctx.enter_context(nc.psum_tensor("ps", [P, 8, 512], F32))

        def sem(name):
            return ctx.enter_context(nc.semaphore(name))

        landed = [sem(f"landed{j}") for j in range(RING)]
        ada_landed = [sem(f"ada_landed{j}") for j in range(2)]
        consts_in = sem("consts_in")
        x_in = sem("x_in")
        cond_in = sem("cond_in")
        context_in = sem("context_in")
        tables_in = sem("tables_in")
        ret_tables_in = sem("ret_tables_in")
        heads_in = sem("heads_in")
        ones_set = sem("ones_set")
        eps_set = sem("eps_set")
        c_silu = sem("c_silu")
        ada_step = sem("ada_step")
        ada2_landed = [sem(f"ada2_landed{j}") for j in range(RING)]
        ada2_done = sem("ada2_done")
        ada_done = sem("ada_done")
        mod_ready = sem("mod_ready")
        hi_done = sem("hi_done")
        lo_done = sem("lo_done")
        chunk_done = sem("chunk_done")
        emptied_d = sem("emptied_d")
        emptied_a = sem("emptied_a")
        sq_done = sem("sq_done")
        sq_summed = sem("sq_summed")
        std_done = sem("std_done")
        scaled = sem("scaled")
        shifted = sem("shifted")
        normed = sem("normed")
        norm_hi = sem("norm_hi")
        norm_split = sem("norm_split")
        act_hi = sem("act_hi")
        act_split = sem("act_split")
        logits = sem("logits")
        relu_done = sem("relu_done")
        idx_summed = sem("idx_summed")
        scored = sem("scored")
        maxed = sem("maxed")
        exped = sem("exped")
        turned = sem("turned")
        copied = sem("copied")
        weighed = sem("weighed")
        y_done = sem("y_done")
        yT_done = sem("yT_done")
        yT_out = sem("yT_out")
        f1_done = sem("f1_done")
        f1_out = sem("f1_out")
        f2_done = sem("f2_done")
        f2_hi = sem("f2_hi")
        decayed = sem("decayed")
        d_ready = sem("d_ready")
        rs_done = sem("rs_done")
        rs_out = sem("rs_out")
        ry_done = sem("ry_done")
        ry_out = sem("ry_out")
        rc_done = sem("rc_done")
        rmean = sem("rmean")
        rcent = sem("rcent")
        rstd = sem("rstd")
        rhi = sem("rhi")
        rgn = sem("rgn")
        dve_step = sem("dve_step")
        act_step = sem("act_step")
        pool_step = sem("pool_step")
        stored = sem("stored")
        passed = sem("passed")

        def flat(t, k, lo=None, n=None):
            v = t[:, bass.ds(k, 1), :] if lo is None else t[:, bass.ds(k, 1), lo:lo + n]
            return v.rearrange("p a t -> p (a t)")

        MIX_CHUNK = [3 * (u // 4) + u % 4 if u % 4 < 3 else None for u in range(NU)]
        assert max(c for c in MIX_CHUNK if c is not None) == MIXG - 1

        def score_slot(u):
            return ps[:, 2, :] if u % 2 else ps[:, 0:2, :].rearrange("p a t -> p (a t)")

        def unit_width(u):
            qt, segs, _, _ = UNITS[u]
            return len(segs) * P * (qt + 1)

        hybrid = {}
        m = d = a = 0
        for name, n, kind in (("qk", QK, "d"), ("vn", VN, "d"), ("gate", GATE, "a"), ("mixg", MIXG, "a"),
                              ("br", BR, "d"), ("out", OUT, "d")):
            hybrid[name] = (m, d, a, n)
            m, d, a = m + n, d + (n if kind == "d" else 0), a + (n if kind == "a" else 0)
        later = {}
        m, d, a = LAYERS * m, LAYERS * d, LAYERS * a
        for name, n, kind in (("up0", 44, "d"), ("down0", 32, "d"), ("four", 8, "d"), ("up1", 44, "d"),
                              ("down1", 32, "d"), ("up2", 44, "d"), ("down2", 32, "d"), ("rq", 8, "d"),
                              ("rk", 8, "d"), ("rv", 16, "d"), ("rg", 16, "a"), ("ro", 16, "d"),
                              ("up3", 44, "d"), ("down3", 32, "d")):
            later[name] = (m, d, a, n)
            m, d, a = m + n, d + (n if kind == "d" else 0), a + (n if kind == "a" else 0)

        def xk(k, halves):
            return x[:, 0:halves, bass.ds(k, 1), :].rearrange("p a k t -> p a (k t)")

        def both(ap, halves):
            return ap.rearrange("p (a t) -> p a t", a=halves)

        SOME = (0, 2)
        RIDERS = {"qk": (0, SOME), "vn": (QK // 2, SOME), "mixg": ((QK + VN) // 2, SOME)}
        ADA_L = (QK + VN + MIXG) // 2
        ADA_H = LAYERS * ADA_L
        ADA_FFNS = 3
        ADA_AFTER = 1
        ADA_F = (KT - ADA_AFTER) * RING
        assert ADA_H + ADA_FFNS * ADA_F == LAYERS * ADA

        def of_layer(name, L):
            m, d, a, n = hybrid[name]
            return m + L * PER_LAYER, d + L * PER_D, a + L * PER_A, n

        def col(name, k):
            return cols[:, bass.ds(COLS[name][0] + k, 1)]

        def mod_gain(lj):
            return lambda k, q: gain[:, lj, bass.ds(k, 1), q]

        def mod_shift(l, row):
            return lambda k, q: mod[:, bass.ds(l * ADA + row * KT + k, 1), q]

        block = ctx.enter_context(nc.Block())

        @block.sync
        def _(e):
            xT = xT_d.rearrange("(k p) t -> p k t", p=P)
            e.dma_start(x[:, 0, :, :], xT[:, :, 0:T]).then_inc(x_in, 16)
            e.dma_start(cb[:, :, :], cond_d).then_inc(cond_in, 16)
            for dst, src in ((cols[:, :], cols_d),
                             (ident[:, :], ident_d), (identb[:, :], identb_d), (mask[:, :], mask_d),
                             (rope[:, :, :], rope_d.rearrange("p (a t) -> p a t", a=2))):
                e.dma_start(dst, src).then_inc(consts_in, 16)

            def load(m0, n, widths, src, first, ada0=0, riders=()):
                with e.Fori(0, n // RING) as i:
                    for j in range(RING):
                        e.wait_ge(lo_done, m0 + RING * i + j + 1)
                        at_ = sum(widths[0:j]) if widths is WD else 0
                        row = i if widths is WD else RING * i + j
                        e.dma_start(raw[:, j, 0:widths[j]],
                                    src[bass.ds(first + row, 1), :, at_:at_ + widths[j]].rearrange("a p n -> p (a n)"))\
                            .then_inc(landed[j], 16)
                        if j in riders:
                            q = riders.index(j)
                            r = ada0 + len(riders) * i + q
                            e.wait_ge(ada_done, r + 1)
                            e.dma_start(ada[:, q % 2, :], ada_d[bass.ds(r, 1)].rearrange("a p n -> p (a n)"))\
                                .then_inc(ada_landed[q % 2], 16)

            with e.Fori(0, LAYERS) as L:
                per = PER_LAYER - VN
                m0, w0, r0 = of_layer("qk", L)[0], per * L, ADA_L * L
                load(m0, RING, W8, w1_d, w0)
                load(m0 + RING, QK - RING, W8, w1_d, w0 + RING, r0, SOME)
                load(m0 + QK, VN, WV, wv_d, VN * L, r0 + QK // 2 - 2, SOME)
                m0, w0, r0 = m0 + QK + VN, w0 + QK, r0 + (QK + VN) // 2
                load(m0, RING, W8, w1_d, w0, r0 - 2, SOME)
                load(m0 + RING, GATE, W8, w1_d, w0 + RING)
                m0, w0 = m0 + GATE + RING, w0 + GATE + RING
                load(m0, MIXG, W8, w1_d, w0, r0, SOME)
                load(m0 + MIXG, BR - RING + OUT, W8, w1_d, w0 + MIXG)
            e.wait_ge(ada_done, 2 + ADA_H)
            e.dma_start(x[:, 1, :, :], xT[:, :, T:2 * T]).then_inc(context_in, 16)

            def ffn(f):
                load(later[f"up{f}"][0], 2 * FT, W8, wu_d, 2 * FT * f)
                m0 = later[f"down{f}"][0]
                if f >= ADA_FFNS:
                    load(m0, RING * KT, WD, wd_d, KT * f)
                    return
                load(m0, RING * ADA_AFTER, WD, wd_d, KT * f)
                e.wait_ge(chunk_done, 1 + m0)
                e.dma_start(cb2[:, :, :], cond_d).then_inc(cond_in, 16)
                with e.Fori(0, KT - ADA_AFTER) as i:
                    for j in range(RING):
                        e.wait_ge(lo_done, m0 + RING * (ADA_AFTER + i) + j + 1)
                        at_ = sum(WD[0:j])
                        e.dma_start(raw[:, j, 0:WD[j]],
                                    wd_d[bass.ds(KT * f + ADA_AFTER + i, 1), :, at_:at_ + WD[j]]
                                    .rearrange("a p n -> p (a n)")).then_inc(landed[j], 16)
                        r = ADA_F * f + RING * i + j
                        e.wait_ge(ada2_done, r + 1)
                        e.dma_start(ada2[:, j, :], ada_d[bass.ds(ADA_H + r, 1)].rearrange("a p n -> p (a n)"))\
                            .then_inc(ada2_landed[j], 16)

            ffn(0)
            e.wait_ge(chunk_done, 1 + later["down0"][0] + RING * KT)
            e.dma_start(dft[:, :, :], dft_d[:, 0:4 * T].rearrange("p (a t) -> p a t", a=2)).then_inc(tables_in, 16)
            e.dma_start(dftn[:, :, :, :], dft_d[:, 4 * T:8 * T].rearrange("p (a b t) -> p a b t", a=TT, b=2))\
                .then_inc(tables_in, 16)
            load(later["four"][0], KT, W8, w2_d, 0)
            ffn(1)
            ffn(2)
            e.wait_ge(chunk_done, 1 + later["down2"][0] + RING * KT)
            e.dma_start(dist[:, :, :, :], dist_d.rearrange("p (a b t) -> p a b t", a=2, b=4)).then_inc(ret_tables_in, 16)
            e.dma_start(dmask[:, :, :, :], dmask_d.rearrange("p (a b t) -> p a b t", a=2, b=2)).then_inc(ret_tables_in, 16)
            e.dma_start(rope2[:, :, :], rope2_d.rearrange("p (a t) -> p a t", a=2)).then_inc(ret_tables_in, 16)
            load(later["rq"][0], 64, W8, w2_d, KT)
            ffn(3)
            e.wait_ge(normed, 4 + 3 * KT)
            e.dma_start(out_d.rearrange("(k p) t -> p k t", p=P), hf[:, :, 0:T]).then_inc(stored, 16)
            e.wait_ge(stored, 16)

        @block.scalar
        def _(e):
            n_sq, n_scaled, n_shifted = Tally(), Tally(), Tally()

            def split(lap, mm, c, width):
                e.wait_ge(landed[c % RING], 16 * lap + 16)
                if not (isinstance(mm, int) and mm < RING):
                    e.wait_ge(chunk_done, 1 + mm - RING + 1)
                e.activation(wh[:, c % RING, 0:width], raw[:, c % RING, 0:width], ACT.Copy).then_inc(hi_done, 1)

            def phase(base, widths, after, empty=None, n_own=()):
                m0, _, _, n = base
                lap0 = hybrid_lap(m0)

                def turn(i, nxt):
                    for j in range(RING):
                        c = j + AHEAD
                        w = widths[c] if c < RING else nxt and nxt[c % RING]
                        if w:
                            split(lap0 + i + c // RING, m0 + RING * i + c, c, w)
                        if empty:
                            empty(i, j)

                whole = n // RING - (after != widths)
                if whole:
                    with turns(e, whole, *n_own) as i:
                        turn(i, widths)
                if after != widths:
                    turn(whole, after)

            def hybrid_lap(m0):
                return m0 // RING if isinstance(m0, int) else lap_of[0]

            lap_of = [None]

            def norm(cols_n, shift, dest, has_split):
                e.wait_ge(sq_summed, n_sq())
                e.activation(rs[:, 0:cols_n], ps[:, 7, 0:cols_n], ACT.Sqrt, bias=eps[:, :], scale=1.0 / D)\
                    .then_inc(std_done, 1)
                if has_split and shift:
                    with turns(e, KT // 4, (n_scaled, 4), (n_shifted, 4)) as i:
                        for pair in ((0, 1), (2, 3)):
                            for j in pair:
                                e.wait_ge(scaled, n_scaled())
                                for q in range(cols_n // T):
                                    part = nb[:, j, T * q:T * q + T]
                                    last = e.activation(part, part, ACT.Identity, bias=shift(4 * i + j, q))
                                last.then_inc(shifted, 1)
                            for j in pair:
                                e.wait_ge(shifted, n_shifted())
                                e.activation(flat(hh, 4 * i + j, 0, cols_n), nb[:, j, 0:cols_n], ACT.Copy)\
                                    .then_inc(norm_hi, 1)
                    return
                with turns(e, KT // 4, (n_scaled, 4)) as i:
                    for j in range(4):
                        e.wait_ge(scaled, n_scaled())
                        for q in range(cols_n // T):
                            src, out = nb[:, j, T * q:T * q + T], dest(4 * i + j, q)
                            if shift is None:
                                last = e.activation(out, src, ACT.Copy)
                            else:
                                last = e.activation(out, src, ACT.Identity, bias=shift(4 * i + j, q))
                        last.then_inc(norm_hi if has_split else normed, 1)

            def to_hh(k, q):
                return flat(hh, k, T * q, T)

            e.wait_ge(eps_set, 2)
            e.wait_ge(cond_in, 16)
            e.activation(cb[:, :, :], cb[:, :, :], ACT.Silu).then_inc(c_silu, 1)
            e.activation(spare[:, 5:6], eps[:, :], ACT.Copy).then_inc(emptied_a, 4)
            e.wait_ge(consts_in, 80)
            for c in range(AHEAD):
                split(0, c, c, CW)

            n_relu, n_exp, n_copy = Tally(), Tally(), Tally()
            per = (n_sq, 1), (n_scaled, KT), (n_relu, TT), (n_exp, NU), (n_copy, NU)
            with turns(e, LAYERS, *per) as L:
                def laps(name):
                    lap_of[0] = hybrid[name][0] // RING + L * (PER_LAYER // RING)
                    return of_layer(name, L)

                norm(T, None, to_hh, True)
                phase(laps("qk"), W8, WV)

                m0 = laps("vn")[0]
                for c in range(AHEAD, VN + AHEAD):
                    split(lap_of[0] + c // RING, m0 + c, c, WV[0] if c < VN else CW)
                    if c == 2 * AHEAD:
                        e.wait_ge(emptied_d, 4 + of_layer("qk", L)[1] + QK)
                        for jq in range(4):
                            for r in range(2):
                                dst = 64 * (jq % 2) + 32 * r
                                e.dma_start(heads[dst:dst + 32, jq // 2:NPOS // 2:2, :],
                                            rot[32 * jq:32 * jq + 32, r::2, :]).then_inc(heads_in, 16)
                        for jq, half in ((2, 1), (3, 0)):
                            for r in range(2):
                                dst = 64 * half + 32 * r
                                e.dma_start(heads[dst:dst + 32, NPOS // 2, :],
                                            rot[32 * jq:32 * jq + 32, QK - 2 + r, :]).then_inc(heads_in, 16)

                for qt in range(TT):
                    w = P * (qt + 1)
                    e.wait_ge(logits, n_relu())
                    if qt:
                        e.wait_ge(idx_summed, n_relu.now - 1)
                    bank = 6 - 2 * qt
                    e.activation(relu[:, :, 0:2 * w], ps[:, bank:bank + 2, 0:2 * w], ACT.Relu)\
                        .then_inc(relu_done, 1)

                def silu_gate(i, j):
                    e.wait_ge(chunk_done, 1 + of_layer("gate", L)[0] + RING * i + j + 1)
                    e.activation(flat(sg, RING * i + j, T, T), ps[:, j, 0:T], ACT.Silu).then_inc(emptied_a, 1)

                phase(laps("gate"), W8, W8, silu_gate)

                def exp(u):
                    w = unit_width(u)
                    e.wait_ge(maxed, n_exp())
                    if u >= 2:
                        e.wait_ge(turned, n_exp.now - 2)
                    e.activation(prob[u % 2][:, 0:w], score_slot(u)[:, 0:w], ACT.Exp, bias=nmax[:, u:u + 1],
                                 scale=HD ** -0.5, accum_out=rsum[:, u:u + 1]).then_inc(exped, 1)

                m0 = laps("mixg")[0]
                exp(0)
                for u in range(NU):
                    c = MIX_CHUNK[u]
                    if c is not None:
                        split(lap_of[0] + (c + AHEAD) // RING, m0 + c + AHEAD, c + AHEAD, CW)
                    if u + 1 < NU:
                        exp(u + 1)
                    if c is not None:
                        e.wait_ge(chunk_done, 1 + m0 + c + 1)
                        e.activation(mg[:, c, :], ps[:, 6 + c % 2, 0:T], ACT.Exp, scale=-1.0).then_inc(emptied_a, 1)
                    w = unit_width(u)
                    e.wait_ge(turned, n_copy())
                    if u >= 2:
                        e.wait_ge(weighed, n_copy.now - 2)
                    e.activation(probT[u % 2][:, 0:w], ps[:, 3:5, :].rearrange("p a t -> p (a t)")[:, 0:w],
                                 ACT.Copy).then_inc(copied, 1)

                phase(laps("br"), W8, W8)
                phase(laps("out"), W8, W8)

            norm(T, None, lambda k, q: xk(k, 1)[:, 0, :], False)

            def ffn(f, l, jn, halves, width_after):
                norm(halves * T, mod_shift(l, 3 * jn), to_hh, True)
                base = later[f"up{f}"]

                def silu(i, j):
                    if j % 2 == 0:
                        return
                    e.wait_ge(chunk_done, 1 + base[0] + RING * i + j)
                    e.wait_ge(emptied_d, 4 + base[1] + RING * i + j - 1 - 2)
                    e.activation(tn[:, j // 2, 0:halves * T], ps[:, j - 1, 0:halves * T], ACT.Silu)\
                        .then_inc(act_step, 1)

                phase(base, W8, WD, silu)
                if f < ADA_FFNS:
                    e.wait_ge(cond_in, 16 * f + 32)
                    e.activation(cb2[:, :, :], cb2[:, :, :], ACT.Silu).then_inc(c_silu, 1)
                phase(later[f"down{f}"], WD, width_after)

            e.wait_ge(mod_ready, 2)
            ffn(0, 0, 0, 2, W8)
            norm(2 * T, mod_shift(0, 3), lambda k, q: flat(hf, k, T * q, T), False)
            phase(later["four"], W8, W8)
            e.wait_ge(mod_ready, 3)
            ffn(1, 0, 2, 2, W8)
            e.wait_ge(mod_ready, 4)
            ffn(2, 1, 0, 2, W8)

            e.wait_ge(mod_ready, 5)
            norm(2 * T, mod_shift(1, 3), to_hh, True)
            phase(later["rq"], W8, W8)
            phase(later["rk"], W8, W8)
            phase(later["rv"], W8, W8)

            def silu_ret(i, j):
                e.wait_ge(chunk_done, 1 + later["rg"][0] + RING * i + j + 1)
                e.activation(flat(sgr, RING * i + j), ps[:, j, 0:T], ACT.Silu).then_inc(emptied_a, 1)

            phase(later["rg"], W8, W8, silu_ret)
            e.wait_ge(ret_tables_in, 48)

            def decays(h):
                if h:
                    e.wait_ge(rs_out, 4 * h)
                for b in range(2):
                    e.activation(dec[:, b, :, :], dist[:, b, :, :], ACT.Exp,
                                 scale=lg[:, RH * b + h:RH * b + h + 1]).then_inc(decayed, 1)

            decays(0)
            for h in range(RH):
                if h + 1 < RH:
                    decays(h + 1)
                e.wait_ge(rc_done, 4 * h + 4)
                e.activation(rs[:, 0:T], ps[:, 7, 0:T], ACT.Sqrt, bias=eps[:, :], scale=1.0 / RDV)\
                    .then_inc(rstd, 1)
            phase(later["ro"], W8, W8)
            ffn(3, 1, 2, 1, None)
            norm(T, None, lambda k, q: flat(hf, k, 0, T), False)

        @block.gpsimd
        def _(e):
            n_hi, n_nhi = Tally(), Tally()
            e.memset(eps[:, :], EPS).then_inc(eps_set, 1)
            e.memset(ones[:, :], 1.0).then_inc(eps_set, 1)
            e.memset(spare[:, 0:1], 0.0).then_inc(lo_done, RING)
            e.memset(spare[:, 1:2], 0.0).then_inc(norm_split, 4)
            e.memset(top8[:, :], 0.0).then_inc(normed, 4)
            e.memset(spare[:, 6:7], 0.0).then_inc(ada_done, 2)
            e.memset(lg[:, :], 0.0).then_inc(ada2_done, RING)
            e.memset(spare[:, 7:8], 0.0).then_inc(chunk_done, 1)

            def split(mm, c, width):
                e.wait_ge(hi_done, mm + 1)
                e.tensor_tensor(wl[:, c % RING, 0:width], raw[:, c % RING, 0:width],
                                wh[:, c % RING, 0:width].bitcast(F32), ALU.subtract).then_inc(lo_done, 1)

            def phase(base, widths, after, extra=None, n_own=()):
                m0, n = base[0], base[3]

                def turn(i, nxt):
                    for j in range(RING):
                        c = j + AHEAD
                        w = widths[c] if c < RING else nxt and nxt[c % RING]
                        if w:
                            split(m0 + RING * i + c, c, w)
                        if extra:
                            extra(i, j)

                whole = n // RING - (after != widths)
                if whole:
                    with turns(e, whole, *n_own) as i:
                        turn(i, widths)
                if after != widths:
                    turn(whole, after)

            def norm_low(cols_n):
                with turns(e, KT // 4, (n_nhi, 4)) as i:
                    for j in range(4):
                        e.wait_ge(norm_hi, n_nhi())
                        e.tensor_tensor(flat(hl, 4 * i + j, 0, cols_n), nb[:, j, 0:cols_n],
                                        flat(hh, 4 * i + j, 0, cols_n).bitcast(F32), ALU.subtract)\
                            .then_inc(norm_split, 1)

            def gated_low():
                with turns(e, KT // 2, (n_nhi, 2)) as i:
                    for j in range(2):
                        e.wait_ge(norm_hi, n_nhi())
                        e.tensor_tensor(flat(hl, 2 * i + j, T, T), hn[:, j, 0:T],
                                        flat(hh, 2 * i + j, T, T).bitcast(F32), ALU.subtract)\
                            .then_inc(norm_split, 1)

            for c in range(AHEAD):
                split(c, c, CW)
            with turns(e, LAYERS, (n_nhi, 3 * KT)) as L:
                norm_low(T)
                phase(of_layer("qk", L), W8, WV)
                phase(of_layer("vn", L), WV, W8)
                phase(of_layer("gate", L), W8, W8)
                phase(of_layer("mixg", L), W8, W8)
                gated_low()

                def merged_low(i, j):
                    e.wait_ge(norm_hi, n_nhi())
                    e.tensor_tensor(flat(hl, RING * i + j, 0, T), hn[:, j % 2, 0:T],
                                    flat(hh, RING * i + j, 0, T).bitcast(F32), ALU.subtract)\
                        .then_inc(norm_split, 1)

                phase(of_layer("br", L), W8, W8, merged_low, ((n_nhi, RING),))
                phase(of_layer("out", L), W8, W8)

            n_act = Tally()

            def ffn(f, halves, after):
                norm_low(halves * T)

                def act_low(i, j):
                    if j % 2 == 0:
                        return
                    e.wait_ge(act_hi, n_act())
                    e.tensor_tensor(flat(al, 2 * i + j // 2, 0, halves * T), hn[:, j // 2, 0:halves * T],
                                    flat(ah, 2 * i + j // 2, 0, halves * T).bitcast(F32), ALU.subtract)\
                        .then_inc(act_split, 1)

                phase(later[f"up{f}"], W8, WD, act_low, ((n_act, 2),))
                phase(later[f"down{f}"], WD, after)

            ffn(0, 2, W8)
            phase(later["four"], W8, W8)
            ffn(1, 2, W8)
            ffn(2, 2, W8)
            norm_low(2 * T)
            for name in ("rq", "rk", "rv", "rg"):
                phase(later[name], W8, W8)
            for f in range(4 * RH):
                e.wait_ge(rhi, f + 1)
                here = slice(T * (f % 2), T * (f % 2) + T)
                e.tensor_tensor(hl[:, f // 2, here], yr[:, f % 4, :], hh[:, f // 2, here].bitcast(F32), ALU.subtract)\
                    .then_inc(rgn, 1)
            phase(later["ro"], W8, W8)
            ffn(3, 1, None)

        @block.vector
        def _(e):
            step = Tally()
            n_std, n_normed, n_nsplit = Tally(), Tally(), Tally()

            def norm(cols_n, split, gain_of):
                e.wait_ge(std_done, n_std())
                e.reciprocal(rs[:, 0:cols_n], rs[:, 0:cols_n]).then_inc(dve_step, 1)
                e.wait_ge(dve_step, step())
                e.sem_inc(passed, 1)
                freed, n_freed = (norm_split, n_nsplit) if split else (normed, n_normed)
                with turns(e, KT // 4, (n_freed, 4)) as i:
                    for j in range(4):
                        e.wait_ge(freed, n_freed())
                        for q in range(cols_n // T):
                            last = e.scalar_tensor_tensor(out=nb[:, j, T * q:T * q + T],
                                                          in0=xk(4 * i + j, 2)[:, q, :], scalar=gain_of(4 * i + j, q),
                                                          in1=rs[:, T * q:T * q + T], op0=ALU.mult, op1=ALU.mult)
                        last.then_inc(scaled, 1)

            def no_squares(w):
                e.memset(sq[:, 0, 0:w], 0.0).then_inc(dve_step, 1)
                own(1)

            def add_squares(k, halves):
                e.tensor_tensor(both(sq[:, 1, 0:halves * T], halves), xk(k, halves), xk(k, halves), ALU.mult)\
                    .then_inc(dve_step, 1)
                own(1)
                e.tensor_tensor(sq[:, 0, 0:halves * T], sq[:, 0, 0:halves * T], sq[:, 1, 0:halves * T], ALU.add)\
                    .then_inc(dve_step, 1)
                own(1)

            def own(k):
                e.wait_ge(dve_step, step(k))

            e.memset(spare[:, 2:3], 0.0).then_inc(emptied_d, 4)
            e.memset(spare[:, 3:4], 0.0).then_inc(act_split, 2)
            e.wait_ge(x_in, 16)
            no_squares(T)
            for k in range(KT):
                add_squares(k, 1)
            e.sem_inc(sq_done, 1)
            e.wait_ge(consts_in, 80)

            def rotate(ps1, ps2, cs, sn, out1, out2, ready, count):
                e.tensor_tensor(tn[:, 0, 0:T], ps1, cs, ALU.mult).then_inc(dve_step, 1)
                e.tensor_tensor(tn[:, 0, T:2 * T], ps2, sn, ALU.mult).then_inc(dve_step, 1)
                e.tensor_tensor(tn[:, 1, 0:T], ps1, sn, ALU.mult).then_inc(dve_step, 1)
                e.tensor_tensor(tn[:, 1, T:2 * T], ps2, cs, ALU.mult).then_inc(dve_step, 1)
                own(4)
                e.tensor_tensor(out1, tn[:, 0, 0:T], tn[:, 0, T:2 * T], ALU.subtract).then_inc(dve_step, 1)
                own(1)
                e.tensor_tensor(out2, tn[:, 1, 0:T], tn[:, 1, T:2 * T], ALU.add).then_inc(ready, count)

            def modulate(name, i, j):
                ada0, riders = RIDERS[name]
                if j not in riders:
                    return
                slot = riders.index(j) % 2
                r = layer[0] * ADA_L + ada0 + len(riders) * i + riders.index(j)
                lap = layer[0] * (ADA_L // 2) + ada0 // 2 + i * (len(riders) // 2) + riders.index(j) // 2
                e.wait_ge(ada_landed[slot], 16 * lap + 16)
                for q in range(2):
                    last = e.scalar_tensor_tensor(out=ada_prod[:, :], in0=ada[:, slot, :], scalar=1.0, in1=cb[:, q, :],
                                                  op0=ALU.mult, op1=ALU.mult,
                                                  accum_out=mod[:, bass.ds(r, 1), q])
                    last.then_inc(ada_step, 1) if q == 0 else last.then_inc(ada_done, 1)
                    if q == 0:
                        e.wait_ge(ada_step, r + 1)
                e.wait_ge(ada_done, r + 3)

            def modulate2(f, o):
                for q in range(RING):
                    r = ADA_F * f + RING * (o - ADA_AFTER) + q
                    e.wait_ge(ada2_landed[q], 16 * (ADA_F // RING * f + o - ADA_AFTER) + 16)
                    for c, done in ((0, ada_step), (1, ada2_done)):
                        e.scalar_tensor_tensor(out=ps[:, 4:6, :].rearrange("p a t -> p (a t)"), in0=ada2[:, q, :],
                                               scalar=1.0, in1=cb2[:, c, :], op0=ALU.mult, op1=ALU.mult,
                                               accum_out=mod[:, bass.ds(ADA_H + r, 1), c]).then_inc(done, 1)
                        e.wait_ge(done, ADA_H + r + 1 if c == 0 else RING + r + 1)

            def gains(l, norms):
                ab, g0 = COLS["ada_b"][0] + ADA * l, COLS["norm_g_2"][0]
                lo, hi = 3 * KT * norms[0], 3 * KT * (norms[-1] + 1)
                for q in range(2):
                    sums = mod[:, ADA * l + lo:ADA * l + hi, q]
                    e.tensor_tensor(sums, sums, cols[:, ab + lo:ab + hi], ALU.add).then_inc(dve_step, 1)
                own(2)
                for jn in norms:
                    for q in range(2):
                        k0 = g0 + (3 * l + jn) * KT
                        c0 = ADA * l + 3 * jn * KT
                        e.scalar_tensor_tensor(out=gain[:, 3 * l + jn, :, q], scalar=1.0,
                                               in0=mod[:, c0 + KT:c0 + 2 * KT, q],
                                               in1=cols[:, k0:k0 + KT], op0=ALU.add, op1=ALU.mult)\
                            .then_inc(dve_step, 1)
                        e.tensor_scalar(gate[:, 3 * l + jn, :, q], mod[:, c0 + 2 * KT:c0 + 3 * KT, q],
                                        1.0 if jn == 1 else 0.5, None, ALU.mult).then_inc(dve_step, 1)
                own(4 * len(norms))
                e.sem_inc(mod_ready, 1)

            layer = [None]
            e.wait_ge(c_silu, 1)

            n_relu, n_scored, n_weighed, n_yT = Tally(), Tally(), Tally(), Tally()
            idx_steps = TT * (3 + 1 + 2 * (TOPK // 8) + 2)
            STEPS_L = 1 + 5 * (QK // 2) + VG + 1 + idx_steps + 2 * NU + MIXG + KT + 4 * BR + 1 + 2 * OUT
            per = ((step, STEPS_L), (n_std, 1), (n_nsplit, 3 * KT),
                   (n_relu, TT), (n_scored, NU), (n_weighed, NU), (n_yT, KT))
            with turns(e, LAYERS, *per) as L:
                layer[0] = L
                norm(T, True, lambda k, q: col("norm_g", L * KT + k))
                m0, d0, _, _ = of_layer("qk", L)
                with turns(e, QK // RING, (step, 10)) as i:
                    for j in (0, 2):
                        e.wait_ge(chunk_done, 1 + m0 + RING * i + j + 2)
                        e.wait_ge(emptied_d, 4 + d0 + RING * i + j)
                        rotate(ps[:, j, 0:T], ps[:, j + 1, 0:T], rope[:, 0, :], rope[:, 1, :],
                               flat(rot, RING * i + j), flat(rot, RING * i + j + 1), emptied_d, 2)
                        modulate("qk", i, j)
                m0, d0, _, _ = of_layer("vn", L)
                for g in range(VG):
                    for j in SOME:
                        modulate("vn", g, j)
                    e.wait_ge(chunk_done, 1 + m0 + 4 * g + 4)
                    for tt in range(TT):
                        last = e.tensor_copy(vn[:, tt, VW * g:VW * g + VW], ps[:, 4 + 2 * (g % 2) + tt, 0:VW])
                        if tt == 0:
                            last.then_inc(dve_step, 1)
                            step()
                    last.then_inc(emptied_d, 4)
                e.wait_ge(emptied_d, 4 + d0 + VN)
                e.tensor_scalar(iw[:, :, :], vn[:, :, 1216:1220], 1.0 / 16, None, ALU.mult).then_inc(dve_step, 1)
                own(1)

                for qt in range(TT):
                    w = P * (qt + 1)
                    acc = idx[:, qt, 0:w]
                    e.wait_ge(relu_done, n_relu())
                    e.tensor_scalar(acc, relu[:, 0, 0:w], iw[:, qt, 0:1], None, ALU.mult).then_inc(dve_step, 1)
                    own(1)
                    for h in range(1, 4):
                        last = e.scalar_tensor_tensor(out=acc, in0=relu[:, h % 2, w * (h // 2):w * (h // 2) + w], scalar=iw[:, qt, h:h + 1],
                                                      in1=acc, op0=ALU.mult, op1=ALU.add)
                        if h < 3:
                            last.then_inc(dve_step, 1)
                            own(1)
                    last.then_inc(idx_summed, 1)
                    e.wait_ge(idx_summed, n_relu.now)
                    tri = mask[:, 0:P]
                    e.tensor_tensor(idx[:, qt, w - P:w], idx[:, qt, w - P:w], tri, ALU.add).then_inc(dve_step, 1)
                    own(1)
                    for n in range(TOPK // 8):
                        e.sem_inc(passed, 1)
                        e.max(top8[:, :], acc).then_inc(dve_step, 1)
                        own(1)
                        e.sem_inc(passed, 1)
                        e.match_replace(acc, top8[:, :], acc, TAKEN).then_inc(dve_step, 1)
                        own(1)
                    pk = picked[:, P * qt:P * qt + w]
                    e.tensor_scalar(pk, acc, TAKEN / 2, NEG, ALU.is_gt, ALU.mult).then_inc(dve_step, 1)
                    own(1)
                    e.tensor_tensor(pk[:, w - P:w], pk[:, w - P:w], tri, ALU.add).then_inc(dve_step, 1)
                    own(1)

                def maximum(u):
                    w = unit_width(u)
                    e.wait_ge(scored, n_scored())
                    e.reduce_max(rmax[:, u:u + 1], score_slot(u)[:, 0:w], axis=AX_X).then_inc(dve_step, 1)
                    own(1)
                    e.tensor_scalar(nmax[:, u:u + 1], rmax[:, u:u + 1], -HD ** -0.5, None, ALU.mult)\
                        .then_inc(maxed, 1)

                def finish(u):
                    qt, _, _, yc = UNITS[u]
                    e.wait_ge(weighed, n_weighed())
                    e.reciprocal(rrec[:, u:u + 1], rsum[:, u:u + 1]).then_inc(dve_step, 1)
                    own(1)
                    e.tensor_scalar(y[:, qt, yc:yc + HD], ps[:, 5, 0:HD], rrec[:, u:u + 1], None, ALU.mult)\
                        .then_inc(y_done, 1)

                a0 = of_layer("mixg", L)[2]
                maximum(0)
                for u in range(NU):
                    if u + 1 < NU:
                        maximum(u + 1)
                    if MIX_CHUNK[u] is not None:
                        modulate("mixg", MIX_CHUNK[u] // RING, MIX_CHUNK[u] % RING)
                    if u:
                        c = MIX_CHUNK[u - 1]
                        if c is not None:
                            e.wait_ge(emptied_a, 4 + a0 + c + 1)
                            e.tensor_scalar(mg[:, c, :], mg[:, c, :], 1.0, None, ALU.add).then_inc(dve_step, 1)
                            own(1)
                            e.reciprocal(mg[:, c, :], mg[:, c, :])
                        finish(u - 1)
                finish(NU - 1)

                for f in range(KT):
                    e.wait_ge(yT_done, n_yT())
                    e.wait_ge(norm_split, n_nsplit.now + f + 3)
                    e.tensor_tensor(hn[:, f % 2, 0:T], ps[:, f % 4, 0:T], sg[:, f, T:2 * T], ALU.mult).then_inc(dve_step, 1)
                    own(1)
                    e.tensor_copy(hh[:, f, T:2 * T], hn[:, f % 2, 0:T]).then_inc(norm_hi, 1)
                n_nsplit(KT)

                m0, d0, _, _ = of_layer("br", L)
                with turns(e, BR // RING, (step, 4 * RING), (n_nsplit, RING)) as i:
                    for j in range(RING):
                        bank = 4 - 4 * (j % 2)
                        e.wait_ge(chunk_done, 1 + m0 + RING * i + j + 1)
                        for b in range(3):
                            last = e.tensor_tensor(tn[:, b // 2, T * (b % 2):T * (b % 2) + T], ps[:, bank + b, 0:T],
                                                   flat(mg, b * KT + RING * i + j), ALU.mult)
                            last.then_inc(dve_step, 1) if b < 2 else last.then_inc(emptied_d, 1)
                        own(2)
                        e.tensor_tensor(tn[:, 0, 0:T], tn[:, 0, 0:T], tn[:, 0, T:2 * T], ALU.add).then_inc(dve_step, 1)
                        e.wait_ge(emptied_d, 4 + d0 + RING * i + j + 1)
                        own(1)
                        e.wait_ge(norm_split, n_nsplit() + 2)
                        e.tensor_tensor(hn[:, j % 2, 0:T], tn[:, 0, 0:T], tn[:, 1, 0:T], ALU.add).then_inc(dve_step, 1)
                        own(1)
                        e.tensor_copy(flat(hh, RING * i + j, 0, T), hn[:, j % 2, 0:T]).then_inc(norm_hi, 1)
                m0, d0, _, _ = of_layer("out", L)
                no_squares(T)
                e.sem_inc(passed, 1)
                with turns(e, OUT // RING, (step, 2 * RING)) as i:
                    for j in range(RING):
                        e.wait_ge(chunk_done, 1 + m0 + RING * i + j + 1)
                        xs = xk(RING * i + j, 1)[:, 0, :]
                        e.tensor_tensor(xs, ps[:, j, 0:T], xs, ALU.add).then_inc(emptied_d, 1)
                        e.wait_ge(emptied_d, 4 + d0 + RING * i + j + 1)
                        add_squares(RING * i + j, 1)
                e.sem_inc(sq_done, 1)

            gains(0, (0, 1))
            dc = COLS["decay"][0]
            e.scalar_tensor_tensor(out=lg[:, :], in0=cols[:, dc:dc + 8], scalar=-1.0, in1=cols[:, dc:dc + 8],
                                   op0=ALU.mult, op1=ALU.min).then_inc(mod_ready, 1)

            norm(T, False, lambda k, q: col("final_norm_g", k))
            e.wait_ge(context_in, 16)
            no_squares(2 * T)
            for k in range(KT):
                e.wait_ge(normed, 4 + k + 1)
                add_squares(k, 2)
            e.sem_inc(sq_done, 1)

            n_act = Tally()

            def ffn(f, l, jn, halves, *next_gains):
                norm(halves * T, True, mod_gain(3 * l + jn))
                w = halves * T
                STEPS_TILE = halves - 1 + 2
                m0, d0, _, _ = later[f"up{f}"]
                with turns(e, 2 * FT // RING, (n_act, 2)) as i:
                    for j in (0, 1):
                        e.wait_ge(chunk_done, 1 + m0 + RING * i + 2 * j + 2)
                        e.wait_ge(act_step, n_act())
                        e.wait_ge(act_split, n_act.now)
                        e.tensor_tensor(hn[:, j, 0:w], tn[:, j, 0:w], ps[:, 2 * j + 1, 0:w], ALU.mult)\
                            .then_inc(emptied_d, 2)
                        e.wait_ge(emptied_d, 4 + d0 + RING * i + 2 * j + 2)
                        e.tensor_copy(flat(ah, 2 * i + j, 0, w), hn[:, j, 0:w]).then_inc(act_hi, 1)
                m0, d0, _, _ = later[f"down{f}"]

                def add_tile(o, bank):
                    e.wait_ge(chunk_done, 1 + m0 + RING * o + RING)
                    for q in range(halves):
                        xs = xk(o, 2)[:, q, :]
                        last = e.scalar_tensor_tensor(out=xs, in0=ps[:, bank, T * q:T * q + T],
                                                      scalar=gate[:, 3 * l + jn, bass.ds(o, 1), q], in1=xs,
                                                      op0=ALU.mult, op1=ALU.add)
                        if q < halves - 1:
                            last.then_inc(dve_step, 1)
                            step()
                    last.then_inc(emptied_d, RING)
                    e.wait_ge(emptied_d, 4 + d0 + RING * o + RING)
                    add_squares(o, halves)

                no_squares(w)
                if f < ADA_FFNS:
                    add_tile(0, 0)
                    e.wait_ge(c_silu, f + 2)
                    with turns(e, KT // 2 - 1, (step, 2 * STEPS_TILE)) as i:
                        for j in range(2):
                            modulate2(f, 2 * i + 1 + j)
                            add_tile(2 * i + 1 + j, (1 + j) % 2)
                    modulate2(f, KT - 1)
                    gains(*next_gains)
                    add_tile(KT - 1, 1)
                else:
                    with turns(e, KT // 2, (step, 2 * STEPS_TILE)) as i:
                        for j in range(2):
                            add_tile(2 * i + j, j)
                e.sem_inc(sq_done, 1)

            ffn(0, 0, 0, 2, 0, (2,))

            norm(2 * T, False, mod_gain(1))
            for n in range(16):
                b, r = divmod(n, 8)
                g, tt = divmod(r, 2)
                e.wait_ge(f1_done, n + 1)
                e.tensor_copy(pq[:, b, tt, g, :], ps[:, n % 4, :]).then_inc(f1_out, 1)
            for n in range(16):
                b, f = divmod(n, 8)
                e.wait_ge(f2_done, n + 1)
                dst = hh[:, f, T * b:T * b + T]
                e.tensor_copy(dst, ps[:, 4 + n % 4, 0:T]).then_inc(dve_step, 1)
                own(1)
                e.tensor_tensor(hl[:, f, T * b:T * b + T], ps[:, 4 + n % 4, 0:T], dst.bitcast(F32), ALU.subtract)\
                    .then_inc(f2_hi, 1)
            m0, d0, _, _ = later["four"]
            fb = COLS["four_b"][0]
            no_squares(2 * T)
            with turns(e, KT // RING, (step, 4 * RING)) as i:
                for j in range(RING):
                    o = RING * i + j
                    e.wait_ge(chunk_done, 1 + m0 + RING * i + j + 1)
                    e.wait_ge(emptied_d, 4 + d0 + RING * i + j)
                    for q in range(2):
                        e.tensor_scalar(tn[:, 0, T * q:T * q + T], ps[:, j, T * q:T * q + T],
                                        cols[:, bass.ds(fb + o, 1)], gate[:, 1, bass.ds(o, 1), q], ALU.add, ALU.mult)\
                            .then_inc(dve_step, 1)
                    own(2)
                    xs = xk(o, 2)
                    e.tensor_tensor(xs, xs, both(tn[:, 0, :], 2), ALU.add).then_inc(emptied_d, 1)
                    e.wait_ge(emptied_d, 4 + d0 + RING * i + j + 1)
                    add_squares(o, 2)
            e.sem_inc(sq_done, 1)

            ffn(1, 0, 2, 2, 1, (0,))
            ffn(2, 1, 0, 2, 1, (1, 2))

            norm(2 * T, True, mod_gain(4))
            e.wait_ge(ret_tables_in, 48)
            for name, dst in (("rq", qT), ("rk", kT)):
                m0, d0, _, _ = later[name]
                with turns(e, KT // RING, (step, 14 if name == "rk" else 10)) as i:
                    for j in (0, 2):
                        e.wait_ge(chunk_done, 1 + m0 + RING * i + j + 2)
                        e.wait_ge(emptied_d, 4 + d0 + RING * i + j)
                        if name == "rk":
                            for b in range(2):
                                e.tensor_copy(flat(kT, RING * i + j + b, T, T), ps[:, j + b, T:2 * T])\
                                    .then_inc(dve_step, 1)
                                step()
                        rotate(ps[:, j, 0:T], ps[:, j + 1, 0:T], rope2[:, 0, :], rope2[:, 1, :],
                               flat(dst, RING * i + j, 0, T), flat(dst, RING * i + j + 1, 0, T), emptied_d, 2)
            m0, d0, _, _ = later["rv"]
            for g in range(RH):
                e.wait_ge(chunk_done, 1 + m0 + 4 * g + 4)
                for tt in range(2 * TT):
                    last = e.tensor_copy(vr[:, tt, RDV * g:RDV * g + RDV], ps[:, 4 * (g % 2) + tt, :])
                    if tt < 2 * TT - 1:
                        last.then_inc(dve_step, 1)
                        step()
                last.then_inc(emptied_d, 4)

            def decayed_scores(h):
                e.wait_ge(decayed, 2 * h + 2)
                for b in range(2):
                    e.tensor_tensor(dec[:, b, 0:2, :], dec[:, b, 0:2, :], dmask[:, b, :, :], ALU.mult)\
                        .then_inc(dve_step, 1)
                own(2)
                e.tensor_tensor(dec[:, 0, :, :], dec[:, 0, :, :], dec[:, 1, :, :], ALU.add).then_inc(dve_step, 1)
                own(1)
                for jt in range(4):
                    e.wait_ge(rs_done, 4 * h + jt + 1)
                    e.scalar_tensor_tensor(out=sT[:, jt, :], in0=ps[:, jt % 2, 0:T], scalar=1.0 / 16,
                                           in1=dec[:, 0, jt, :], op0=ALU.mult, op1=ALU.mult).then_inc(rs_out, 1)

            decayed_scores(0)
            for h in range(RH):
                if h:
                    e.wait_ge(rgn, 4 * h)
                for dv in range(4):
                    e.wait_ge(ry_done, 4 * h + dv + 1)
                    e.tensor_copy(yr[:, dv, :], ps[:, 2 + dv, 0:T]).then_inc(ry_out, 1)
                if h + 1 < RH:
                    decayed_scores(h + 1)
                e.wait_ge(rmean, h + 1)
                e.tensor_scalar(sq[:, 0, T:2 * T], ps[:, 6, 0:T], 1.0 / RDV, None, ALU.mult).then_inc(dve_step, 1)
                own(1)
                for dv in range(4):
                    e.tensor_tensor(yr[:, dv, :], yr[:, dv, :], sq[:, 0, T:2 * T], ALU.subtract).then_inc(dve_step, 1)
                own(4)
                for dv in range(4):
                    if h or dv >= 2:
                        e.wait_ge(rc_done, 4 * h + dv - 1)
                    e.tensor_tensor(sq[:, dv % 2, 0:T], yr[:, dv, :], yr[:, dv, :], ALU.mult).then_inc(rcent, 1)
                e.wait_ge(rstd, h + 1)
                e.reciprocal(rs[:, 0:T], rs[:, 0:T]).then_inc(dve_step, 1)
                own(1)
                for dv in range(4):
                    e.tensor_tensor(yr[:, dv, :], yr[:, dv, :], rs[:, 0:T], ALU.mult).then_inc(dve_step, 1)
                own(4)
                for dv in range(4):
                    e.tensor_tensor(yr[:, dv, :], yr[:, dv, :], sgr[:, 4 * h + dv, :], ALU.mult).then_inc(dve_step, 1)
                own(4)
                for dv in range(4):
                    f = 4 * h + dv
                    e.tensor_copy(hh[:, f // 2, T * (f % 2):T * (f % 2) + T], yr[:, dv, :]).then_inc(rhi, 1)
            m0, d0, _, _ = later["ro"]
            no_squares(T)
            with turns(e, KT // 2, (step, 4)) as i:
                for j in range(2):
                    e.wait_ge(chunk_done, 1 + m0 + RING * i + 2 * j + 2)
                    xs = xk(2 * i + j, 1)[:, 0, :]
                    e.scalar_tensor_tensor(out=xs, in0=ps[:, j, 0:T], scalar=gate[:, 4, bass.ds(2 * i + j, 1), 0],
                                           in1=xs, op0=ALU.mult, op1=ALU.add).then_inc(emptied_d, 2)
                    e.wait_ge(emptied_d, 4 + d0 + RING * i + 2 * j + 2)
                    add_squares(2 * i + j, 1)
            e.sem_inc(sq_done, 1)
            ffn(3, 1, 2, 1)
            norm(T, False, lambda k, q: col("final_g_2", k))

        @block.tensor
        def _(e):
            n_sq, n_split = Tally(), Tally()

            def norm(cols_n, split):
                e.wait_ge(sq_done, n_sq())
                e.matmul(ps[:, 7, 0:cols_n], ones[:, :], sq[:, 0, 0:cols_n], start=True, stop=True)\
                    .then_inc(sq_summed, 1)
                if split:
                    n_split(KT)

            def tile_ready(k):
                e.wait_ge(norm_split, n_split.now - KT + k + 5)

            def products(bank, j, tiles, k0, move, lo, n, first, last, ready=None):
                mh, ml = move
                for t in tiles:
                    w = slice(t * P, t * P + P)
                    k = k0 + t
                    if ready:
                        ready(k)
                    hi, low = mh[:, k, lo:lo + n], ml[:, k, lo:lo + n]
                    e.matmul(ps[:, bank, 0:n], wh[:, j, w], hi, start=(first and t == tiles[0]), stop=False)
                    e.matmul(ps[:, bank, 0:n], wh[:, j, w], low, start=False, stop=False)
                    end = e.matmul(ps[:, bank, 0:n], wl[:, j, w], hi, start=False,
                                   stop=(last and t == tiles[-1]))
                return end

            h = (hh, hl)

            def plain(base, cols_n, freed, lo=0, ready=None):
                m0, d0, a0, n = base
                e.sem_inc(passed, 1)
                with e.Fori(0, n // RING) as i:
                    for j in range(RING):
                        e.wait_ge(lo_done, RING + m0 + RING * i + j + 1)
                        f0 = d0 if freed is emptied_d else a0
                        e.wait_ge(freed, f0 + RING * i + j + 1)
                        products(j, j, range(KT), 0, h, lo, cols_n, True, True, None if j else ready)\
                            .then_inc(chunk_done, 1)

            def natural(j, c, width, bank, tts, first, last):
                for tt in range(tts):
                    for t in range(2):
                        tok = slice(P * tt, P * tt + P)
                        w = slice(t * width, t * width + width)
                        k = 2 * c + t
                        out = ps[:, bank + tt, 0:width]
                        e.matmul(out, hh[:, k, tok], wh[:, j, w], start=(first and t == 0), stop=False)
                        e.matmul(out, hh[:, k, tok], wl[:, j, w], start=False, stop=False)
                        end = e.matmul(out, hl[:, k, tok], wh[:, j, w], start=False, stop=(last and t == 1))
                return end

            e.wait_ge(eps_set, 2)

            n_y, n_sc, n_ex, n_co = Tally(), Tally(), Tally(), Tally()
            n_relu, n_yTo = Tally(), Tally()
            per = ((n_sq, 1), (n_split, 3 * KT), (n_y, NU), (n_ex, NU), (n_co, NU), (n_relu, TT))
            with turns(e, LAYERS, *per) as L:
                norm(T, True)
                plain(of_layer("qk", L), T, emptied_d, ready=tile_ready)
                m0, d0, a0, _ = of_layer("vn", L)
                for g in range(VG):
                    for c in range(4):
                        e.wait_ge(lo_done, RING + m0 + 4 * g + c + 1)
                        if g == 2 and c == 0:
                            e.wait_ge(emptied_d, 4 + d0 + 4)
                        natural(c, c, VW, 4 + 2 * (g % 2), TT, c == 0, c == 3).then_inc(chunk_done, 1)

                e.wait_ge(heads_in, 192 * L + 192)

                def head(pl, lo, n):
                    tile, half = pl
                    return heads[64 * half:64 * half + 64, tile, lo:lo + n]

                for qt in range(TT):
                    w = P * (qt + 1)
                    e.wait_ge(emptied_d, 4 + d0 + 4 * (qt + 2))
                    for ih in range(4):
                        pos = IQ + ih
                        key = (24, 0) if pos % 2 == 0 else (23, 1)
                        lo = w * (ih // 2)
                        end = e.matmul(ps[:, 6 - 2 * qt + ih % 2, lo:lo + w],
                                       head((pos // 2, pos % 2), P * qt, P), head(key, 0, w), start=True, stop=True)
                    end.then_inc(logits, 1)
                plain(of_layer("gate", L), T, emptied_a)
                e.wait_ge(relu_done, n_relu(TT))
                m0, d0, a0, _ = of_layer("mixg", L)
                e.wait_ge(emptied_a, 4 + a0)

                def mix_chunk(c):
                    e.wait_ge(lo_done, RING + m0 + c + 1)
                    e.wait_ge(emptied_a, a0 + c + 3)
                    products(6 + c % 2, c % RING, range(KT), 0, h, 0, T, True, True).then_inc(chunk_done, 1)

                def score(u):
                    qt, segs, _, _ = UNITS[u]
                    w = P * (qt + 1)
                    if u >= 2:
                        e.wait_ge(exped, n_ex.now + u - 1)
                    if u == 20:
                        e.wait_ge(maxed, NU * L + 1)
                    for s, (qp, kp, mk) in enumerate(segs):
                        at_ = w * s
                        bank, lo = 2 * (u % 2) + at_ // 512, at_ % 512
                        e.matmul(ps[:, bank, lo:lo + w], head(qp, P * qt, P), head(kp, 0, w), start=True, stop=False)
                        if mk == "picked":
                            out, src = ps[:, bank, lo:lo + w], picked[:, P * qt:P * qt + w]
                        elif (mk, qt) == ("tri", 1):
                            out, src = ps[:, bank, lo + P:lo + w], mask[:, 0:P]
                        else:
                            m_at, m_n = MASK[mk, qt]
                            out, src = ps[:, bank, lo:lo + w], mask[:, m_at:m_at + m_n]
                        end = e.matmul(out, identb[:, :], src, start=False, stop=True)
                    end.then_inc(scored, 1)

                def weigh(u):
                    qt, segs, vcols, _ = UNITS[u]
                    e.wait_ge(copied, n_co.now + u + 1)
                    if u >= 1:
                        e.wait_ge(y_done, n_y.now + u)
                    blocks = [(s, kt) for s in range(len(segs)) for kt in range(qt + 1)]
                    for b, (s, kt) in enumerate(blocks):
                        end = e.matmul(ps[:, 5, 0:HD], probT[u % 2][:, b * P:b * P + P],
                                       vn[:, kt, vcols[s]:vcols[s] + HD], start=(b == 0), stop=(b == len(blocks) - 1))
                    end.then_inc(weighed, 1)

                score(0)
                for u in range(NU):
                    if u + 1 < NU:
                        score(u + 1)
                    if MIX_CHUNK[u] is not None:
                        mix_chunk(MIX_CHUNK[u])
                    if u:
                        weigh(u - 1)
                    e.wait_ge(exped, n_ex.now + u + 1)
                    if u:
                        e.wait_ge(copied, n_co.now + u)
                    for b in range(unit_width(u) // P):
                        end = e.transpose(ps[:, 3 + b // 4, (b % 4) * P:(b % 4) * P + P],
                                          prob[u % 2][:, b * P:b * P + P], ident[:, :])
                    end.then_inc(turned, 1)
                weigh(NU - 1)
                n_ex(NU)
                n_co(NU)
                n_y(NU)
                e.wait_ge(y_done, n_y.now)
                for f in range(KT):
                    if f >= 4:
                        e.wait_ge(norm_hi, 3 * KT * L + KT + f - 3)
                    for tt in range(TT):
                        end = e.transpose(ps[:, f % 4, P * tt:P * tt + P], y[:, tt, f * P:f * P + P], ident[:, :])
                    end.then_inc(yT_done, 1)
                n_split(KT)

                m0, d0, a0, n = of_layer("br", L)
                e.wait_ge(emptied_a, 4 + a0)
                e.sem_inc(passed, 1)
                with e.Fori(0, n // RING) as i:
                    for j in range(RING):
                        e.wait_ge(lo_done, RING + m0 + RING * i + j + 1)
                        e.wait_ge(emptied_d, d0 + RING * i + j + 3)
                        bank = 4 - 4 * (j % 2)
                        ready = None if j else tile_ready
                        products(bank, j, range(0, 3), 0, h, T, T, True, True, ready)
                        products(bank + 1, j, range(3, 6), 0, h, T, T, True, True, ready)
                        products(bank + 2, j, range(6, 8), 0, h, T, T, True, True, ready).then_inc(chunk_done, 1)
                e.wait_ge(norm_split, n_split(KT) + 4)
                plain(of_layer("out", L), T, emptied_d)

            norm(T, False)
            n_act = Tally()

            def ffn(f, halves):
                w = halves * T
                norm(w, True)
                m0, d0, a0, n = later[f"up{f}"]
                with e.Fori(0, n // RING) as i:
                    for j in range(RING):
                        e.wait_ge(lo_done, RING + m0 + RING * i + j + 1)
                        e.wait_ge(emptied_d, d0 + RING * i + j - j % 2 + 2)
                        products(j, j, range(KT), 0, h, 0, w, True, True, None if j else tile_ready)\
                            .then_inc(chunk_done, 1)
                m0, d0, a0, n = later[f"down{f}"]
                e.wait_ge(emptied_d, 4 + d0 - 2)
                with e.Fori(0, n // (2 * RING)) as i:
                    for o in range(2):
                        for j in range(RING):
                            c = RING * o + j
                            e.wait_ge(lo_done, RING + m0 + 2 * RING * i + c + 1)
                            if j == 0:
                                e.wait_ge(emptied_d, 4 + d0 + 2 * RING * i + c - RING)
                            e.wait_ge(act_split, n_act.now + sum(DOWN[0:j + 1]) + 2)
                            products(o, j, range(DOWN[j]), sum(DOWN[0:j]), (ah, al), 0, w, j == 0, j == 3)\
                                .then_inc(chunk_done, 1)
                n_act(FT)

            ffn(0, 2)

            norm(2 * T, False)
            e.wait_ge(tables_in, 32)
            e.wait_ge(emptied_d, 4 + later["four"][1])
            for n in range(16):
                b, r = divmod(n, 8)
                g, tt = divmod(r, 2)
                e.wait_ge(normed, 4 + KT + 2 * g + 2)
                if n >= 4:
                    e.wait_ge(f1_out, n - 3)
                for kk in range(2):
                    tok = T * b + P * tt
                    end = e.matmul(ps[:, n % 4, :], hf[:, 2 * g + kk, tok:tok + P], dft[:, kk, :], start=(kk == 0),
                                   stop=(kk == 1))
                end.then_inc(f1_done, 1)
            for n in range(16):
                b, f = divmod(n, 8)
                e.wait_ge(f1_out, 8 * b + 8)
                if n >= 4:
                    e.wait_ge(f2_hi, n - 3)
                for q, (tt, part) in enumerate((tt, part) for tt in range(TT) for part in range(2)):
                    lo = T * part + P * (f % 2)
                    end = e.matmul(ps[:, 4 + n % 4, 0:T], pq[:, b, tt, f // 2, lo:lo + P], dftn[:, tt, part, :],
                                   start=(q == 0), stop=(q == 3))
                end.then_inc(f2_done, 1)
            e.wait_ge(f2_hi, 16)
            plain(later["four"], 2 * T, emptied_d)
            ffn(1, 2)
            ffn(2, 2)

            norm(2 * T, True)
            plain(later["rq"], T, emptied_d, ready=tile_ready)
            plain(later["rk"], 2 * T, emptied_d)
            m0, d0, a0, _ = later["rv"]
            for g in range(RH):
                for c in range(4):
                    e.wait_ge(lo_done, RING + m0 + 4 * g + c + 1)
                    if c == 0:
                        e.wait_ge(emptied_d, 4 + d0 + max(0, 4 * g - 4))
                    natural(c, c, RDV, 4 * (g % 2), 2 * TT, c == 0, c == 3).then_inc(chunk_done, 1)
            e.wait_ge(emptied_d, 4 + d0 + 12)
            plain(later["rg"], T, emptied_a)
            e.wait_ge(emptied_d, 4 + later["ro"][1])
            e.wait_ge(emptied_a, 4 + later["ro"][2])

            def scores(h_):
                for jt in range(4):
                    n = 4 * h_ + jt
                    if n >= 2:
                        e.wait_ge(rs_out, n - 1)
                    for dd in range(2):
                        end = e.matmul(ps[:, jt % 2, 0:T], kT[:, 2 * h_ + dd, P * jt:P * jt + P], qT[:, 2 * h_ + dd, :],
                                       start=(dd == 0), stop=(dd == 1))
                    end.then_inc(rs_done, 1)

            scores(0)
            for h_ in range(RH):
                for dv in range(4):
                    n = 4 * h_ + dv
                    e.wait_ge(rs_out, 4 * h_ + 4)
                    if n >= 4:
                        e.wait_ge(ry_out, n - 3)
                    for jt in range(4):
                        lo = RDV * h_ + P * dv
                        end = e.matmul(ps[:, 2 + dv, 0:T], vr[:, jt, lo:lo + P], sT[:, jt, :], start=(jt == 0),
                                       stop=(jt == 3))
                    end.then_inc(ry_done, 1)
                if h_ + 1 < RH:
                    scores(h_ + 1)
                e.wait_ge(ry_out, 4 * h_ + 4)
                for dv in range(4):
                    end = e.matmul(ps[:, 6, 0:T], ones[:, :], yr[:, dv, :], start=(dv == 0), stop=(dv == 3))
                end.then_inc(rmean, 1)
                for dv in range(4):
                    e.wait_ge(rcent, 4 * h_ + dv + 1)
                    end = e.matmul(ps[:, 7, 0:T], ones[:, :], sq[:, dv % 2, 0:T], start=(dv == 0), stop=(dv == 3))
                    end.then_inc(rc_done, 1)
            m0, d0, a0, n = later["ro"]
            with e.Fori(0, n // RING) as i:
                for j in range(RING):
                    e.wait_ge(lo_done, RING + m0 + RING * i + j + 1)
                    if j % 2 == 0:
                        e.wait_ge(emptied_d, 4 + d0 + RING * i + j - 2)
                    e.wait_ge(rgn, KT * (j % 2) + KT)
                    for t in range(KT):
                        f = KT * (j % 2) + t
                        w = slice(t * P, t * P + P)
                        mh, ml = (b[:, f // 2, T * (f % 2):T * (f % 2) + T] for b in h)
                        out = ps[:, j // 2, 0:T]
                        e.matmul(out, wh[:, j, w], mh, start=(f == 0), stop=False)
                        e.matmul(out, wh[:, j, w], ml, start=False, stop=False)
                        end = e.matmul(out, wl[:, j, w], mh, start=False, stop=(f == 2 * KT - 1))
                    end.then_inc(chunk_done, 1)
            ffn(3, 1)
            norm(T, False)


IN_SIZES = (384, 384, 384, 384, 384, 64, 64, 384, 256, 64, 4, 768, 768, 768, 256, 3072)
IN_AT = dict(zip(("a_q", "a_k", "a_v", "a_g", "b_q", "b_k", "b_v", "b_g", "i_q", "i_k", "i_w", "c_q", "c_k", "c_v",
                  "c_g", "m_g"), zip(np.cumsum((0,) + IN_SIZES[:-1]).tolist(), IN_SIZES)))


def tiles(w):
    k, n = w.shape
    return w.reshape(k // P, P, n // P, P).transpose(2, 1, 0, 3).reshape(n // P, P, k)


def natural_chunks(w, width):
    g = w.shape[1] // width
    return w.reshape(4, 2, P, g, width).transpose(3, 0, 2, 1, 4).reshape(4 * g, P, 2 * width)


def rows(v):
    return v.reshape(-1, P).transpose(1, 0)


def tables():
    f32 = np.float32
    inv = (1.0 / (f32(10000.0) ** (np.arange(0, HD, 2, dtype=f32) / f32(HD)))).astype(f32)
    ang = np.arange(T, dtype=f32)[:, None] * inv[None, :]
    cos, sin = np.cos(ang).T, np.sin(ang).T
    rope = np.concatenate([np.tile(cos, (4, 1)), np.tile(sin, (4, 1))], 1).astype(f32)

    i = np.arange(T)
    diff = i[:, None] - i[None, :]
    ok = {"tri": diff >= 0, "w128": (diff >= 0) & (diff <= 128), "d4": (diff >= 0) & (diff % 4 == 0),
          "d16": (diff >= 0) & (diff % 16 == 0)}
    mask = np.zeros((P, MASKW), f32)
    for (name, qt), (at, n) in MASK.items():
        mask[:, at:at + n] = np.where(ok[name][P * qt:P * qt + P, 0:n], 0.0, NEG)

    n = np.arange(T)
    ph = 2 * np.pi * ((n[:, None] * n[None, :]) % T) / T
    c, s = np.cos(ph), np.sin(ph)
    by_feature = np.concatenate([c, s], 1).reshape(2, P, 2 * T).transpose(1, 0, 2).reshape(P, -1)
    by_token = (np.stack([c, -s], 1) / T).reshape(TT, P, 2, T).transpose(1, 0, 2, 3).reshape(P, -1)
    dft = np.concatenate([by_feature, by_token], 1).astype(f32)

    rws = T // 64
    row = np.repeat(np.arange(rws, dtype=f32), 64)
    col = np.tile(np.arange(64, dtype=f32), rws)
    inv2 = f32(10000.0) ** (-np.arange(64, dtype=f32) / f32(64))
    ang2 = np.concatenate([row[:, None] * inv2, col[:, None] * inv2], 1).astype(f32)
    rope2 = np.concatenate([np.cos(ang2).T, np.sin(ang2).T], 1).astype(f32)

    j, q = np.arange(T)[:, None], np.arange(T)[None, :]
    fwd = np.concatenate([np.maximum(q - j, 0), q - j + T], 0)
    bwd = np.concatenate([np.maximum(j - q, 0), T - q + j], 0)
    dist = np.stack([fwd, bwd]).reshape(2, 4, P, T).transpose(2, 0, 1, 3).reshape(P, -1).astype(np.float16)
    dmask = np.stack([q >= j, j >= q]).reshape(2, 2, P, T).transpose(2, 0, 1, 3).reshape(P, -1).astype(np.float16)
    return rope, mask, dft, rope2, dist, dmask


def kernel(x, norm_g, w_in, w_br_a, w_br_b, w_br_c, w_out, final_norm_g, c_2, ctx_2, c_ctx_2, ada_w_2, ada_b_2,
           norm_g_2, final_g_2, ffn_w_gate_2, ffn_w_up_2, ffn_w_down_2, four_w_2, four_b_2, ret_w_in_2,
           ret_w_out_2, ret_decay_2):
    import ml_dtypes
    import concourse.bacc as _bacc
    from concourse import mybir as _mybir
    from concourse.bass_utils import run_bass_kernel_spmd as _run

    xT = np.concatenate([x[0].transpose(1, 0), ctx_2[0].transpose(1, 0)], 1)
    decay = np.broadcast_to(ret_decay_2.reshape(1, 8), (P, 8))
    cond = np.broadcast_to(np.stack([c_2[0], c_ctx_2])[None], (P, 2, D))
    cols = np.concatenate([rows(norm_g), rows(final_norm_g), rows(norm_g_2), rows(final_g_2), rows(four_b_2),
                           rows(ada_b_2), decay], 1)
    ada = np.concatenate([w.transpose(1, 0).reshape(ADA, P, D) for w in ada_w_2], 0)

    heads = ([("a_q", h) for h in range(6)] + [("a_k", h) for h in range(6)] + [("c_q", h) for h in range(12)]
             + [("c_k", h) for h in range(12)] + [("b_q", h) for h in range(6)] + [("i_q", h) for h in range(4)]
             + [("b_k", 0), ("i_k", 0)])
    qk_cols = []
    for g in range(NPOS // 4):
        for half in range(2):
            for name, h in heads[4 * g:4 * g + 4]:
                at = IN_AT[name][0] + HD * h + 32 * half
                qk_cols += list(range(at, at + 32))

    def span(*names):
        return [i for name in names for i in range(IN_AT[name][0], IN_AT[name][0] + IN_AT[name][1])]

    v_cols = span("a_v", "b_v", "c_v", "i_w")
    g_cols = span("a_g", "b_g", "c_g", "m_g")
    w1, wv = [], []
    for l in range(LAYERS):
        branch = np.concatenate([w_br_a[l], w_br_b[l], w_br_c[l]], 0)
        w1 += [tiles(w_in[l][:, qk_cols]), tiles(w_in[l][:, g_cols]), tiles(branch), tiles(w_out[l])]
        padded = np.concatenate([w_in[l][:, v_cols], np.zeros((D, VG * VW - len(v_cols)), np.float32)], 1)
        wv.append(natural_chunks(padded, VW))
    w1, wv = np.concatenate(w1, 0), np.concatenate(wv, 0)

    wu, wd = [], []
    for l in range(LAYERS):
        for f in range(2):
            both = np.stack([tiles(ffn_w_gate_2[l, f]), tiles(ffn_w_up_2[l, f])], 1)
            wu.append(both.reshape(2 * FT, P, CW))
            wd.append(tiles(ffn_w_down_2[l, f]))
    wu, wd = np.concatenate(wu, 0), np.concatenate(wd, 0)
    ret = ret_w_in_2[0]
    ro = tiles(ret_w_out_2[0]).reshape(KT, P, 2, CW).transpose(0, 2, 1, 3).reshape(2 * KT, P, CW)
    w2 = np.concatenate([tiles(four_w_2[0]), tiles(ret[:, 0:D]), tiles(ret[:, D:2 * D]),
                         natural_chunks(ret[:, 2 * D:4 * D], RDV), tiles(ret[:, 4 * D:6 * D]), ro], 0)
    rope, mask, dft, rope2, dist, dmask = tables()

    given = [("xT", xT), ("cols", cols), ("cond", cond), ("ada", ada), ("w1", w1), ("wv", wv), ("wu", wu), ("wd", wd), ("w2", w2),
             ("rope", rope), ("mask", mask.astype(ml_dtypes.bfloat16)), ("ident", np.eye(P, dtype=np.float32)),
             ("identb", np.eye(P, dtype=ml_dtypes.bfloat16)), ("dft", dft), ("rope2", rope2), ("dist", dist),
             ("dmask", dmask)]
    nc = _bacc.Bacc("TRN2", target_bir_lowering=False, num_devices=1)
    arrays, args = {}, []
    for name, a in given:
        a = np.ascontiguousarray(a)
        arrays[f"in_{name}_dram"] = a
        args.append(nc.dram_tensor(f"in_{name}_dram", a.shape, _mybir.dt.from_np(a.dtype), kind="ExternalInput").ap())
    args.append(nc.dram_tensor("out_0_dram", (D, T), F32, kind="ExternalOutput").ap())
    program(nc, *args)
    r = _run(nc, [arrays], core_ids=[0])
    return r.results[0]["out_0_dram"].transpose(1, 0).reshape(1, T, D)
```
